# Optimizing a Trainium2 kernel written in Bass

```python
import math
import jax, jax.numpy as jnp
from jax import lax
import numpy as np

D_MODEL = 1024
BATCH = 1
SEQ = 256
DEPTH = 1
DEC_BATCH = 8
DEC_SEQ = 1
PAST_LEN = 2048
PAGE_SIZE = 128

SSM_D_INNER = 2 * D_MODEL
SSM_HEADDIM = 64
SSM_HEADS = SSM_D_INNER // SSM_HEADDIM
SSM_GROUPS = 4
SSM_STATE = 128
SSM_CONV = 4
SSM_CHUNK = 128
SSM_CONV_CH = SSM_D_INNER + 2 * SSM_GROUPS * SSM_STATE
ATT_HEADS = 16
ATT_KV_HEADS = 4
ATT_GROUP = ATT_HEADS // ATT_KV_HEADS
ATT_HEAD_DIM = D_MODEL // ATT_HEADS
ATT_Q_DIM = ATT_HEADS * ATT_HEAD_DIM
ATT_KV_DIM = ATT_KV_HEADS * ATT_HEAD_DIM
WINDOW = 128
ROPE_THETA = 10000.0
MEM_LEN = 256
MEM_HEADS = 4
MEM_HEAD_DIM = D_MODEL // MEM_HEADS
MEM_Q_DIM = MEM_HEADS * MEM_HEAD_DIM
MOE_GROUPS = 4
MOE_EXPERTS_PER_GROUP = 8
MOE_EXPERTS = MOE_GROUPS * MOE_EXPERTS_PER_GROUP
MOE_TOP_K = 2
MOE_D_FF = 256

N_BRANCHES = 3
EPS = 1e-6

OFF_Z = N_BRANCHES * D_MODEL
OFF_XBC = OFF_Z + SSM_D_INNER
OFF_DT = OFF_XBC + SSM_CONV_CH
OFF_Q = OFF_DT + SSM_HEADS
OFF_K = OFF_Q + ATT_Q_DIM
OFF_V = OFF_K + ATT_KV_DIM
OFF_MQ = OFF_V + ATT_KV_DIM
IN_TOTAL = OFF_MQ + MEM_Q_DIM

kernel_name = 'hybrid_ssd_swa_mem_hmoe_step'

def rms_norm(x, g):
    xf = x.astype(jnp.float32)
    y = xf * lax.rsqrt(jnp.mean(xf * xf, axis=-1, keepdims=True) + EPS)
    return (y * g.astype(jnp.float32)).astype(x.dtype)

def rope(x, pos):
    half = x.shape[-1] // 2
    inv = ROPE_THETA ** (-jnp.arange(half, dtype=jnp.float32) / half)
    ang = pos.astype(jnp.float32)[:, None] * inv[None, :]
    cos = jnp.cos(ang)[:, None, :]
    sin = jnp.sin(ang)[:, None, :]
    xf = x.astype(jnp.float32)
    x1, x2 = xf[..., :half], xf[..., half:]
    return jnp.concatenate([x1 * cos - x2 * sin, x2 * cos + x1 * sin], axis=-1).astype(x.dtype)

def front(x, lw):
    hn = rms_norm(x, lw['norm1_g'])
    proj = jnp.einsum('bld,de->ble', hn, lw['w_in'])
    return jnp.split(proj, [OFF_Z, OFF_XBC, OFF_DT, OFF_Q, OFF_K, OFF_V, OFF_MQ], axis=-1)

def causal_conv(xh, w, b):
    L = xh.shape[1] - (SSM_CONV - 1)
    out = xh[:, 0:L] * w[0]
    for j in range(1, SSM_CONV):
        out = out + xh[:, j:j + L] * w[j]
    return out + b

def ssd(x, dt, a, bm, cm, h0, chunk):
    b, L, H, P = x.shape
    G, N = bm.shape[2], bm.shape[3]
    R = H // G
    nc = L // chunk
    f32 = jnp.float32
    xc = x.reshape(b, nc, chunk, G, R, P).astype(f32)
    bc = bm.reshape(b, nc, chunk, G, N).astype(f32)
    cc = cm.reshape(b, nc, chunk, G, N).astype(f32)
    dtc = dt.reshape(b, nc, chunk, G, R)
    acum = jnp.cumsum(dtc * a.reshape(G, R), axis=2)
    t = jnp.arange(chunk)
    causal = (t[:, None] >= t[None, :])[:, :, None, None]
    seg = acum[:, :, :, None] - acum[:, :, None, :]
    decay = jnp.exp(jnp.where(causal, seg, -jnp.inf))
    cb = jnp.einsum('bctgn,bcsgn->bctsg', cc, bc)
    wts = cb[..., None] * decay * dtc[:, :, None]
    y_diag = jnp.einsum('bctsgr,bcsgrp->bctgrp', wts, xc)
    decay_end = jnp.exp(acum[:, :, -1:] - acum)
    states = jnp.einsum('bclgn,bclgr,bclgrp->bcgrpn', bc, decay_end * dtc, xc)
    chunk_decay = jnp.exp(acum[:, :, -1])

    def step(h, inp):
        s, d = inp
        return h * d[..., None, None] + s, h

    h_init = h0.reshape(b, G, R, P, N).astype(f32)
    h_last, h_prev = lax.scan(step, h_init, (jnp.moveaxis(states, 1, 0), jnp.moveaxis(chunk_decay, 1, 0)))
    h_prev = jnp.moveaxis(h_prev, 0, 1)
    y_off = jnp.einsum('bctgn,bcgrpn->bctgrp', cc, h_prev) * jnp.exp(acum)[..., None]
    y = (y_diag + y_off).reshape(b, L, H, P)
    return y.astype(x.dtype), h_last.reshape(b, H, P, N).astype(h0.dtype)

def mamba_branch(z, xbc_hist, dt_raw, h0, chunk, lw):
    b, L = z.shape[0], z.shape[1]
    xbc = jax.nn.silu(causal_conv(xbc_hist, lw['ssm_conv_w'], lw['ssm_conv_b']))
    xs, bm, cm = jnp.split(xbc, [SSM_D_INNER, SSM_D_INNER + SSM_GROUPS * SSM_STATE], axis=-1)
    xs = xs.reshape(b, L, SSM_HEADS, SSM_HEADDIM)
    bm = bm.reshape(b, L, SSM_GROUPS, SSM_STATE)
    cm = cm.reshape(b, L, SSM_GROUPS, SSM_STATE)
    dt = jax.nn.softplus(dt_raw.astype(jnp.float32) + lw['ssm_dt_bias'].astype(jnp.float32))
    a = -jnp.exp(lw['ssm_a_log'].astype(jnp.float32))
    y, h_new = ssd(xs, dt, a, bm, cm, h0, chunk)
    y = y + lw['ssm_d'][:, None].astype(y.dtype) * xs
    y = y.reshape(b, L, SSM_D_INNER)
    return rms_norm(y * jax.nn.silu(z), lw['ssm_norm_g']), h_new

def qkv_prep(q, k, v, pos, lw):
    b, L = q.shape[0], q.shape[1]
    q = rope(rms_norm(q.reshape(b, L, ATT_HEADS, ATT_HEAD_DIM), lw['att_q_norm_g']), pos)
    k = rope(rms_norm(k.reshape(b, L, ATT_KV_HEADS, ATT_HEAD_DIM), lw['att_k_norm_g']), pos)
    return q, k, v.reshape(b, L, ATT_KV_HEADS, ATT_HEAD_DIM)

def window_attend(q, k, v, qpos, kpos, sink):
    s = jnp.einsum('...qkgd,...skd->...kgqs', q, k).astype(jnp.float32) * (ATT_HEAD_DIM ** -0.5)
    diff = qpos[..., :, None] - kpos[..., None, :]
    mask = (diff >= 0) & (diff < WINDOW) & (kpos[..., None, :] >= 0)
    s = jnp.where(mask[..., None, None, :, :], s, -jnp.inf)
    snk = sink.astype(jnp.float32).reshape(ATT_KV_HEADS, ATT_GROUP, 1, 1)
    m = jnp.maximum(jnp.max(s, axis=-1, keepdims=True), snk)
    p = jnp.exp(s - m)
    p = p / (jnp.sum(p, axis=-1, keepdims=True) + jnp.exp(snk - m))
    return jnp.einsum('...kgqs,...skd->...qkgd', p.astype(v.dtype), v)

def swa_prompt(q, k, v, sink):
    b, L = q.shape[0], q.shape[1]
    nb = L // WINDOW
    qb = q.reshape(b, nb, WINDOW, ATT_KV_HEADS, ATT_GROUP, ATT_HEAD_DIM)

    def with_prev(t):
        t = t.reshape(b, nb, WINDOW, ATT_KV_HEADS, ATT_HEAD_DIM)
        prev = jnp.concatenate([jnp.zeros_like(t[:, :1]), t[:, :-1]], axis=1)
        return jnp.concatenate([prev, t], axis=2)

    qpos = jnp.arange(L).reshape(nb, WINDOW)
    kpos = jnp.concatenate([qpos - WINDOW, qpos], axis=1)
    o = window_attend(qb, with_prev(k), with_prev(v), qpos, kpos, sink)
    return o.reshape(b, L, ATT_Q_DIM)

def mem_kv(mem, lw):
    b, M = mem.shape[0], mem.shape[1]
    kv = jnp.einsum('bmd,de->bme', rms_norm(mem, lw['mem_norm_g']), lw['w_mem_kv'])
    kv = kv.reshape(b, M, 2, MEM_HEADS, MEM_HEAD_DIM)
    return rms_norm(kv[:, :, 0], lw['mem_k_norm_g']), kv[:, :, 1]

def mem_attend(mq, mk, mv, lw):
    b, L = mq.shape[0], mq.shape[1]
    q = rms_norm(mq.reshape(b, L, MEM_HEADS, MEM_HEAD_DIM), lw['mem_q_norm_g'])
    s = jnp.einsum('blhd,bmhd->bhlm', q, mk).astype(jnp.float32) * (MEM_HEAD_DIM ** -0.5)
    p = jax.nn.softmax(s, axis=-1).astype(mv.dtype)
    return jnp.einsum('bhlm,bmhd->blhd', p, mv).reshape(b, L, MEM_Q_DIM)

def hier_moe(h, lw):
    T = h.shape[0]
    lg = jnp.einsum('td,dg->tg', h, lw['w_router_group']).astype(jnp.float32) + lw['b_router_group'].astype(jnp.float32)
    pg = jax.nn.softmax(lg, axis=-1)
    g = jnp.argmax(pg, axis=-1)
    pg_top = jnp.take_along_axis(pg, g[:, None], axis=-1)
    le = jnp.einsum('td,de->te', h, lw['w_router_expert']).astype(jnp.float32) + lw['b_router_expert'].astype(jnp.float32)
    le = le.reshape(T, MOE_GROUPS, MOE_EXPERTS_PER_GROUP)
    le_g = jnp.take_along_axis(le, g[:, None, None], axis=1)[:, 0]
    pe = jax.nn.softmax(le_g, axis=-1)
    topv, topi = lax.top_k(pe, MOE_TOP_K)
    wts = pg_top * topv / jnp.sum(topv, axis=-1, keepdims=True)
    eid = g[:, None] * MOE_EXPERTS_PER_GROUP + topi
    comb = jnp.sum(jax.nn.one_hot(eid, MOE_EXPERTS, dtype=jnp.float32) * wts[..., None], axis=1).astype(h.dtype)
    out = jnp.zeros_like(h)
    for e in range(MOE_EXPERTS):
        act = jax.nn.silu(h @ lw['w_exp_gate'][e]) * (h @ lw['w_exp_up'][e])
        out = out + comb[:, e:e + 1] * (act @ lw['w_exp_down'][e])
    return out

def back(x, gates, y_ssm, y_swa, y_mem, lw):
    gt = jax.nn.sigmoid(gates.astype(jnp.float32)).astype(x.dtype)
    gt = gt.reshape(gates.shape[0], gates.shape[1], N_BRANCHES, D_MODEL)
    merged = (gt[:, :, 0] * jnp.einsum('ble,ed->bld', y_ssm, lw['w_br_ssm'])
              + gt[:, :, 1] * jnp.einsum('ble,ed->bld', y_swa, lw['w_br_swa'])
              + gt[:, :, 2] * jnp.einsum('ble,ed->bld', y_mem, lw['w_br_mem']))
    x1 = x + jnp.einsum('bld,de->ble', merged, lw['w_out'])
    b, L = x1.shape[0], x1.shape[1]
    h = rms_norm(x1, lw['norm2_g']).reshape(b * L, D_MODEL)
    return x1 + hier_moe(h, lw).reshape(b, L, D_MODEL)

def prompt_layer(x, mem, lw):
    b, L = x.shape[0], x.shape[1]
    gates, z, xbc, dt_raw, q, k, v, mq = front(x, lw)
    xbc_hist = jnp.pad(xbc, ((0, 0), (SSM_CONV - 1, 0), (0, 0)))
    h0 = jnp.zeros((b, SSM_HEADS, SSM_HEADDIM, SSM_STATE), x.dtype)
    y_ssm, ssm_new = mamba_branch(z, xbc_hist, dt_raw, h0, SSM_CHUNK, lw)
    conv_new = xbc[:, L - (SSM_CONV - 1):]
    q, k, v = qkv_prep(q, k, v, jnp.arange(L), lw)
    y_swa = swa_prompt(q, k, v, lw['att_sink'])
    mk, mv = mem_kv(mem, lw)
    y_mem = mem_attend(mq, mk, mv, lw)
    y = back(x, gates, y_ssm, y_swa, y_mem, lw)
    return y, conv_new, ssm_new, k[:, L - WINDOW:], v[:, L - WINDOW:], mk, mv

def sample_layer(x, conv_st, ssm_st, swa_k, swa_v, mk, mv, lw):
    b, L = x.shape[0], x.shape[1]
    gates, z, xbc, dt_raw, q, k, v, mq = front(x, lw)
    xbc_hist = jnp.concatenate([conv_st, xbc], axis=1)
    y_ssm, ssm_new = mamba_branch(z, xbc_hist, dt_raw, ssm_st, L, lw)
    conv_new = xbc_hist[:, L:]
    qpos = PAST_LEN + jnp.arange(L)
    q, k, v = qkv_prep(q, k, v, qpos, lw)
    kk = jnp.concatenate([swa_k, k], axis=1)
    vv = jnp.concatenate([swa_v, v], axis=1)
    kpos = PAST_LEN - WINDOW + jnp.arange(WINDOW + L)
    qb = q.reshape(b, L, ATT_KV_HEADS, ATT_GROUP, ATT_HEAD_DIM)
    y_swa = window_attend(qb, kk, vv, qpos, kpos, lw['att_sink']).reshape(b, L, ATT_Q_DIM)
    y_mem = mem_attend(mq, mk, mv, lw)
    y = back(x, gates, y_ssm, y_swa, y_mem, lw)
    return y, conv_new, ssm_new, kk[:, L:], vv[:, L:]

def setup_inputs(seed: int = 0) -> dict:
    key = jax.random.key(seed)
    ks = iter(jax.random.split(key, 48))
    f32 = jnp.float32

    def nrm(shape, scale):
        return jax.random.normal(next(ks), shape, f32) * scale

    def gain(shape):
        return 1.0 + nrm(shape, 0.05)

    dt = jnp.exp(jax.random.uniform(next(ks), (DEPTH, SSM_HEADS), f32, math.log(1e-3), math.log(1e-1)))
    dt_bias = dt + jnp.log(-jnp.expm1(-dt))
    a_log = jnp.log(jax.random.uniform(next(ks), (DEPTH, SSM_HEADS), f32, 1.0, 16.0))
    return {
        'x_prompt': nrm((BATCH, SEQ, D_MODEL), 1.0),
        'x_sample': nrm((DEC_BATCH, DEC_SEQ, D_MODEL), 1.0),
        'state_conv': nrm((DEPTH, DEC_BATCH, SSM_CONV - 1, SSM_CONV_CH), 1.0),
        'state_ssm': nrm((DEPTH, DEC_BATCH, SSM_HEADS, SSM_HEADDIM, SSM_STATE), 0.5),
        'cache_swa_k': nrm((DEPTH, DEC_BATCH, WINDOW, ATT_KV_HEADS, ATT_HEAD_DIM), 1.0),
        'cache_swa_v': nrm((DEPTH, DEC_BATCH, WINDOW, ATT_KV_HEADS, ATT_HEAD_DIM), 1.0),
        'cache_mem_k': nrm((DEPTH, DEC_BATCH, MEM_LEN, MEM_HEADS, MEM_HEAD_DIM), 1.0),
        'cache_mem_v': nrm((DEPTH, DEC_BATCH, MEM_LEN, MEM_HEADS, MEM_HEAD_DIM), 1.0),
        'mem_prompt': nrm((BATCH, MEM_LEN, D_MODEL), 1.0),
        'norm1_g': gain((DEPTH, D_MODEL)),
        'w_in': nrm((DEPTH, D_MODEL, IN_TOTAL), D_MODEL ** -0.5),
        'ssm_conv_w': nrm((DEPTH, SSM_CONV, SSM_CONV_CH), SSM_CONV ** -0.5),
        'ssm_conv_b': nrm((DEPTH, SSM_CONV_CH), 0.02),
        'ssm_dt_bias': dt_bias,
        'ssm_a_log': a_log,
        'ssm_d': gain((DEPTH, SSM_HEADS)),
        'ssm_norm_g': gain((DEPTH, SSM_D_INNER)),
        'att_q_norm_g': gain((DEPTH, ATT_HEAD_DIM)),
        'att_k_norm_g': gain((DEPTH, ATT_HEAD_DIM)),
        'att_sink': nrm((DEPTH, ATT_HEADS), 0.5),
        'mem_norm_g': gain((DEPTH, D_MODEL)),
        'w_mem_kv': nrm((DEPTH, D_MODEL, 2 * MEM_Q_DIM), D_MODEL ** -0.5),
        'mem_q_norm_g': gain((DEPTH, MEM_HEAD_DIM)),
        'mem_k_norm_g': gain((DEPTH, MEM_HEAD_DIM)),
        'w_br_ssm': nrm((DEPTH, SSM_D_INNER, D_MODEL), SSM_D_INNER ** -0.5),
        'w_br_swa': nrm((DEPTH, ATT_Q_DIM, D_MODEL), ATT_Q_DIM ** -0.5),
        'w_br_mem': nrm((DEPTH, MEM_Q_DIM, D_MODEL), MEM_Q_DIM ** -0.5),
        'w_out': nrm((DEPTH, D_MODEL, D_MODEL), D_MODEL ** -0.5),
        'norm2_g': gain((DEPTH, D_MODEL)),
        'w_router_group': nrm((DEPTH, D_MODEL, MOE_GROUPS), D_MODEL ** -0.5),
        'b_router_group': nrm((DEPTH, MOE_GROUPS), 0.01),
        'w_router_expert': nrm((DEPTH, D_MODEL, MOE_EXPERTS), D_MODEL ** -0.5),
        'b_router_expert': nrm((DEPTH, MOE_EXPERTS), 0.01),
        'w_exp_gate': nrm((DEPTH, MOE_EXPERTS, D_MODEL, MOE_D_FF), D_MODEL ** -0.5),
        'w_exp_up': nrm((DEPTH, MOE_EXPERTS, D_MODEL, MOE_D_FF), D_MODEL ** -0.5),
        'w_exp_down': nrm((DEPTH, MOE_EXPERTS, MOE_D_FF, D_MODEL), MOE_D_FF ** -0.5),
    }

def reference(x_prompt, x_sample, state_conv, state_ssm, cache_swa_k, cache_swa_v, cache_mem_k, cache_mem_v,
              mem_prompt, norm1_g, w_in, ssm_conv_w, ssm_conv_b, ssm_dt_bias, ssm_a_log, ssm_d, ssm_norm_g,
              att_q_norm_g, att_k_norm_g, att_sink, mem_norm_g, w_mem_kv, mem_q_norm_g, mem_k_norm_g,
              w_br_ssm, w_br_swa, w_br_mem, w_out, norm2_g, w_router_group, b_router_group,
              w_router_expert, b_router_expert, w_exp_gate, w_exp_up, w_exp_down):
    xp, xs = x_prompt, x_sample
    p_conv, p_ssm, p_k, p_v, p_mk, p_mv = [], [], [], [], [], []
    s_conv, s_ssm, s_k, s_v = [], [], [], []
    for l in range(DEPTH):
        lw = dict(norm1_g=norm1_g[l], w_in=w_in[l], ssm_conv_w=ssm_conv_w[l], ssm_conv_b=ssm_conv_b[l],
                  ssm_dt_bias=ssm_dt_bias[l], ssm_a_log=ssm_a_log[l], ssm_d=ssm_d[l], ssm_norm_g=ssm_norm_g[l],
                  att_q_norm_g=att_q_norm_g[l], att_k_norm_g=att_k_norm_g[l], att_sink=att_sink[l],
                  mem_norm_g=mem_norm_g[l], w_mem_kv=w_mem_kv[l], mem_q_norm_g=mem_q_norm_g[l],
                  mem_k_norm_g=mem_k_norm_g[l], w_br_ssm=w_br_ssm[l], w_br_swa=w_br_swa[l],
                  w_br_mem=w_br_mem[l], w_out=w_out[l], norm2_g=norm2_g[l], w_router_group=w_router_group[l],
                  b_router_group=b_router_group[l], w_router_expert=w_router_expert[l],
                  b_router_expert=b_router_expert[l], w_exp_gate=w_exp_gate[l], w_exp_up=w_exp_up[l],
                  w_exp_down=w_exp_down[l])
        xp, c1, c2, c3, c4, c5, c6 = prompt_layer(xp, mem_prompt, lw)
        p_conv.append(c1); p_ssm.append(c2); p_k.append(c3); p_v.append(c4); p_mk.append(c5); p_mv.append(c6)
        xs, d1, d2, d3, d4 = sample_layer(xs, state_conv[l], state_ssm[l], cache_swa_k[l], cache_swa_v[l],
                                          cache_mem_k[l], cache_mem_v[l], lw)
        s_conv.append(d1); s_ssm.append(d2); s_k.append(d3); s_v.append(d4)
    return (xp, xs,
            jnp.stack(p_conv), jnp.stack(p_ssm), jnp.stack(p_k), jnp.stack(p_v), jnp.stack(p_mk), jnp.stack(p_mv),
            jnp.stack(s_conv), jnp.stack(s_ssm), jnp.stack(s_k), jnp.stack(s_v))


_drawn_inputs = setup_inputs


def setup_inputs(seed=0):
    import zlib

    import numpy as np

    out = dict(_drawn_inputs(seed))
    spreads = {}
    factors = {'att_q_norm_g': 3.985,
     'att_sink': 8.0,
     'mem_q_norm_g': 5.475,
     'b_router_group': 8.204,
     'b_router_expert': 3.58}
    for name, (base, spread) in spreads.items():
        noise = np.random.default_rng([zlib.crc32(name.encode()), seed]).standard_normal(out[name].shape)
        drawn = base * np.exp(spread * noise) if base else spread * noise
        out[name] = __import__('jax').numpy.asarray(drawn.astype(out[name].dtype))
    for name, factor in factors.items():
        out[name] = (out[name] * factor).astype(out[name].dtype)
    return out
```

```python
from contextlib import ExitStack

import numpy as np

import concourse.bass as bass
from concourse import mybir

P = 128
D_MODEL = 1024
SEQ = 256
BATCH_S = 8
PAST_LEN = 2048
T = SEQ + BATCH_S
KT = D_MODEL // P
D_INNER = 2048
HEADDIM = 64
SSM_HEADS = 32
SSM_GROUPS = 4
STATE = 128
CONV_TAPS = 4
CONV_CH = D_INNER + 2 * SSM_GROUPS * STATE
CONV_T = CONV_CH // P
XS_T = D_INNER // P
KV = 4
HD = 64
WINDOW = 128
MEM = 256
MEM_H = 4
MEM_D = 256
GROUPS = 4
PER_GROUP = 8
EXPERTS = GROUPS * PER_GROUP
D_FF = 256
FF_T = D_FF // P
EPS = 1e-6
OFF_GATE, OFF_Z = 0, 3 * D_MODEL
OFF_XBC = OFF_Z + D_INNER
OFF_DT = OFF_XBC + CONV_CH
OFF_Q = OFF_DT + SSM_HEADS
OFF_K = OFF_Q + 1024
OFF_V = OFF_K + KV * HD
OFF_MQ = OFF_V + KV * HD
ROUTES = GROUPS + EXPERTS

CW = 256
CHUNK = KT * CW
WBUFS = 3
EXPERT_WORDS = 2 * KT * D_FF + FF_T * D_MODEL
MOE_BUFS = 4

ALU = mybir.AluOpType
ACT = mybir.ActivationFunctionType
AX = mybir.AxisListType
F32 = mybir.dt.float32

VEC = {}
_at = 0
for _name, _n in (("g1", KT), ("gmem", KT), ("conv_w", CONV_TAPS * CONV_T), ("conv_b", CONV_T), ("ssm_g", XS_T),
                  ("ssm_d", XS_T), ("gq", 1), ("gk", 1), ("gmq", 2), ("gmk", 2), ("g2", KT), ("sink_col", 1),
                  ("dt_bias", SSM_HEADS), ("a_log", SSM_HEADS), ("route_b", ROUTES), ("sink", 16)):
    VEC[_name] = (_at, _n)
    _at += _n
VEC_W = _at
TAB = {}
_at = 0
for _name, _n in (("ident", P), ("causal", 3 * P), ("rot", P), ("half_ones", P), ("ones", P), ("window", 2 * P),
                  ("cos", T), ("sin", T), ("first_g", GROUPS), ("first_e", PER_GROUP)):
    TAB[_name] = (_at, _n)
    _at += _n
TAB_W = _at

MAP = {}


def _place(*names):
    at = 0
    for name, words in names:
        MAP[name] = (at, words)
        at += words
    assert at <= 53200, at


_place(
    ("HN", KT * T),
    ("W", WBUFS * CHUNK),
    ("X", CONV_T * T),
    ("C", CONV_T * T),
    ("Q", 8 * T),
    ("KD", KV * T),
    ("MQ", 8 * T),
    ("VT", 3 * KV * HD),
    ("XD", 2 * D_INNER),
    ("Z", XS_T * T),
    ("G", 24 * T),
    ("MK", 8 * MEM),
    ("MV", 2 * D_MODEL),
    ("S", 3072),
    ("tab", TAB_W), ("vec", VEC_W),
    ("DT", 3 * SSM_HEADS), ("DTA", 3 * SSM_HEADS), ("AC", 2 * SSM_HEADS), ("WE", 2 * SSM_HEADS),
    ("BT", 2 * 4 * STATE), ("RS", T), ("TQ", T), ("EX", 2 * XS_T * BATCH_S), ("XS", XS_T * BATCH_S),
    ("ST", 64),
)


def build_program(nc, ins, outs):
    ctx = ExitStack()
    with ctx:
        top = max(a + n for a, n in MAP.values())
        M = ctx.enter_context(nc.sbuf_tensor("M", [P, top], F32))
        psum = [ctx.enter_context(nc.psum_tensor(f"bank{i}", [P, 512], F32)) for i in range(8)]
        filled = [ctx.enter_context(nc.semaphore(f"filled{i}")) for i in range(8)]
        drained = [ctx.enter_context(nc.semaphore(f"drained{i}")) for i in range(8)]
        sems, counts = {}, {}

        def sem(name):
            if name not in sems:
                sems[name] = ctx.enter_context(nc.semaphore(name))
                counts[name] = 0
            return sems[name]

        def at(name, a=0, b=None, rows=P):
            off, n = MAP[name]
            b = n if b is None else b
            return M[0:rows, off + a:off + b]

        def tiles(name, w, a=0, b=None, rows=P):
            return at(name, a, b, rows).rearrange("p (j w) -> p j w", w=w)

        def tab(name, rows=P):
            a, n = TAB[name]
            return at("tab", a, a + n, rows)

        def vec(name, a=0, b=None, rows=P):
            off, n = VEC[name]
            b = n if b is None else b
            return at("vec", off + a, off + b, rows)

        def over(ap, n):
            return ap.unsqueeze(2).to_broadcast([ap.shape[0], ap.shape[1], n])

        def each(ap, n):
            return ap.unsqueeze(1).to_broadcast([ap.shape[0], n, ap.shape[1]])

        def done(eng, instruction, name):
            s = sem(name)
            counts[name] += 1
            instruction.then_inc(s, 1)
            eng.wait_ge(s, counts[name])

        HN, X, C, Z = tiles("HN", T), tiles("X", T), tiles("C", T), tiles("Z", T)
        Q, KD, MQ, G = tiles("Q", T), tiles("KD", T), tiles("MQ", T), tiles("G", T)
        MK, MV, VT = tiles("MK", MEM), tiles("MV", D_MODEL), tiles("VT", KV * HD)
        XD = tiles("XD", D_INNER)
        DT, DTA, AC, WE = (tiles(n, SSM_HEADS) for n in ("DT", "DTA", "AC", "WE"))
        BT = tiles("BT", 4 * STATE)
        RS, TQ = at("RS"), at("TQ")
        EX = at("EX").rearrange("p (a j b) -> p a j b", a=2, b=BATCH_S)
        XS = tiles("XS", BATCH_S)
        ident = tab("ident")
        ones = tab("ones")
        XT, XSQ = tiles("Z", T, 0, 8 * T), tiles("Z", T, 8 * T, 16 * T)
        MT, MSQ = tiles("G", MEM, 0, 2048), tiles("G", MEM, 2048, 4096)
        MN = tiles("XD", MEM, 0, 2048)
        RSM = tiles("G", MEM, 4096, 5120)
        NEWC = at("G", 0, 27 * CONV_T).rearrange("p (j k) -> p j k", k=27)
        HIST = at("G", 648, 648 + 24 * CONV_T).rearrange("p (j b k) -> p j b k", b=BATCH_S, k=3)
        CB = tiles("G", 3 * P, 1224, 2760)
        KSQ, QSQ = tiles("G", T, 2760, 3816), tiles("G", T, 3816, 5928)
        DTX, DAX = at("Z", 0, 2048, 8), at("Z", 2048, 4096, 8)
        SBC = at("X", 4096, 5120, 8)
        HS = [at("X", 2048 * i, 2048 * (i + 1)).rearrange("p (j n) -> p j n", n=STATE) for i in range(2)]
        T2 = at("S", 0, 2048)
        BB = at("S", 2048, 3072)
        SM, PTs = at("XD", 0, 1024), at("XD", 1024, 2048)
        RING = [at("C", 4224, 6272), at("XD", 2048, 4096)]
        SC, SC2 = at("G", 6336 - 64, 6336), at("G", 6336 - 192, 6336 - 64)

        X1 = HN
        MERGED = M[:, MAP["MK"][0]:MAP["MK"][0] + 8 * T].rearrange("p (j w) -> p j w", w=T)
        HT = tiles("C", T, 0, 8 * T)
        WR = at("S", 0, KT * ROUTES).rearrange("p (k n) -> p k n", n=ROUTES)
        COMB = at("S", 600, 600 + 96).rearrange("p (t e) -> p t e", e=EXPERTS)
        COMBT = at("S", 700, 700 + T, 32)
        comb_at = MAP["C"][0] + 8 * T
        COMBB = M[:, comb_at:comb_at + EXPERTS * T]
        slot_at = [comb_at + EXPERTS * T, comb_at + EXPERTS * T + EXPERT_WORDS,
                   comb_at + EXPERTS * T + 2 * EXPERT_WORDS, MAP["X"][0]]
        act_at = MAP["MK"][0] + 8 * T
        SG = [M[:, act_at + T * f:act_at + T * (f + 1)] for f in range(FF_T)]
        ACTT = [M[:, act_at + T * (2 + f):act_at + T * (3 + f)] for f in range(FF_T)]
        assert slot_at[2] + EXPERT_WORDS <= act_at and act_at + 4 * T <= MAP["S"][0]

        def expert_weights(j):
            o, n = slot_at[j], KT * D_FF
            return (M[:, o:o + n].rearrange("p (k f) -> p k f", f=D_FF),
                    M[:, o + n:o + 2 * n].rearrange("p (k f) -> p k f", f=D_FF),
                    M[:, o + 2 * n:o + 3 * n].rearrange("p (f n) -> p f n", f=FF_T))

        w_in, w_mem = ins["w_in"], ins["w_mem_kv"]
        chunks = []

        def cols(w, c0, n=CW, k0=0):
            return w[k0:k0 + D_MODEL, c0:c0 + n].rearrange("(k p) n -> p k n", p=P)

        for i in range(8):
            chunks.append((("mem", i), [(cols(w_mem, CW * i), 0, CW)]))
        for i in range(12):
            chunks.append((("xbc", i), [(cols(w_in, OFF_XBC + CW * i), 0, CW)]))
        chunks.append((("dt", 0), [(cols(w_in, OFF_DT, SSM_HEADS), 0, SSM_HEADS)]))
        for i in range(2):
            chunks.append((("kd", i), [(cols(w_in, OFF_K + HD * (2 * i + g), HD), P * g + HD * twice, HD)
                                       for g in range(2) for twice in range(2)]))
        chunks.append((("v", 0), [(cols(w_in, OFF_V), 0, CW)]))
        for i in range(4):
            chunks.append((("q", i), [(cols(w_in, OFF_Q + CW * i), 0, CW)]))
        for i in range(4):
            chunks.append((("mq", i), [(cols(w_in, OFF_MQ + CW * i), 0, CW)]))
        for i in range(8):
            chunks.append((("z", i), [(cols(w_in, OFF_Z + CW * i), 0, CW)]))
        for i in range(12):
            chunks.append((("gate", i), [(cols(w_in, OFF_GATE + CW * i), 0, CW)]))
        for i in range(4):
            chunks.append((("swa", i), [(cols(ins["w_br_swa"], CW * i), 0, CW)]))
            chunks.append((("memb", i), [(cols(ins["w_br_mem"], CW * i), 0, CW)]))
        for i in range(4):
            chunks.append((("ssma", i), [(cols(ins["w_br_ssm"], CW * i), 0, CW)]))
            chunks.append((("ssmb", i), [(cols(ins["w_br_ssm"], CW * i, CW, D_MODEL), 0, CW)]))
        for i in range(4):
            chunks.append((("out", i), [(cols(ins["w_out"], CW * i), 0, CW)]))
        number = {name: n for n, (name, _) in enumerate(chunks)}
        chunk_in = [sem(f"chunk_in{i}") for i in range(WBUFS)]

        def chunk(n):
            return tiles("W", CW, CHUNK * (n % WBUFS), CHUNK * (n % WBUFS + 1))

        place, uses, last_use = {}, [0] * 8, {}
        expert_in = [sem(f"expert_in{j}") for j in range(MOE_BUFS)]
        half_free = [sem(f"half_free{f}") for f in range(FF_T)]
        act_ready = [sem(f"act_ready{f}") for f in range(FF_T)]
        down_filled = [sem(f"down_filled{q}") for q in range(4)]
        down_read = [sem(f"down_read{q}") for q in range(4)]

        def wait_filled(eng, name):
            bank, n = place[name]
            eng.wait_ge(filled[bank], n + 1)
            return psum[bank]

        def wait_drained(eng, name):
            bank, n = place[name]
            eng.wait_ge(drained[bank], n + 1)

        def drains(instruction, name):
            instruction.then_inc(drained[place[name][0]], 1)

        block = ctx.enter_context(nc.Block())

        @block.tensor
        def _(pe):
            ring = [0]
            at_chunk = [0]
            chunk_arrivals = {}

            def opened(name, bank):
                n = uses[bank]
                uses[bank] += 1
                place[name] = (bank, n)
                if n:
                    pe.wait_ge(drained[bank], n)
                return psum[bank]

            def full(mm, name):
                mm.then_inc(filled[place[name][0]], 1)

            def next_proj(name):
                ring[0] += 1
                return opened(name, (ring[0] - 1) % 3)

            def arrive(name):
                n = number[name]
                pe.wait_ge(chunk_in[n % WBUFS], chunk_value[n])
                return chunk(n)

            def feature_tile(name, w, c, x, n, chunk_name):
                bank = next_proj(name)
                for k in range(KT):
                    mm = pe.matmul(bank[:, 0:n], w[:, k, P * c:P * (c + 1)], x[:, k, 0:n],
                                   start=(k == 0), stop=(k == KT - 1))
                full(mm, name)
                last_use[chunk_name] = name

            chunk_value, seen = {}, [0] * WBUFS
            for n, (_, parts) in enumerate(chunks):
                seen[n % WBUFS] += 16 * len(parts)
                chunk_value[n] = seen[n % WBUFS]

            def squares(name, bank, sq, first, n_tiles, n, weights=None):
                b = opened(name, bank)
                for k in range(n_tiles):
                    mm = pe.matmul(b[:, 0:n], ones if weights is None else weights, sq[:, first + k, 0:n],
                                   start=(k == 0), stop=(k == n_tiles - 1))
                full(mm, name)

            pe.wait_ge(sem("tables_in"), 32)
            pe.wait_ge(sem("x_squared"), 1)
            squares("ss_x", 3, XSQ, 0, KT, T)
            pe.wait_ge(sem("mem_squared"), 1)
            squares("ss_mem", 4, MSQ, 0, KT, MEM)

            pe.wait_ge(sem("mem_normed"), 1)
            for i in range(4):
                w = arrive(("mem", i))
                for c in range(2):
                    feature_tile(("mk", 2 * i + c), w, c, MN, MEM, ("mem", i))
            for i in range(4):
                w = arrive(("mem", 4 + i))
                for mt in range(2):
                    name = ("mv", i, mt)
                    b = next_proj(name)
                    for k in range(KT):
                        mm = pe.matmul(b[:, 0:CW], MN[:, k, P * mt:P * (mt + 1)], w[:, k, :],
                                       start=(k == 0), stop=(k == KT - 1))
                    full(mm, name)
                    last_use[("mem", 4 + i)] = name
            pe.wait_ge(sem("mk_squared"), 1)
            for h in range(MEM_H):
                squares(("ss_mk", h), 3 + h, MSQ, 2 * h, 2, MEM)

            pe.wait_ge(sem("x_normed"), 1)
            for i in range(12):
                w = arrive(("xbc", i))
                for c in range(2):
                    feature_tile(("xbc", 2 * i + c), w, c, HN, T, ("xbc", i))
            arrive(("dt", 0))
            off = MAP["W"][0] + CHUNK * (number[("dt", 0)] % WBUFS)
            w = M[:, off:off + KT * SSM_HEADS].rearrange("p (k n) -> p k n", n=SSM_HEADS)
            b = next_proj("dt")
            for t, rows in enumerate((P, P, BATCH_S)):
                for k in range(KT):
                    mm = pe.matmul(b[0:rows, 32 * t:32 * t + 32], HN[:, k, P * t:P * t + rows], w[:, k, :],
                                   start=(k == 0), stop=(k == KT - 1))
            full(mm, "dt")
            last_use[("dt", 0)] = "dt"
            for i in range(2):
                w = arrive(("kd", i))
                for c in range(2):
                    feature_tile(("kd", 2 * i + c), w, c, HN, T, ("kd", i))
            w = arrive(("v", 0))
            for t, rows in enumerate((P, P, BATCH_S)):
                b = next_proj(("v", t))
                for k in range(KT):
                    mm = pe.matmul(b[0:rows, 0:CW], HN[:, k, P * t:P * t + rows], w[:, k, :],
                                   start=(k == 0), stop=(k == KT - 1))
                full(mm, ("v", t))
                last_use[("v", 0)] = ("v", t)
            for i in range(4):
                w = arrive(("q", i))
                for c in range(2):
                    feature_tile(("q", 2 * i + c), w, c, HN, T, ("q", i))
                if i == 1:
                    pe.wait_ge(sem("dta"), 1)
                    b = opened("acum", 3)
                    pe.matmul(b[:, 0:32], tab("causal")[:, 0:P], DTA[:, 0, :], start=True, stop=True)
                    pe.matmul(b[:, 32:64], ones, DTA[:, 0, :], start=True, stop=False)
                    pe.matmul(b[:, 32:64], tab("causal")[:, 0:P], DTA[:, 1, :], start=False, stop=True)
                    pe.matmul(b[:, 64:96], ones, DTA[:, 0, :], start=True, stop=False)
                    full(pe.matmul(b[:, 64:96], ones, DTA[:, 1, :], start=False, stop=True), "acum")
                    pe.wait_ge(sem("dt_expanded"), 1)
                    b = opened("ex", 4)
                    for a, src in enumerate((DTX, DAX)):
                        for j in range(XS_T):
                            c0 = (a * XS_T + j) * BATCH_S
                            mm = pe.matmul(b[:, c0:c0 + BATCH_S], src[:, P * j:P * (j + 1)], ident[0:8, 0:8],
                                           start=True, stop=True)
                    full(mm, "ex")

            for i in range(4):
                w = arrive(("mq", i))
                for c in range(2):
                    feature_tile(("mq", 2 * i + c), w, c, HN, T, ("mq", i))
                    j = 2 * i + c
                    if j == 0:
                        pe.wait_ge(sem("conv_active"), 3)
                    if j < 4:
                        for half in range(2):
                            b = opened(("xtok", half, j), 3 + half)
                            for q in range(4):
                                mm = pe.transpose(b[:, P * q:P * (q + 1)], C[:, 4 * j + q, P * half:P * (half + 1)],
                                                  ident)
                            full(mm, ("xtok", half, j))
                    if j == 4:
                        for half in range(2):
                            b = opened(("btok", half), 5 + half)
                            for q in range(4):
                                mm = pe.transpose(b[:, P * q:P * (q + 1)], C[:, XS_T + q, P * half:P * (half + 1)],
                                                  ident)
                            full(mm, ("btok", half))
                        for a in range(2):
                            b = opened(("sbc", a), 3 + a)
                            for q in range(4):
                                mm = pe.transpose(b[0:8, P * q:P * (q + 1)], C[:, XS_T + 4 * a + q, SEQ:T], ident)
                            full(mm, ("sbc", a))
                    if j == 5:
                        for g in range(4):
                            b = opened(("cb", g), 3 + g)
                            pe.matmul(b[:, 0:SEQ], C[:, XS_T + g, 0:P], C[:, XS_T + 4 + g, 0:SEQ],
                                      start=True, stop=True)
                            full(pe.matmul(b[:, SEQ:3 * P], C[:, XS_T + g, P:SEQ], C[:, XS_T + 4 + g, P:SEQ],
                                           start=True, stop=True), ("cb", g))

            def ssd_bcast(u):
                for a in range(2):
                    b = opened(("acb", u, a), 3 + a)
                    for q in range(2):
                        h = 4 * u + 2 * a + q
                        o = b[:, SEQ * q:SEQ * (q + 1)]
                        pe.matmul(o, DTA[:, 0, h:h + 1].to_broadcast([P, P]), tab("causal")[:, 0:SEQ],
                                  start=True, stop=False)
                        mm = pe.matmul(o[:, P:SEQ], DTA[:, 1, h:h + 1].to_broadcast([P, P]),
                                       tab("causal")[:, 0:P], start=False, stop=True)
                    full(mm, ("acb", u, a))

            def ssd_y(u):
                pe.wait_ge(sem("decay_ready"), u + 1)
                D = tiles("S", 3 * P, 1536 * (u % 2), 1536 * (u % 2 + 1))
                b = opened(("y", u), 5)
                for q in range(4):
                    h = 4 * u + q
                    o = b[64 * (q % 2):64 * (q % 2) + 64, SEQ * (q // 2):SEQ * (q // 2 + 1)]
                    pe.matmul(o, XD[:, 0, HEADDIM * h:HEADDIM * (h + 1)], D[:, q, 0:SEQ], start=True, stop=False)
                    mm = pe.matmul(o[:, P:SEQ], XD[:, 1, HEADDIM * h:HEADDIM * (h + 1)], D[:, q, SEQ:3 * P],
                                   start=False, stop=True)
                full(mm, ("y", u))

            def qk(j):
                src, sq = (Q[:, j, :], QSQ[:, j, :]) if j < 8 else (KD[:, j - 8, :], KSQ[:, j - 8, :])
                if j == 0:
                    pe.wait_ge(sem("qk_squared"), 2)
                    pe.wait_ge(sem("qk_scaled"), 2)
                b = opened(("qk_ss", j), 6)
                full(pe.matmul(b[:, 0:T], tab("half_ones"), sq, start=True, stop=True), ("qk_ss", j))
                b = opened(("qk_rot", j), 7)
                full(pe.matmul(b[:, 0:T], tab("rot"), src, start=True, stop=True), ("qk_rot", j))

            def state(g):
                if g == 0:
                    pe.wait_ge(sem("xd_weighed"), 1)
                b = opened(("state", g), 3 + g % 2)
                for q in range(4):
                    j = 4 * g + q
                    for half in range(2):
                        mm = pe.matmul(b[:, P * q:P * (q + 1)], XD[:, half, P * j:P * (j + 1)],
                                       BT[:, half, P * g:P * (g + 1)], start=(half == 0), stop=(half == 1))
                full(mm, ("state", g))

            def swa_scores(u):
                g, blk = u // 2, u % 2
                for hh in range(2):
                    b = opened(("s", u, hh), 3 + hh)
                    rows = slice(64 * hh, 64 * hh + 64)
                    for jj in range(2):
                        for back in range(blk + 1):
                            mm = pe.matmul(b[:, 256 * jj + P * back:256 * jj + P * (back + 1)],
                                           Q[rows, 2 * g + jj, P * blk:P * (blk + 1)],
                                           KD[rows, g, P * (blk - back):P * (blk - back + 1)],
                                           start=True, stop=True)
                    full(mm, ("s", u, hh))

            def swa_turn(u):
                pe.wait_ge(sem("probs"), u + 1)
                p = SM.rearrange("p (k w) -> p k w", w=256)
                for back in range(u % 2 + 1):
                    b = opened(("pt", u, back), 5 + back)
                    for hh in range(2):
                        for jj in range(2):
                            mm = pe.transpose(b[:, P * (2 * hh + jj):P * (2 * hh + jj + 1)],
                                              p[:, 2 * jj + hh, P * back:P * (back + 1)], ident)
                    full(mm, ("pt", u, back))

            def swa_out(u):
                g, blk = u // 2, u % 2
                for back in range(blk + 1):
                    wait_drained(pe, ("pt", u, back))
                b = opened(("o", u), 7)
                for hh in range(2):
                    for back in range(blk + 1):
                        mm = pe.matmul(b[64 * hh:64 * hh + 64, 0:256], VT[:, blk - back, HD * g:HD * (g + 1)],
                                       PTs[:, 512 * back + 256 * hh:512 * back + 256 * (hh + 1)],
                                       start=(back == 0), stop=(back == blk))
                full(mm, ("o", u))

            def mem_scores(h):
                b = opened(("ms", h), 3)
                for qb in range(2):
                    for dt in range(2):
                        mm = pe.matmul(b[:, MEM * qb:MEM * (qb + 1)], MQ[:, 2 * h + dt, P * qb:P * (qb + 1)],
                                       MK[:, 2 * h + dt, :], start=(dt == 0), stop=(dt == 1))
                full(mm, ("ms", h))

            def mem_turn(h):
                pe.wait_ge(sem("probs"), 8 + h + 1)
                b = opened(("mpt", h), 5)
                for mt in range(2):
                    for qb in range(2):
                        mm = pe.transpose(b[:, P * (2 * mt + qb):P * (2 * mt + qb + 1)],
                                          SM[:, MEM * qb + P * mt:MEM * qb + P * (mt + 1)], ident)
                full(mm, ("mpt", h))

            def mem_out(h):
                wait_drained(pe, ("mpt", h))
                b = opened(("mo", h), 7)
                for dt in range(2):
                    for mt in range(2):
                        mm = pe.matmul(b[:, 256 * dt:256 * (dt + 1)],
                                       MV[:, mt, MEM_D * h + P * dt:MEM_D * h + P * (dt + 1)],
                                       PTs[:, 256 * mt:256 * (mt + 1)], start=(mt == 0), stop=(mt == 1))
                full(mm, ("mo", h))

            def sample_bc(b_):
                for a in range(2):
                    name = ("bb", b_, a)
                    b = opened(name, 3 + a)
                    full(pe.matmul(b[:, :], ident[0:8, b_:b_ + 1].to_broadcast([8, P]),
                                   SBC[:, 512 * a:512 * (a + 1)], start=True, stop=True), name)

            def ring_arrives(r):
                pe.wait_ge(sem(f"ring_in{r % 2}"), 16 * (r // 2 + 1) + 16 * BATCH_S * (r == 18))
                return RING[r % 2]

            def sample_mem_scores(b_):
                kc = ring_arrives(b_).rearrange("p (h dt m) -> p h dt m", dt=2, m=MEM)
                b = opened(("sms", b_), 6)
                for mt in range(2):
                    for h in range(MEM_H):
                        for dt in range(2):
                            mm = pe.matmul(b[:, 4 * mt + h:4 * mt + h + 1], kc[:, h, dt, P * mt:P * (mt + 1)],
                                           MQ[:, 2 * h + dt, SEQ + b_:SEQ + b_ + 1],
                                           start=(dt == 0), stop=(dt == 1))
                full(mm, ("sms", b_))

            def sample_swa_scores(part):
                ring_arrives(8 + part)
                pe.wait_ge(sem("new_key"), part + 1)
                kc = RING[part].rearrange("p (g b m) -> p g b m", b=4, m=P)
                for hh in range(2):
                    rows = slice(64 * hh, 64 * hh + 64)
                    b = opened(("sss", part, hh), 6 + hh)
                    for b_ in range(4):
                        for g in range(KV):
                            c0 = 8 * b_ + 2 * g
                            mm = pe.matmul(b[:, c0:c0 + 2], kc[rows, g, b_, :],
                                           Q[rows, 2 * g:2 * g + 2, SEQ + 4 * part + b_], start=True, stop=True)
                    full(mm, ("sss", part, hh))

            def sample_turn():
                wait_drained(pe, ("sms", BATCH_S - 1))
                b = opened("sct", 3)
                for mt in range(2):
                    mm = pe.transpose(b[0:32, P * mt:P * (mt + 1)], SC[:, 32 * mt:32 * (mt + 1)], ident)
                wait_drained(pe, ("sss", 1, 0))
                wait_drained(pe, ("sss", 1, 1))
                full(pe.transpose(b[:, 256:384], SC2, ident), "sct")

            def sample_back():
                pe.wait_ge(sem("sample_probs"), 2)
                b = opened("spt", 4)
                for mt in range(2):
                    pe.transpose(b[:, 32 * mt:32 * (mt + 1)], SM[0:32, P * mt:P * (mt + 1)], ident[0:32, 0:32])
                full(pe.transpose(b[:, 64:192], SM[:, 256:384], ident), "spt")

            def sample_mem_out(b_):
                vc = ring_arrives(10 + b_).rearrange("p (mt n) -> p mt n", mt=2)
                if b_ == 0:
                    wait_drained(pe, "spt")
                b = opened(("smo", b_), 5)
                for h in range(MEM_H):
                    for dt in range(2):
                        c = 2 * h + dt
                        for mt in range(2):
                            mm = pe.matmul(b[:, c:c + 1], vc[:, mt, P * c:P * (c + 1)],
                                           PTs[:, 32 * mt + 4 * b_ + h:32 * mt + 4 * b_ + h + 1],
                                           start=(mt == 0), stop=(mt == 1))
                full(mm, ("smo", b_))

            def sample_swa_out():
                vc = ring_arrives(18).rearrange("p (b n) -> p b n", b=BATCH_S)
                b = opened("sso", 6)
                for b_ in range(BATCH_S):
                    for g in range(KV):
                        for hh in range(2):
                            c0 = 64 + 16 * b_ + 4 * g + 2 * hh
                            mm = pe.matmul(b[64 * hh:64 * hh + 64, 8 * b_ + 2 * g:8 * b_ + 2 * g + 2],
                                           vc[:, b_, HD * g:HD * (g + 1)], PTs[:, c0:c0 + 2],
                                           start=True, stop=True)
                full(mm, "sso")

            for i in range(40):
                name = ("z", i // 2) if i < 16 else ("gate", (i - 16) // 2)
                w = arrive(name)
                feature_tile(("zg", i), w, i % 2, HN, T, name)
                if i < 8:
                    ssd_bcast(i)
                if 1 <= i < 9:
                    ssd_y(i - 1)
                if i < 12:
                    qk(i)
                if 10 <= i < 14:
                    state(i - 10)
                if i in (12, 13):
                    for h in (2 * i - 24, 2 * i - 23):
                        if h == 0:
                            pe.wait_ge(sem("mq_squared"), 1)
                        squares(("ss_mq", h), 6 + h % 2, QSQ, 2 * h, 2, T)
                if i == 14:
                    pe.wait_ge(sem("qk_ready"), 12)
                if 14 <= i < 22:
                    swa_scores(i - 14)
                if 15 <= i < 23:
                    swa_turn(i - 15)
                if 16 <= i < 24:
                    swa_out(i - 16)
                if i == 23:
                    pe.wait_ge(sem("mq_ready"), 1)
                    pe.wait_ge(sem("mk_ready"), 1)
                if 23 <= i < 27:
                    mem_scores(i - 23)
                if 24 <= i < 28:
                    mem_turn(i - 24)
                if 25 <= i < 29:
                    mem_out(i - 25)
                if 14 <= i < 38 and (i - 14) % 3 == 0:
                    sample_bc((i - 14) // 3)
                if 24 <= i < 32:
                    sample_mem_scores(i - 24)
                if i in (32, 33):
                    sample_swa_scores(i - 32)
                if i == 35:
                    sample_turn()
                if i == 37:
                    sample_back()
                if 38 <= i:
                    sample_mem_out(2 * (i - 38))
                    sample_mem_out(2 * (i - 38) + 1)
            for b_ in range(4, BATCH_S):
                sample_mem_out(b_)
            sample_swa_out()

            wait_drained(pe, ("mo", 3))
            wait_drained(pe, ("smo", BATCH_S - 1))
            wait_drained(pe, "sso")
            for i in range(4):
                for kind, x in (("swa", Q), ("memb", MQ)):
                    w = arrive((kind, i))
                    for c in range(2):
                        feature_tile((kind, 2 * i + c), w, c, x, T, (kind, i))
            pe.wait_ge(sem("y_squared"), 1)
            squares("ss_y", 3, X, 0, XS_T, T)
            pe.wait_ge(sem("y_ready"), 1)
            for i in range(4):
                wa = arrive(("ssma", i))
                wb = arrive(("ssmb", i))
                for c in range(2):
                    name = ("ssm", 2 * i + c)
                    b = next_proj(name)
                    for k in range(XS_T):
                        w = wa if k < KT else wb
                        mm = pe.matmul(b[:, 0:T], w[:, k % KT, P * c:P * (c + 1)], C[:, k, :],
                                       start=(k == 0), stop=(k == XS_T - 1))
                    full(mm, name)
                    last_use[("ssma", i)] = last_use[("ssmb", i)] = name
            pe.wait_ge(sem("merged"), 8)
            for i in range(4):
                w = arrive(("out", i))
                for c in range(2):
                    feature_tile(("out", 2 * i + c), w, c, MERGED, T, ("out", i))
            pe.wait_ge(sem("x1_squared"), 1)
            squares("ss_x1", 4, X, 0, KT, T)
            pe.wait_ge(sem("h_ready"), 1)
            pe.wait_ge(sem("router_in"), 16)
            b = opened("route", 5)
            for t, rows in enumerate((P, P, BATCH_S)):
                for k in range(KT):
                    mm = pe.matmul(b[0:rows, 64 * t:64 * t + ROUTES], HT[:, k, P * t:P * t + rows],
                                   WR[:, k, :], start=(k == 0), stop=(k == KT - 1))
            full(mm, "route")
            pe.wait_ge(sem("comb"), 1)
            b = opened("combT", 6)
            for t, rows in enumerate((P, P, BATCH_S)):
                mm = pe.transpose(b[0:32, P * t:P * t + rows], COMB[0:rows, t, :], ident[0:rows, 0:rows])
            full(mm, "combT")
            wait_drained(pe, "combT")
            for e in range(EXPERTS):
                b = opened(("comb", e), 3 + e % 4)
                full(pe.matmul(b[:, 0:T], ident[0:32, e:e + 1].to_broadcast([32, P]), COMBT,
                               start=True, stop=True), ("comb", e))

            pe.wait_ge(drained[0], uses[0])
            for b in range(8):
                if uses[b]:
                    pe.wait_ge(drained[b], uses[b])
            pe.sem_inc(down_filled[3], 1)
            with pe.Fori(0, EXPERTS // MOE_BUFS) as it:
                for j in range(MOE_BUFS):
                    e = it * MOE_BUFS + j
                    gate, up, down = expert_weights(j)
                    pe.wait_ge(expert_in[j], it * 48 + 48)
                    for f in range(FF_T):
                        for which, w in ((0, gate), (1, up)):
                            bank = 2 * f + which
                            if which == 0:
                                pe.wait_ge(half_free[f], e + 1)
                            for k in range(KT):
                                mm = pe.matmul(psum[bank][:, 0:T], w[:, k, P * f:P * (f + 1)], HT[:, k, :],
                                               start=(k == 0), stop=(k == KT - 1))
                            mm.then_inc(sem(f"expert_{('gate', 'up')[which]}{f}"), 1)
                    for r in range(2):
                        for f in range(FF_T):
                            if r == 0:
                                pe.wait_ge(act_ready[f], e + 2)
                            for q in range(4):
                                if f == 0:
                                    pe.wait_ge(down_read[q], e * 2 + (r + 1))
                                mm = pe.matmul(psum[4 + q][:, 0:T], down[:, f, P * (4 * r + q):P * (4 * r + q + 1)],
                                               ACTT[f][:, 0:T], start=(f == 0), stop=(f == 1))
                                if f == 1:
                                    mm.then_inc(down_filled[q], 1)

        @block.sync
        def _(sp):
            sp.dma_start(at("tab"), ins["tables"]).then_inc(sem("tables_in"), 16)
            sp.dma_start(at("vec"), ins["vectors"]).then_inc(sem("tables_in"), 16)
            sp.dma_start(XT, ins["xT"]).then_inc(sem("x_in"), 16)
            sp.dma_start(MT, ins["memT"]).then_inc(sem("mem_in"), 16)

            def load_chunk(n):
                name, parts = chunks[n]
                if n >= WBUFS:
                    wait_filled(sp, last_use[chunks[n - WBUFS][0]])
                for src, c0, width in parts:
                    if name == ("dt", 0):
                        off = MAP["W"][0] + CHUNK * (n % WBUFS)
                        dst = M[:, off:off + KT * width].rearrange("p (k n) -> p k n", n=width)
                    else:
                        dst = chunk(n)[:, :, c0:c0 + width]
                    sp.dma_start(dst, src).then_inc(chunk_in[n % WBUFS], 16)

            def load_ring(r):
                dst = RING[r % 2]
                if r == 0:
                    for g in range(4):
                        wait_filled(sp, ("cb", g))
                    for a in range(2):
                        wait_filled(sp, ("sbc", a))
                        wait_filled(sp, ("btok", a))
                elif r == 1:
                    wait_filled(sp, ("state", 3))
                elif r < 10:
                    wait_filled(sp, ("sms", r - 2))
                elif r < 12:
                    wait_filled(sp, ("sss", r - 10, 1))
                    sp.wait_ge(sem(f"s_k_out{r - 10}"), 16)
                else:
                    wait_filled(sp, ("smo", r - 12))
                if r < 8:
                    src = ins["mem_kT"][r]
                elif r < 10:
                    src = ins["swa_kT"][r - 8]
                elif r < 18:
                    src = ins["mem_v"][r - 10]
                else:
                    src = ins["swa_v"]
                sp.dma_start(dst, src).then_inc(sem(f"ring_in{r % 2}"), 16)
                if r == 18:
                    sp.wait_ge(sem("ring_in0"), 160)
                    wait_drained(sp, ("v", 2))
                    for b_ in range(BATCH_S):
                        sp.dma_start(dst[0:1, 256 * b_:256 * (b_ + 1)], VT[b_:b_ + 1, 2, :]
                                     ).then_inc(sem("ring_in0"), 16)

            first_z = number[("z", 0)]
            r = 0
            for n in range(number[("swa", 0)]):
                load_chunk(n)
                m = n - first_z
                while r < 12 and m >= 0 and m >= (27 + r) / 2 - (5 if r < 2 else 0):
                    load_ring(r)
                    r += 1
            while r < 19:
                load_ring(r)
                r += 1
            for n in range(number[("swa", 0)], number[("out", 0)]):
                load_chunk(n)
            wait_filled(sp, ("zg", 39))
            sp.dma_start(HN, ins["xT"]).then_inc(sem("x_again"), 16)
            for n in range(number[("out", 0)], len(chunks)):
                load_chunk(n)

            def load_expert(e, j):
                gate, up, down = expert_weights(j)
                for dst, src, p in ((gate, ins["w_exp_gate"], "(k p) f -> p k f"), (up, ins["w_exp_up"], "(k p) f -> p k f"),
                                    (down, ins["w_exp_down"], "(k p) f -> p k f")):
                    sp.dma_start(dst, src[e].rearrange(p, p=P)).then_inc(expert_in[j], 16)

            wait_filled(sp, ("memb", 7))
            sp.wait_ge(sem("s_v_out"), 16)
            sp.wait_ge(sem("y_gated"), 1)
            load_expert(0, 0)
            sp.wait_ge(sem("merged"), 8)
            load_expert(1, 1)
            wait_filled(sp, ("out", 7))
            load_expert(2, 2)
            wait_filled(sp, "ss_x1")
            load_expert(3, 3)
            with sp.Fori(1, EXPERTS // MOE_BUFS) as it:
                for j in range(MOE_BUFS):
                    sp.wait_ge(down_filled[3], it * (2 * MOE_BUFS) + (2 * j + 3 - 2 * MOE_BUFS))
                    load_expert(it * MOE_BUFS + j, j)
            for q in range(4):
                sp.wait_ge(down_read[q], 2 * EXPERTS + 1)
            sp.dma_start(outs["yT"], X1).then_inc(sem("y_out"), 16)
            sp.wait_ge(sem("y_out"), 16)

        @block.gpsimd
        def _(pool):
            pool.wait_ge(sem("mk_ready"), 1)
            pool.dma_start(outs["p_mem_kT"], MK).then_inc(sem("p_mem_out"), 16)
            pool.dma_start(HIST, ins["histT"]).then_inc(sem("hist_in"), 16)
            for i in range(4):
                for mt in range(2):
                    wait_drained(pool, ("mv", i, mt))
            pool.dma_start(outs["p_mem_v"], MV).then_inc(sem("p_mem_out"), 16)
            for t in range(3):
                wait_drained(pool, ("v", t))
            pool.dma_start(outs["p_swa_v"], VT[:, 1, :]).then_inc(sem("p_v_out"), 16)
            pool.wait_ge(sem("new_conv"), 1)
            pool.dma_start(outs["newconvT"], NEWC).then_inc(sem("conv_out"), 16)

            def load_state(b):
                if b >= 2:
                    pool.wait_ge(sem(f"s_ssm_out{b % 2}"), 16 * (b // 2))
                pool.dma_start(HS[b % 2], ins["state_ssm"][b].rearrange("(j p) n -> p j n", p=P)
                               ).then_inc(sem(f"state_in{b % 2}"), 16)

            pool.wait_ge(sem("conv_active"), 3)
            load_state(0)
            load_state(1)
            pool.wait_ge(sem("qk_ready"), 12)
            pool.dma_start(outs["p_swa_kT"], KD[0:64, :, P:SEQ]).then_inc(sem("p_k_out"), 16)
            for g in range(4):
                wait_drained(pool, ("state", g))
            pool.dma_start(outs["p_ssm"].rearrange("(j p) n -> p j n", p=P),
                           at("S", 0, 2048).rearrange("p (j n) -> p j n", n=STATE)).then_inc(sem("p_ssm_out"), 16)

            def store_state(b):
                pool.wait_ge(sem("state_new"), b + 1)
                pool.dma_start(outs["s_ssm"][b].rearrange("(j p) n -> p j n", p=P), HS[b % 2]
                               ).then_inc(sem(f"s_ssm_out{b % 2}"), 16)

            for b in range(BATCH_S):
                store_state(b)
                if b + 2 < BATCH_S:
                    pool.wait_ge(sem("sample_y"), b + 1)
                    load_state(b + 2)
                if b == 5:
                    for part in range(2):
                        pool.wait_ge(sem("new_key"), part + 1)
                        pool.dma_start(outs["s_swa_kT"][part], RING[part][0:64, :]).then_inc(sem(f"s_k_out{part}"), 16)
            pool.wait_ge(sem("ring_in0"), 160 + 16 * BATCH_S)
            pool.dma_start(outs["s_swa_v"], RING[0]).then_inc(sem("s_v_out"), 16)
            pool.wait_ge(sem("samples_done"), 1)
            pool.dma_start(WR, ins["w_router"].rearrange("(k p) n -> p k n", p=P)).then_inc(sem("router_in"), 16)
            for name, n in (("p_mem_out", 32), ("p_v_out", 16), ("conv_out", 16), ("p_k_out", 16), ("p_ssm_out", 16),
                            ("s_ssm_out0", 64), ("s_ssm_out1", 64), ("s_k_out0", 16), ("s_k_out1", 16), ("s_v_out", 16)):
                pool.wait_ge(sem(name), n)

        @block.scalar
        def _(act):
            a = nc.scalar

            def evac(name, dst, n, rows=P, src=None):
                b = wait_filled(act, name)
                drains(a.activation(dst, b[0:rows, 0:n] if src is None else src(b), ACT.Copy), name)

            def rstd(name, dst, width, n):
                b = wait_filled(act, name)
                a.preload_act_table_set("natural_log_exp_and_others")
                drains(a.activation(dst, b[:, 0:n], ACT.Ln, scale=1.0 / width, bias=EPS), name)
                wait_drained(act, name)
                done(act, a.activation(dst, dst, ACT.Exp, scale=-0.5), "rstd")

            act.wait_ge(sem("x_in"), 16)
            a.activation(XSQ, XT, ACT.Square).then_inc(sem("x_squared"), 1)
            act.wait_ge(sem("mem_in"), 16)
            a.activation(MSQ, MT, ACT.Square).then_inc(sem("mem_squared"), 1)
            rstd("ss_x", RS, D_MODEL, T)
            rstd("ss_mem", TQ[:, 0:MEM], D_MODEL, MEM)
            for j in range(8):
                evac(("mk", j), MK[:, j, :], MEM)
            wait_drained(act, ("mk", 7))
            a.activation(MSQ, MK, ACT.Square).then_inc(sem("mk_squared"), 1)
            for i in range(4):
                for mt in range(2):
                    evac(("mv", i, mt), MV[:, mt, CW * i:CW * (i + 1)], CW)
            for h in range(MEM_H):
                rstd(("ss_mk", h), RSM[:, h, :], MEM_D, MEM)

            def silu_conv(batch):
                act.wait_ge(sem("convolved"), batch + 1)
                v = C[:, 8 * batch:8 * (batch + 1), :]
                a.activation(v, v, ACT.Silu).then_inc(sem("conv_active"), 1)

            for j in range(CONV_T):
                evac(("xbc", j), X[:, j, :], T)
                if j == 13:
                    silu_conv(0)
                if j == 21:
                    silu_conv(1)
            for j in range(KV):
                evac(("kd", j), KD[:, j, :], T)
            wait_drained(act, ("kd", 3))
            a.activation(KSQ, KD, ACT.Square).then_inc(sem("qk_squared"), 1)
            for t, rows in enumerate((P, P, BATCH_S)):
                evac(("v", t), VT[0:rows, t, :], CW, rows)
            act.wait_ge(sem("dt_minus_abs"), 1)
            a.preload_act_table_set("natural_log_exp_and_others")
            E1, U1, L1 = (at("S", 96 * i, 96 * (i + 1)) for i in range(1, 4))
            done(act, a.activation(E1, E1, ACT.Exp), "dt_exp")
            act.wait_ge(sem("dt_one_plus"), 1)
            done(act, a.activation(L1, U1, ACT.Ln), "dt_ln")
            a.activation(at("S", 384, 384 + 32), vec("a_log"), ACT.Exp).then_inc(sem("a_exp"), 1)
            act.wait_ge(sem("dta"), 1)
            a.activation(at("S", 416, 448, 8), DTA[0:8, 2, :], ACT.Exp).then_inc(sem("da_exp"), 1)
            for j in range(8):
                evac(("q", j), Q[:, j, :], T)
                if j == 1:
                    silu_conv(2)
            wait_drained(act, ("q", 7))
            a.activation(QSQ, Q, ACT.Square).then_inc(sem("qk_squared"), 1)
            act.wait_ge(sem("to_end"), 1)
            a.activation(WE, WE, ACT.Exp).then_inc(sem("end_decay"), 1)
            for j in range(8):
                evac(("mq", j), MQ[:, j, :], T)
                if j == 4:
                    for half in range(2):
                        evac(("btok", half), BT[:, half, :], 512)
                    for k in range(2):
                        evac(("sbc", k), SBC[:, 512 * k:512 * (k + 1)], 512, 8)

            for i in range(42):
                if i < 40:
                    evac(("zg", i), Z[:, i, :] if i < 16 else G[:, i - 16, :], T)
                if i < 8:
                    act.wait_ge(sem("segments"), i + 1)
                    D = at("S", 1536 * (i % 2), 1536 * (i % 2 + 1))
                    a.activation(D, D, ACT.Exp).then_inc(sem("decay_exp"), 1)
                if i < 12:
                    if i:
                        act.wait_ge(sem("qk_ready"), i)
                    rstd(("qk_ss", i), RS, HD, T)
                if i == 9:
                    wait_filled(act, ("qk_ss", 7))
                    wait_drained(act, ("mq", 7))
                    a.activation(QSQ, MQ, ACT.Square).then_inc(sem("mq_squared"), 1)
                if 10 <= i < 14:
                    if i == 10:
                        wait_filled(act, ("y", 7))
                    g = i - 10
                    evac(("state", g), at("S", 512 * g, 512 * (g + 1)), 512)
                if i in (12, 13):
                    for h in (2 * i - 24, 2 * i - 23):
                        if h == 0:
                            act.wait_ge(sem("qk_ready"), 12)
                        else:
                            act.wait_ge(sem("mq_scaled"), h)
                        rstd(("ss_mq", h), RS, MEM_D, T)
                if 16 <= i < 24:
                    u = i - 16
                    g, blk = u // 2, u % 2
                    evac(("o", u), Q[:, 2 * g:2 * g + 2, P * blk:P * (blk + 1)], 256,
                         src=lambda b: b[:, 0:256].rearrange("p (j q) -> p j q", j=2))
                if 25 <= i < 29:
                    h = i - 25
                    evac(("mo", h), MQ[:, 2 * h:2 * h + 2, 0:SEQ], 512,
                         src=lambda b: b[:, :].rearrange("p (j q) -> p j q", j=2))
                if 14 <= i < 22:
                    u = i - 14
                    width = P * (u % 2 + 1)
                    act.wait_ge(sem("swa_max"), u + 1)
                    for k in range(4):
                        p = SM[:, 256 * k:256 * k + width]
                        a.activation(p, p, ACT.Exp, bias=at("ST", 4 + k, 5 + k), accum_out=at("ST", 8 + k, 9 + k))
                    a.activation(at("ST", 12, 16), at("ST", 12, 16), ACT.Exp).then_inc(sem("exps"), 1)
                if 23 <= i < 27:
                    h = i - 23
                    act.wait_ge(sem("mem_max"), h + 1)
                    if h:
                        wait_filled(act, ("mpt", h - 1))
                    else:
                        wait_filled(act, ("pt", 7, 1))
                    b = wait_filled(act, ("ms", h))
                    a.activation(SM[:, 0:MEM], b[:, 0:MEM], ACT.Exp, bias=at("ST", 20, 21), scale=MEM_D ** -0.5,
                                 accum_out=at("ST", 24, 25)).then_inc(sem("mem_exp0"), 1)
                    done(act, a.activation(SM[:, MEM:2 * MEM], b[:, MEM:2 * MEM], ACT.Exp, bias=at("ST", 21, 22),
                                           scale=MEM_D ** -0.5, accum_out=at("ST", 25, 26)), "exps")
                if 14 <= i < 38 and (i - 14) % 3 == 0:
                    b_ = (i - 14) // 3
                    if b_ == 0:
                        act.wait_ge(sem("p_ssm_out"), 16)
                    else:
                        act.wait_ge(sem("sample_y"), b_)
                    for k in range(2):
                        evac(("bb", b_, k), BB[:, 512 * k:512 * (k + 1)], 512)
                if 24 <= i < 32:
                    b_ = i - 24
                    evac(("sms", b_), SC.rearrange("p (mt b h) -> p mt b h", mt=2, h=MEM_H)[:, :, b_, :], 8,
                         src=lambda b: b[:, 0:8].rearrange("p (mt h) -> p mt h", mt=2))
                if i in (32, 33):
                    for hh in range(2):
                        dst = SC2[:, 64 * (i - 32):64 * (i - 31)].rearrange("p (bg hh jj) -> p bg hh jj", hh=2, jj=2)
                        evac(("sss", i - 32, hh), dst[:, :, hh, :], 32,
                             src=lambda b: b[:, 0:32].rearrange("p (bg jj) -> p bg jj", jj=2))
                if i == 36:
                    act.wait_ge(sem("sample_max"), 1)
                    b = wait_filled(act, "sct")
                    wait_filled(act, ("mpt", 3))
                    a.activation(SM[0:32, 0:MEM], b[0:32, 0:MEM], ACT.Exp, bias=at("ST", 32, 33, 32),
                                 scale=MEM_D ** -0.5, accum_out=at("ST", 34, 35, 32)).then_inc(sem("sexp0"), 1)
                    a.activation(SM[:, 256:384], b[:, 256:384], ACT.Exp, bias=at("ST", 33, 34),
                                 scale=HD ** -0.5, accum_out=at("ST", 35, 36)).then_inc(sem("sexp1"), 1)
                    a.activation(at("ST", 36, 37), at("ST", 36, 37), ACT.Exp).then_inc(sem("sample_exps"), 1)
                if i in (38, 39):
                    for b_ in (2 * (i - 38), 2 * (i - 38) + 1):
                        evac(("smo", b_), MQ[:, 0:8, SEQ + b_], 8)
            for b_ in range(4, BATCH_S):
                evac(("smo", b_), MQ[:, 0:8, SEQ + b_], 8)
            evac("sso", Q[:, 0:8, SEQ:T].rearrange("p t b -> p b t"), 64,
                 src=lambda b: b[:, 0:64].rearrange("p (b t) -> p b t", b=BATCH_S))
            wait_drained(act, ("zg", 39))
            wait_drained(act, ("zg", 38))
            wait_drained(act, ("zg", 37))
            a.activation(at("Z"), at("Z"), ACT.Silu).then_inc(sem("z_active"), 1)
            a.activation(at("G"), at("G"), ACT.Sigmoid).then_inc(sem("gates_active"), 1)
            act.wait_ge(sem("y_gated"), 1)
            act.wait_ge(sem("s_ssm_out0"), 64)
            act.wait_ge(sem("s_ssm_out1"), 64)
            a.activation(X[:, 0:XS_T, :], C[:, 0:XS_T, :], ACT.Square).then_inc(sem("y_squared"), 1)
            rstd("ss_y", RS, D_INNER, T)
            act.wait_ge(sem("x1_made"), 1)
            a.activation(X[:, 0:KT, :], X1, ACT.Square).then_inc(sem("x1_squared"), 1)
            rstd("ss_x1", RS, D_MODEL, T)
            act.wait_ge(sem("route_args"), 1)
            done(act, a.activation(at("S", 1100, 1112), at("S", 1100, 1112), ACT.Exp), "route_exp")
            done(act, a.activation(at("S", 1112, 1115), at("S", 1112, 1115), ACT.Exp), "route_exp")
            for e in range(EXPERTS):
                if e % 2:
                    evac(("comb", e), COMBB[:, T * e:T * (e + 1)], T)
            with act.Fori(0, EXPERTS) as e:
                for f in range(FF_T):
                    act.wait_ge(sem(f"expert_gate{f}"), e + 1)
                    act.wait_ge(act_ready[f], e + 1)
                    a.activation(SG[f], psum[2 * f][:, 0:T], ACT.Silu).then_inc(sem(f"silu{f}"), 1)

        @block.vector
        def _(dve):
            v = nc.vector

            def link(ins_):
                done(dve, ins_, "vector_chain")

            dve.wait_ge(sem("tables_in"), 32)
            dve.wait_ge(sem("x_in"), 16)
            dve.wait_ge(sem("rstd"), 1)
            link(v.tensor_tensor(HN, XT, each(RS, KT), ALU.mult))
            v.tensor_tensor(HN, HN, over(vec("g1"), T), ALU.mult).then_inc(sem("x_normed"), 1)
            dve.wait_ge(sem("mem_in"), 16)
            dve.wait_ge(sem("rstd"), 2)
            link(v.tensor_tensor(MN, MT, each(TQ[:, 0:MEM], KT), ALU.mult))
            v.tensor_tensor(MN, MN, over(vec("gmem"), MEM), ALU.mult).then_inc(sem("mem_normed"), 1)
            for h in range(MEM_H):
                dve.wait_ge(sem("rstd"), 3 + h)
                for dt in range(2):
                    t = MK[:, 2 * h + dt, :]
                    last = v.scalar_tensor_tensor(t, t, vec("gmk", dt, dt + 1), RSM[:, h, :], ALU.mult, ALU.mult)
            last.then_inc(sem("mk_ready"), 1)

            def tap(j, k):
                a_, _n = VEC["conv_w"]
                return at("vec", a_ + CONV_T * k + j, a_ + CONV_T * k + j + 1)

            def conv(batch):
                js = range(8 * batch, 8 * (batch + 1))
                wait_drained(dve, ("xbc", js[-1]))
                wait_drained(dve, ("xbc", js[-2]))
                wait_drained(dve, ("xbc", js[-3]))
                for j in js:
                    last = v.tensor_scalar(C[:, j, 0:SEQ], X[:, j, 0:SEQ], tap(j, 3), vec("conv_b", j, j + 1),
                                           ALU.mult, ALU.add)
                link(last)
                for back in range(1, CONV_TAPS):
                    for j in js:
                        last = v.scalar_tensor_tensor(C[:, j, back:SEQ], X[:, j, 0:SEQ - back], tap(j, 3 - back),
                                                      C[:, j, back:SEQ], ALU.mult, ALU.add)
                    link(last)
                cs, xs_ = C[:, js[0]:js[-1] + 1, SEQ:T], X[:, js[0]:js[-1] + 1, SEQ:T]
                tmp = at("S", 512, 512 + 64).rearrange("p (j b) -> p j b", b=BATCH_S)

                def w(k):
                    return over(vec("conv_w", CONV_T * k + js[0], CONV_T * k + js[-1] + 1), BATCH_S)

                link(v.tensor_tensor(cs, xs_, w(3), ALU.mult))
                dve.wait_ge(sem("hist_in"), 16)
                for k in range(3):
                    link(v.tensor_tensor(tmp, HIST[:, js[0]:js[-1] + 1, :, k], w(k), ALU.mult))
                    link(v.tensor_tensor(cs, cs, tmp, ALU.add))
                done(dve, v.tensor_tensor(cs, cs, over(vec("conv_b", js[0], js[-1] + 1), BATCH_S), ALU.add),
                     "convolved")

            conv(0)
            conv(1)
            conv(2)
            new = NEWC[:, :, 0:24].rearrange("p j (b k) -> p j b k", k=3)
            link(v.tensor_copy(new[:, :, :, 0:2], HIST[:, :, :, 1:3]))
            link(v.tensor_copy(new[:, :, :, 2], X[:, :, SEQ:T]))
            done(dve, v.tensor_copy(NEWC[:, :, 24:27], X[:, :, SEQ - 3:SEQ]), "new_conv")

            R0, E1, U1, L1 = (at("S", 96 * i, 96 * (i + 1)) for i in range(4))
            AEXP, DAS = at("S", 384, 416), at("S", 416, 448, 8)
            R3 = R0.rearrange("p (t h) -> p t h", t=3)
            link(v.memset(R0, 0.0))
            b = wait_filled(dve, "dt")
            link(v.tensor_tensor(R3[:, 0:2, :], b[:, 0:64].rearrange("p (t h) -> p t h", t=2),
                                 each(vec("dt_bias"), 2), ALU.add))
            drains(v.tensor_tensor(R3[0:8, 2, :], b[0:8, 64:96], vec("dt_bias", rows=8), ALU.add), "dt")
            wait_drained(dve, "dt")
            link(v.tensor_scalar(E1, R0, -1.0, None, ALU.mult))
            done(dve, v.tensor_tensor(E1, E1, R0, ALU.min), "dt_minus_abs")
            dve.wait_ge(sem("dt_exp"), 1)
            done(dve, v.tensor_scalar(U1, E1, 1.0, None, ALU.add), "dt_one_plus")
            link(v.tensor_scalar(at("S", 448, 544), U1, -1.0, None, ALU.add))
            link(v.tensor_scalar(at("S", 544, 640), at("S", 448, 544), 0.0, None, ALU.is_equal))
            link(v.tensor_tensor(at("S", 448, 544), at("S", 448, 544), at("S", 544, 640), ALU.add))
            link(v.reciprocal(at("S", 448, 544), at("S", 448, 544)))
            dve.wait_ge(sem("dt_ln"), 1)
            link(v.tensor_tensor(L1, L1, at("S", 544, 640), ALU.add))
            link(v.tensor_tensor(L1, L1, E1, ALU.mult))
            link(v.tensor_tensor(L1, L1, at("S", 448, 544), ALU.mult))
            link(v.tensor_scalar(R0, R0, 0.0, None, ALU.max))
            link(v.tensor_tensor(at("DT"), R0, L1, ALU.add))
            dve.wait_ge(sem("a_exp"), 1)
            link(v.tensor_tensor(DTA, DT, each(AEXP, 3), ALU.mult))
            done(dve, v.tensor_scalar(at("DTA"), at("DTA"), -1.0, None, ALU.mult), "dta")
            dve.wait_ge(sem("da_exp"), 1)
            link(v.tensor_copy(DTX.rearrange("p (h d) -> p h d", d=HEADDIM), over(DT[0:8, 2, :], HEADDIM)))
            done(dve, v.tensor_copy(DAX.rearrange("p (h d) -> p h d", d=HEADDIM), over(DAS, HEADDIM)), "dt_expanded")
            b = wait_filled(dve, "acum")
            link(v.tensor_copy(at("AC"), b[:, 0:64]))
            drains(v.tensor_tensor(WE, each(b[:, 64:96], 2), AC, ALU.subtract), "acum")
            wait_drained(dve, "acum")
            done(dve, v.tensor_scalar(at("WE"), at("WE"), 0.0, None, ALU.min), "to_end")
            b = wait_filled(dve, "ex")
            drains(v.tensor_copy(at("EX"), b[:, 0:256]), "ex")
            wait_drained(dve, "ex")
            dve.wait_ge(sem("qk_squared"), 2)
            done(dve, v.tensor_scalar(at("KD"), at("KD"), vec("gk"), None, ALU.mult), "qk_scaled")
            done(dve, v.tensor_scalar(at("Q"), at("Q"), vec("gq"), None, ALU.mult), "qk_scaled")
            dve.wait_ge(sem("conv_active"), 3)
            link(v.tensor_tensor(XS, C[:, 0:XS_T, SEQ:T], EX[:, 0, :, :], ALU.mult))
            for j in range(4):
                for half in range(2):
                    b = wait_filled(dve, ("xtok", half, j))
                    drains(v.tensor_tensor(XD[:, half, 512 * j:512 * (j + 1)].rearrange("p (h d) -> p h d", d=HEADDIM),
                                           b[:, :].rearrange("p (h d) -> p h d", d=HEADDIM),
                                           over(DT[:, half, 8 * j:8 * (j + 1)], HEADDIM), ALU.mult),
                           ("xtok", half, j))
            for g in range(4):
                b = wait_filled(dve, ("cb", g))
                drains(v.tensor_tensor(CB[:, g, :], b[:, 0:3 * P], tab("causal"), ALU.mult), ("cb", g))
                wait_drained(dve, ("cb", g))

            def segments(u):
                if u >= 2:
                    wait_filled(dve, ("y", u - 2))
                D = tiles("S", 3 * P, 1536 * (u % 2), 1536 * (u % 2 + 1))
                for a_ in range(2):
                    b = wait_filled(dve, ("acb", u, a_))
                    for q in range(2):
                        h = 4 * u + 2 * a_ + q
                        o = b[:, SEQ * q:SEQ * (q + 1)]
                        v.tensor_scalar(D[:, 2 * a_ + q, 0:SEQ], o, AC[:, 0, h:h + 1], 0.0,
                                        ALU.subtract, ALU.min)
                        last = v.tensor_scalar(D[:, 2 * a_ + q, SEQ:3 * P], o[:, P:SEQ], AC[:, 1, h:h + 1], 0.0,
                                               ALU.subtract, ALU.min)
                    if a_ == 0:
                        drains(last, ("acb", u, 0))
                drains(last, ("acb", u, 1))
                wait_drained(dve, ("acb", u, 1))
                done(dve, v.tensor_scalar(at("ST", 60, 61), AC[:, 0, 0:1], 0.0, None, ALU.mult), "segments")

            def decays(u):
                dve.wait_ge(sem("decay_exp"), u + 1)
                D = tiles("S", 3 * P, 1536 * (u % 2), 1536 * (u % 2 + 1))
                done(dve, v.tensor_tensor(D, D, each(CB[:, u // 2, :], 4), ALU.mult), "decay_ready")

            def y_add(u):
                b = wait_filled(dve, ("y", u))
                for q in range(2):
                    j = 2 * u + q
                    last = v.scalar_tensor_tensor(C[:, j, 0:SEQ], C[:, j, 0:SEQ], vec("ssm_d", j, j + 1),
                                                  b[:, SEQ * q:SEQ * (q + 1)], ALU.mult, ALU.add)
                drains(last, ("y", u))

            def rotate(j):
                src = Q[:, j, :] if j < 8 else KD[:, j - 8, :]
                b = wait_filled(dve, ("qk_rot", j))
                drains(v.tensor_tensor(TQ, b[:, 0:T], tab("sin"), ALU.mult), ("qk_rot", j))
                wait_drained(dve, ("qk_rot", j))
                link(v.tensor_tensor(src, src, tab("cos"), ALU.mult))
                link(v.tensor_tensor(src, src, TQ, ALU.add))
                dve.wait_ge(sem("rstd"), 7 + j)
                done(dve, v.tensor_tensor(src, src, RS, ALU.mult), "qk_ready")

            def swa_max(u):
                g, blk = u // 2, u % 2
                width = P * (blk + 1)
                if u:
                    for back in range((u - 1) % 2 + 1):
                        wait_filled(dve, ("pt", u - 1, back))
                for hh in range(2):
                    b = wait_filled(dve, ("s", u, hh))
                    for jj in range(2):
                        k = 2 * jj + hh
                        h = 4 * g + k
                        last = v.tensor_tensor_reduce(SM[:, 256 * k:256 * k + width],
                                                      b[:, 256 * jj:256 * jj + width],
                                                      tab("window")[:, 0:width], HD ** -0.5, vec("sink", h, h + 1),
                                                      ALU.add, ALU.max, at("ST", k, k + 1))
                    drains(last, ("s", u, hh))
                    wait_drained(dve, ("s", u, hh))
                link(v.tensor_scalar(at("ST", 4, 8), at("ST", 0, 4), -1.0, None, ALU.mult))
                done(dve, v.tensor_tensor(at("ST", 12, 16), vec("sink", 4 * g, 4 * g + 4), at("ST", 0, 4),
                                          ALU.subtract), "swa_max")

            def swa_probs(u):
                width = P * (u % 2 + 1)
                dve.wait_ge(sem("exps"), u + 1)
                link(v.tensor_tensor(at("ST", 8, 12), at("ST", 8, 12), at("ST", 12, 16), ALU.add))
                link(v.reciprocal(at("ST", 8, 12), at("ST", 8, 12)))
                p = SM.rearrange("p (k w) -> p k w", w=256)[:, :, 0:width]
                done(dve, v.tensor_tensor(p, p, over(at("ST", 8, 12), width), ALU.mult), "probs")

            def swa_turned(u):
                if u:
                    wait_filled(dve, ("o", u - 1))
                for back in range(u % 2 + 1):
                    b = wait_filled(dve, ("pt", u, back))
                    drains(v.tensor_copy(PTs[:, 512 * back:512 * (back + 1)], b[:, :]), ("pt", u, back))

            def mem_max(h):
                b = wait_filled(dve, ("ms", h))
                link(v.tensor_reduce(at("ST", 18, 20), b[:, :].rearrange("p (q m) -> p q m", q=2), AX.X, ALU.max))
                done(dve, v.tensor_scalar(at("ST", 20, 22), at("ST", 18, 20), -(MEM_D ** -0.5), None, ALU.mult),
                     "mem_max")
                dve.wait_ge(sem("exps"), 8 + h + 1)
                drains(v.reciprocal(at("ST", 24, 26), at("ST", 24, 26)), ("ms", h))
                wait_drained(dve, ("ms", h))
                p = SM[:, 0:2 * MEM].rearrange("p (q m) -> p q m", q=2)
                done(dve, v.tensor_tensor(p, p, over(at("ST", 24, 26), MEM), ALU.mult), "probs")

            def mem_turned(h):
                wait_filled(dve, ("mo", h - 1) if h else ("o", 7))
                b = wait_filled(dve, ("mpt", h))
                drains(v.tensor_copy(PTs[:, 0:512], b[:, :]), ("mpt", h))

            def sample(b_, piece):
                H = HS[b_ % 2]
                if piece == 0:
                    dve.wait_ge(sem(f"state_in{b_ % 2}"), 16 * (b_ // 2 + 1))
                    link(v.tensor_tensor(H, H, over(EX[:, 1, :, b_], STATE), ALU.mult))
                elif piece == 1:
                    if b_ == 0:
                        dve.wait_ge(sem("p_ssm_out"), 16)
                    wait_drained(dve, ("bb", b_, 0))
                    t2 = T2.rearrange("p (g j n) -> p g j n", g=4, n=STATE)
                    bcast = BB[:, 0:512].rearrange("p (g n) -> p g n", g=4).unsqueeze(2).to_broadcast([P, 4, 4, STATE])
                    xdt = XS[:, :, b_].rearrange("p (g j) -> p g j", g=4).unsqueeze(3).to_broadcast([P, 4, 4, STATE])
                    link(v.tensor_tensor(t2, bcast, xdt, ALU.mult))
                    h2 = H.rearrange("p j n -> p (j n)")
                    done(dve, v.tensor_tensor(h2, h2, T2, ALU.add), "state_new")
                else:
                    wait_drained(dve, ("bb", b_, 1))
                    t2 = T2.rearrange("p (g j n) -> p g j n", g=4, n=STATE)
                    bcast = BB[:, 512:1024].rearrange("p (g n) -> p g n", g=4).unsqueeze(2).to_broadcast(
                        [P, 4, 4, STATE])
                    h4 = H.rearrange("p (g j) n -> p g j n", g=4)
                    link(v.tensor_tensor(t2, h4, bcast, ALU.mult))
                    done(dve, v.tensor_reduce(EX[:, 0, :, b_], T2.rearrange("p (j n) -> p j n", n=STATE), AX.X,
                                              ALU.add), "sample_y")

            for i in range(40):
                if 1 <= i < 9:
                    decays(i - 1)
                if i < 8:
                    segments(i)
                if 1 <= i < 9:
                    y_add(i - 1)
                if i < 12:
                    rotate(i)
                if i == 9:
                    dve.wait_ge(sem("end_decay"), 1)
                    x3 = at("XD").rearrange("p (h d) -> p h d", d=HEADDIM)
                    done(dve, v.tensor_tensor(x3, x3, over(at("WE"), HEADDIM), ALU.mult), "xd_weighed")
                if i in (12, 13):
                    for h in (2 * i - 24, 2 * i - 23):
                        dve.wait_ge(sem("rstd"), 19 + h)
                        for dt in range(2):
                            t = MQ[:, 2 * h + dt, :]
                            last = v.scalar_tensor_tensor(t, t, vec("gmq", dt, dt + 1), RS, ALU.mult, ALU.mult)
                        done(dve, last, "mq_scaled")
                    if i == 13:
                        done(dve, v.tensor_scalar(at("ST", 61, 62), RS[:, 0:1], 0.0, None, ALU.mult), "mq_ready")
                        wait_filled(dve, ("state", 3))
                if 15 <= i < 23:
                    swa_probs(i - 15)
                    swa_turned(i - 15)
                if 24 <= i < 28:
                    mem_turned(i - 24)
                if 14 <= i < 22:
                    swa_max(i - 14)
                if 23 <= i < 27:
                    mem_max(i - 23)
                if 14 <= i < 38:
                    sample((i - 14) // 3, (i - 14) % 3)
                if i in (31, 32):
                    part = i - 31
                    dve.wait_ge(sem(f"ring_in{part}"), 16 * 5)
                    kc = RING[part].rearrange("p (g b m) -> p g b m", b=4, m=P)
                    done(dve, v.tensor_copy(kc[:, :, :, 0], KD[:, :, SEQ + 4 * part:SEQ + 4 * (part + 1)]), "new_key")
                if i == 36:
                    b = wait_filled(dve, "sct")
                    link(v.tensor_reduce(at("ST", 32, 33, 32), b[0:32, 0:MEM], AX.X, ALU.max))
                    link(v.tensor_scalar(at("ST", 32, 33, 32), at("ST", 32, 33, 32), -(MEM_D ** -0.5), None, ALU.mult))
                    link(v.tensor_reduce(at("ST", 33, 34), b[:, 256:384], AX.X, ALU.max))
                    link(v.tensor_scalar(at("ST", 33, 34), at("ST", 33, 34), HD ** -0.5, vec("sink_col"),
                                         ALU.mult, ALU.max))
                    link(v.tensor_tensor(at("ST", 36, 37), vec("sink_col"), at("ST", 33, 34), ALU.subtract))
                    done(dve, v.tensor_scalar(at("ST", 33, 34), at("ST", 33, 34), -1.0, None, ALU.mult), "sample_max")
                    dve.wait_ge(sem("sample_exps"), 1)
                    drains(v.tensor_tensor(at("ST", 35, 36), at("ST", 35, 36), at("ST", 36, 37), ALU.add), "sct")
                    wait_drained(dve, "sct")
                    link(v.reciprocal(at("ST", 34, 35, 32), at("ST", 34, 35, 32)))
                    link(v.reciprocal(at("ST", 35, 36), at("ST", 35, 36)))
                    done(dve, v.tensor_scalar(SM[0:32, 0:MEM], SM[0:32, 0:MEM], at("ST", 34, 35, 32), None, ALU.mult),
                         "sample_probs")
                    done(dve, v.tensor_scalar(SM[:, 256:384], SM[:, 256:384], at("ST", 35, 36), None, ALU.mult),
                         "sample_probs")
                if i == 37:
                    wait_filled(dve, ("mo", 3))
                    b = wait_filled(dve, "spt")
                    drains(v.tensor_copy(PTs[:, 0:192], b[:, 0:192]), "spt")
            ys = C[:, 0:XS_T, SEQ:T]
            link(v.tensor_tensor(ys, ys, over(vec("ssm_d"), BATCH_S), ALU.mult))
            done(dve, v.tensor_tensor(ys, ys, EX[:, 0, :, :], ALU.add), "samples_done")
            dve.wait_ge(sem("z_active"), 1)
            y_all = C[:, 0:XS_T, :]
            done(dve, v.tensor_tensor(y_all, y_all, Z, ALU.mult), "y_gated")
            dve.wait_ge(sem("y_squared"), 1)
            done(dve, v.tensor_tensor(y_all, y_all, over(vec("ssm_g"), T), ALU.mult), "y_ready")
            dve.wait_ge(sem("gates_active"), 1)
            dve.wait_ge(sem("p_mem_out"), 32)
            wait_filled(dve, ("mo", 3))
            for i in range(4):
                for c in range(2):
                    m = 2 * i + c
                    b = wait_filled(dve, ("swa", m))
                    drains(v.tensor_tensor(MERGED[:, m, :], b[:, 0:T], G[:, 8 + m, :], ALU.mult), ("swa", m))
                for c in range(2):
                    m = 2 * i + c
                    b = wait_filled(dve, ("memb", m))
                    drains(v.tensor_tensor(TQ, b[:, 0:T], G[:, 16 + m, :], ALU.mult), ("memb", m))
                    wait_drained(dve, ("memb", m))
                    link(v.tensor_tensor(MERGED[:, m, :], MERGED[:, m, :], TQ, ALU.add))
            dve.wait_ge(sem("rstd"), 23)
            for m in range(8):
                b = wait_filled(dve, ("ssm", m))
                drains(v.tensor_tensor(TQ, b[:, 0:T], RS, ALU.mult), ("ssm", m))
                wait_drained(dve, ("ssm", m))
                link(v.tensor_tensor(TQ, TQ, G[:, m, :], ALU.mult))
                done(dve, v.tensor_tensor(MERGED[:, m, :], MERGED[:, m, :], TQ, ALU.add), "merged")
            dve.wait_ge(sem("x_again"), 16)
            for m in range(8):
                b = wait_filled(dve, ("out", m))
                drains(v.tensor_tensor(X1[:, m, :], X1[:, m, :], b[:, 0:T], ALU.add), ("out", m))
                wait_drained(dve, ("out", m))
            done(dve, v.tensor_scalar(at("ST", 62, 63), vec("gq"), 0.0, None, ALU.mult), "x1_made")
            dve.wait_ge(sem("rstd"), 24)
            link(v.tensor_tensor(HT, X1, each(RS, KT), ALU.mult))
            done(dve, v.tensor_tensor(HT, HT, over(vec("g2"), T), ALU.mult), "h_ready")

            def r(a_, n, w=None):
                ap = at("S", 1100 + a_, 1100 + a_ + n)
                return ap if w is None else ap.rearrange("p (t e) -> p t e", e=w)

            D4, M2, D8, O8, OG, SEL, LG = (r(0, 12, 4), r(12, 3), r(16, 24, 8), r(40, 24, 8), r(64, 12, 4),
                                           r(80, 96), r(176, 108, ROUTES))
            T12, T24, MX, OH2, ZS = r(300, 12, 4), r(320, 24, 8), r(344, 3), r(350, 24, 8), r(380, 24, 8)
            W1, W2 = r(404, 3), r(407, 3)
            dve.wait_ge(sem("router_in"), 16)
            link(v.memset(r(176, 108), 0.0))
            b = wait_filled(dve, "route")
            for t, rows in enumerate((P, P, BATCH_S)):
                last = v.tensor_tensor(LG[0:rows, t, :], b[0:rows, 64 * t:64 * t + ROUTES],
                                       vec("route_b", rows=rows), ALU.add)
            drains(last, "route")
            wait_drained(dve, "route")

            def first_best(src, width, order, mx, eq, out):
                link(v.tensor_reduce(mx, src, AX.X, ALU.max))
                link(v.tensor_tensor(eq, src, over(mx, width), ALU.is_equal))
                link(v.tensor_tensor(eq, eq, each(tab(order), 3), ALU.mult))
                link(v.tensor_reduce(MX2, eq, AX.X, ALU.max))
                link(v.tensor_tensor(out, eq, over(MX2, width), ALU.is_equal))

            MX2 = r(347, 3)
            first_best(LG[:, :, 0:GROUPS], GROUPS, "first_g", MX, T12, OG)
            link(v.tensor_tensor(D4, LG[:, :, 0:GROUPS], over(MX, GROUPS), ALU.subtract))
            for t in range(3):
                last = v.tensor_tensor(SEL[:, 32 * t:32 * (t + 1)].rearrange("p (g e) -> p g e", g=GROUPS),
                                       LG[:, t, GROUPS:ROUTES].rearrange("p (g e) -> p g e", g=GROUPS),
                                       over(OG[:, t, :], PER_GROUP), ALU.mult)
            link(last)
            link(v.tensor_reduce(ZS, SEL.rearrange("p (t g e) -> p t e g", t=3, g=GROUPS), AX.X, ALU.add))
            first_best(ZS, PER_GROUP, "first_e", MX, T24, O8)
            link(v.tensor_tensor(D8, ZS, over(MX, PER_GROUP), ALU.subtract))
            link(v.scalar_tensor_tensor(D8, O8, -1e30, D8, ALU.mult, ALU.add))
            first_best(D8, PER_GROUP, "first_e", M2, T24, OH2)
            done(dve, v.tensor_scalar(r(410, 3), M2, 1.0, None, ALU.mult), "route_args")
            dve.wait_ge(sem("route_exp"), 2)
            link(v.tensor_reduce(W1, D4, AX.X, ALU.add))
            link(v.reciprocal(W1, W1))
            link(v.tensor_scalar(W2, M2, 1.0, None, ALU.add))
            link(v.reciprocal(W2, W2))
            link(v.tensor_tensor(W1, W1, W2, ALU.mult))
            link(v.tensor_tensor(W2, W1, M2, ALU.mult))
            link(v.tensor_tensor(O8, O8, over(W1, PER_GROUP), ALU.mult))
            link(v.tensor_tensor(OH2, OH2, over(W2, PER_GROUP), ALU.mult))
            link(v.tensor_tensor(O8, O8, OH2, ALU.add))
            for t in range(3):
                last = v.tensor_tensor(COMB[:, t, :].rearrange("p (g e) -> p g e", g=GROUPS),
                                       over(OG[:, t, :], PER_GROUP), each(O8[:, t, :], GROUPS), ALU.mult)
            done(dve, last, "comb")
            b = wait_filled(dve, "combT")
            drains(v.tensor_copy(COMBT, b[0:32, 0:T]), "combT")
            for e in range(0, EXPERTS, 2):
                b = wait_filled(dve, ("comb", e))
                drains(v.tensor_copy(COMBB[:, T * e:T * (e + 1)], b[:, 0:T]), ("comb", e))
            for e in range(EXPERTS - 4, EXPERTS):
                wait_drained(dve, ("comb", e))

            for free in (*half_free, *act_ready, *down_read):
                dve.sem_inc(free, 1)
            with dve.Fori(0, EXPERTS) as e:
                for f in range(FF_T):
                    dve.wait_ge(sem(f"silu{f}"), e + 1)
                    dve.wait_ge(sem(f"expert_up{f}"), e + 1)
                    dve.wait_ge(down_filled[3], e * 2 + 1)
                    v.tensor_tensor(ACTT[f], psum[2 * f + 1][:, 0:T], SG[f], ALU.mult).then_inc(half_free[f], 1)
                    dve.wait_ge(half_free[f], e + 2)
                    v.tensor_tensor(ACTT[f], ACTT[f], COMBB[:, bass.ds(e * T, T)], ALU.mult
                                    ).then_inc(act_ready[f], 1)
                for half in range(2):
                    for q in range(4):
                        dve.wait_ge(down_filled[q], e * 2 + (half + 1 + (q == 3)))
                        dve.wait_ge(down_read[q], e * 2 + (half + 1))
                        v.tensor_tensor(X1[:, 4 * half + q, :], X1[:, 4 * half + q, :], psum[4 + q][:, 0:T], ALU.add
                                        ).then_inc(down_read[q], 1)


def _tables():
    t = np.zeros((P, TAB_W), np.float32)

    def put(name, a):
        o, n = TAB[name]
        t[:, o:o + n] = a

    s, u = np.arange(P)[:, None], np.arange(P)[None, :]
    causal = (s <= u).astype(np.float32)
    put("ident", np.eye(P, dtype=np.float32))
    put("causal", np.concatenate([causal, np.ones((P, P), np.float32), causal], 1))
    rot = np.zeros((P, P), np.float32)
    for m in range(P):
        if m % 64 < 32:
            rot[m + 32, m] = -1.0
        else:
            rot[m - 32, m] = 1.0
    put("rot", rot)
    put("half_ones", (s // 64 == u // 64).astype(np.float32))
    put("ones", np.ones((P, P), np.float32))
    put("window", np.concatenate([np.where(u <= s, 0, -1e30), np.where(u > s, 0, -1e30)], 1))
    inv = np.float32(10000.0) ** (-np.arange(32, dtype=np.float32) / np.float32(32))
    pos = np.concatenate([np.arange(SEQ), np.full(BATCH_S, PAST_LEN)]).astype(np.float32)
    ang = (pos[None, :] * inv[:, None]).astype(np.float32)
    put("cos", np.tile(np.cos(ang), (4, 1)))
    put("sin", np.tile(np.sin(ang), (4, 1)))
    put("first_g", np.arange(GROUPS, 0, -1)[None, :])
    put("first_e", np.arange(PER_GROUP, 0, -1)[None, :])
    return t


def _layout(inp):
    c = np.ascontiguousarray

    def feat(a):
        return a.reshape(-1, P).T

    def rows(a):
        return np.broadcast_to(a.reshape(1, -1), (P, a.size))

    i = {k: np.asarray(a) for k, a in inp.items()}
    xt = np.concatenate([i["x_prompt"][0], i["x_sample"][:, 0]], 0)
    sink = i["att_sink"][0]
    sink_col = np.tile(sink.reshape(KV, 2, 2).transpose(0, 2, 1).reshape(-1), BATCH_S)[:, None]
    parts = {
        "g1": feat(i["norm1_g"][0]), "gmem": feat(i["mem_norm_g"][0]),
        "conv_w": np.concatenate([feat(i["ssm_conv_w"][0, k]) for k in range(CONV_TAPS)], 1),
        "conv_b": feat(i["ssm_conv_b"][0]), "ssm_g": feat(i["ssm_norm_g"][0]),
        "ssm_d": feat(np.repeat(i["ssm_d"][0], HEADDIM)),
        "gq": np.tile(i["att_q_norm_g"][0], 2)[:, None], "gk": np.tile(i["att_k_norm_g"][0], 2)[:, None],
        "gmq": feat(i["mem_q_norm_g"][0]), "gmk": feat(i["mem_k_norm_g"][0]), "g2": feat(i["norm2_g"][0]),
        "sink_col": sink_col, "dt_bias": rows(i["ssm_dt_bias"][0]), "a_log": rows(i["ssm_a_log"][0]),
        "route_b": rows(np.concatenate([i["b_router_group"][0], i["b_router_expert"][0]])), "sink": rows(sink),
    }

    def tiled(a):
        return c(a.T.reshape(-1, P, a.shape[0]).transpose(1, 0, 2))

    kt = i["cache_swa_k"][0].transpose(3, 2, 0, 1).reshape(HD, KV, 2, 4, P)
    kt = np.concatenate([kt, kt], 0).transpose(2, 0, 1, 3, 4)
    return {
        "tables": _tables(),
        "vectors": c(np.concatenate([parts[n] for n in VEC], 1)),
        "xT": tiled(xt),
        "memT": tiled(i["mem_prompt"][0]),
        "histT": c(i["state_conv"][0].transpose(2, 0, 1).reshape(CONV_T, P, BATCH_S, 3).transpose(1, 0, 2, 3)),
        "w_in": i["w_in"][0], "w_mem_kv": i["w_mem_kv"][0], "w_br_ssm": i["w_br_ssm"][0],
        "w_br_swa": i["w_br_swa"][0], "w_br_mem": i["w_br_mem"][0], "w_out": i["w_out"][0],
        "w_router": c(np.concatenate([i["w_router_group"][0], i["w_router_expert"][0]], 1)),
        "w_exp_gate": i["w_exp_gate"][0], "w_exp_up": i["w_exp_up"][0], "w_exp_down": i["w_exp_down"][0],
        "state_ssm": i["state_ssm"][0].reshape(BATCH_S, D_INNER, STATE),
        "mem_kT": c(i["cache_mem_k"][0].reshape(BATCH_S, MEM, MEM_H, 2, P).transpose(0, 4, 2, 3, 1)
                    .reshape(BATCH_S, P, 2048)),
        "mem_v": c(i["cache_mem_v"][0].reshape(BATCH_S, 2, P, D_MODEL).transpose(0, 2, 1, 3).reshape(BATCH_S, P, 2048)),
        "swa_kT": c(kt.reshape(2, P, 2048)),
        "swa_v": c(i["cache_swa_v"][0].reshape(BATCH_S, P, KV * HD).transpose(1, 0, 2).reshape(P, 2048)),
    }


_OUTS = {
    "yT": (P, KT, T), "p_mem_kT": (P, 8, MEM), "p_mem_v": (P, 2, D_MODEL), "p_swa_v": (P, KV * HD),
    "newconvT": (P, CONV_T, 27), "p_swa_kT": (64, KV, P), "p_ssm": (D_INNER, STATE),
    "s_ssm": (BATCH_S, D_INNER, STATE), "s_swa_kT": (2, 64, 2048), "s_swa_v": (P, 2048),
}


def _results(o):
    c = np.ascontiguousarray
    y = o["yT"].transpose(1, 0, 2).reshape(D_MODEL, T).T
    conv = o["newconvT"].transpose(1, 0, 2).reshape(CONV_CH, 27)
    roll = list(range(1, P)) + [0]
    sk = o["s_swa_kT"].reshape(2, HD, KV, 4, P).transpose(0, 3, 4, 2, 1).reshape(BATCH_S, P, KV, HD)[:, roll]
    sv = o["s_swa_v"].reshape(P, BATCH_S, KV, HD).transpose(1, 0, 2, 3)[:, roll]
    return (
        c(y[:SEQ])[None], c(y[SEQ:])[:, None],
        c(conv[:, 24:27].T)[None, None],
        o["p_ssm"].reshape(1, 1, SSM_HEADS, HEADDIM, STATE),
        c(o["p_swa_kT"].transpose(2, 1, 0))[None, None],
        o["p_swa_v"].reshape(1, 1, P, KV, HD),
        c(o["p_mem_kT"].transpose(2, 1, 0).reshape(MEM, MEM_H, MEM_D))[None, None],
        c(o["p_mem_v"].transpose(1, 0, 2).reshape(MEM, MEM_H, MEM_D))[None, None],
        c(conv[:, 0:24].reshape(CONV_CH, BATCH_S, 3).transpose(1, 2, 0))[None],
        o["s_ssm"].reshape(1, BATCH_S, SSM_HEADS, HEADDIM, STATE),
        c(sk)[None], c(sv)[None],
    )


def kernel(**inputs):
    import concourse.bacc as bacc
    from concourse.bass_utils import run_bass_kernel_spmd

    nc = bacc.Bacc("TRN2", target_bir_lowering=False, num_devices=1)
    arrays = _layout(inputs)
    ins = {n: nc.dram_tensor(f"in_{n}", a.shape, mybir.dt.from_np(a.dtype), kind="ExternalInput").ap()
           for n, a in arrays.items()}
    outs = {n: nc.dram_tensor(f"out_{n}", s, F32, kind="ExternalOutput").ap() for n, s in _OUTS.items()}
    build_program(nc, ins, outs)
    got = run_bass_kernel_spmd(nc, [{f"in_{n}": a for n, a in arrays.items()}], core_ids=[0])
    return _results({n: got.results[0][f"out_{n}"] for n in _OUTS})
```

```python
from contextlib import ExitStack

import numpy as np

import concourse.bass as bass
from concourse import mybir

P = 128
D_MODEL = 1024
SEQ = 256
BATCH_S = 8
PAST_LEN = 2048
T = SEQ + BATCH_S
KT = D_MODEL // P
D_INNER = 2048
HEADDIM = 64
SSM_HEADS = 32
SSM_GROUPS = 4
STATE = 128
CONV_TAPS = 4
CONV_CH = D_INNER + 2 * SSM_GROUPS * STATE
CONV_T = CONV_CH // P
XS_T = D_INNER // P
KV = 4
HD = 64
WINDOW = 128
MEM = 256
MEM_H = 4
MEM_D = 256
GROUPS = 4
PER_GROUP = 8
EXPERTS = GROUPS * PER_GROUP
D_FF = 256
FF_T = D_FF // P
EPS = 1e-6
OFF_GATE, OFF_Z = 0, 3 * D_MODEL
OFF_XBC = OFF_Z + D_INNER
OFF_DT = OFF_XBC + CONV_CH
OFF_Q = OFF_DT + SSM_HEADS
OFF_K = OFF_Q + 1024
OFF_V = OFF_K + KV * HD
OFF_MQ = OFF_V + KV * HD
ROUTES = GROUPS + EXPERTS

CW = 256
CHUNK = KT * CW
WBUFS = 3
SLOTS = 32
QUAD = P // SLOTS
QUADS = EXPERTS // QUAD
ALL_ROUNDS = -(-T // SLOTS)
PIECE = KT * D_FF

ALU = mybir.AluOpType
ACT = mybir.ActivationFunctionType
AX = mybir.AxisListType
F32 = mybir.dt.float32

VEC = {}
_at = 0
for _name, _n in (("g1", KT), ("gmem", KT), ("conv_w", CONV_TAPS * CONV_T), ("conv_b", CONV_T), ("ssm_g", XS_T),
                  ("ssm_d", XS_T), ("gq", 1), ("gk", 1), ("gmq", 2), ("gmk", 2), ("g2", KT), ("sink_col", 1),
                  ("dt_bias", SSM_HEADS), ("a_log", SSM_HEADS), ("route_b", ROUTES), ("sink", 16)):
    VEC[_name] = (_at, _n)
    _at += _n
VEC_W = _at
TAB = {}
_at = 0
for _name, _n in (("ident", P), ("causal", 3 * P), ("rot", P), ("half_ones", P), ("ones", P), ("window", 2 * P),
                  ("cos", T), ("sin", T), ("first_g", GROUPS), ("first_e", PER_GROUP), ("slots", SLOTS)):
    TAB[_name] = (_at, _n)
    _at += _n
TAB_W = _at

MAP = {}


def _place(*names):
    at = 0
    for name, words in names:
        MAP[name] = (at, words)
        at += words
    assert at <= 53200, at


_place(
    ("HN", KT * T),
    ("W", WBUFS * CHUNK),
    ("X", CONV_T * T),
    ("C", CONV_T * T),
    ("Q", 8 * T),
    ("KD", KV * T),
    ("MQ", 8 * T),
    ("VT", 3 * KV * HD),
    ("XD", 2 * D_INNER),
    ("pad", 32),
    ("Z", XS_T * T),
    ("G", 24 * T),
    ("MK", 8 * MEM),
    ("MV", 2 * D_MODEL),
    ("S", 3072),
    ("tab", TAB_W), ("vec", VEC_W),
    ("DT", 3 * SSM_HEADS), ("DTA", 3 * SSM_HEADS), ("AC", 2 * SSM_HEADS), ("WE", 2 * SSM_HEADS),
    ("BT", 2 * 4 * STATE), ("RS", T), ("TQ", T), ("EX", 2 * XS_T * BATCH_S), ("XS", XS_T * BATCH_S),
    ("ST", 64),
)


def build_program(nc, ins, outs):
    ctx = ExitStack()
    with ctx:
        top = max(a + n for a, n in MAP.values())
        M = ctx.enter_context(nc.sbuf_tensor("M", [P, top], F32))
        psum = [ctx.enter_context(nc.psum_tensor(f"bank{i}", [P, 512], F32)) for i in range(8)]
        filled = [ctx.enter_context(nc.semaphore(f"filled{i}")) for i in range(8)]
        drained = [ctx.enter_context(nc.semaphore(f"drained{i}")) for i in range(8)]
        sems, counts = {}, {}

        def sem(name):
            if name not in sems:
                sems[name] = ctx.enter_context(nc.semaphore(name))
                counts[name] = 0
            return sems[name]

        def at(name, a=0, b=None, rows=P):
            off, n = MAP[name]
            b = n if b is None else b
            return M[0:rows, off + a:off + b]

        def tiles(name, w, a=0, b=None, rows=P):
            return at(name, a, b, rows).rearrange("p (j w) -> p j w", w=w)

        def tab(name, rows=P):
            a, n = TAB[name]
            return at("tab", a, a + n, rows)

        def vec(name, a=0, b=None, rows=P):
            off, n = VEC[name]
            b = n if b is None else b
            return at("vec", off + a, off + b, rows)

        def over(ap, n):
            return ap.unsqueeze(2).to_broadcast([ap.shape[0], ap.shape[1], n])

        def each(ap, n):
            return ap.unsqueeze(1).to_broadcast([ap.shape[0], n, ap.shape[1]])

        def done(eng, instruction, name):
            s = sem(name)
            counts[name] += 1
            instruction.then_inc(s, 1)
            eng.wait_ge(s, counts[name])

        HN, X, C, Z = tiles("HN", T), tiles("X", T), tiles("C", T), tiles("Z", T)
        Q, KD, MQ, G = tiles("Q", T), tiles("KD", T), tiles("MQ", T), tiles("G", T)
        MK, MV, VT = tiles("MK", MEM), tiles("MV", D_MODEL), tiles("VT", KV * HD)
        XD = tiles("XD", D_INNER)
        DT, DTA, AC, WE = (tiles(n, SSM_HEADS) for n in ("DT", "DTA", "AC", "WE"))
        BT = tiles("BT", 4 * STATE)
        RS, TQ = at("RS"), at("TQ")
        EX = at("EX").rearrange("p (a j b) -> p a j b", a=2, b=BATCH_S)
        XS = tiles("XS", BATCH_S)
        ident = tab("ident")
        ones = tab("ones")
        XT, XSQ = tiles("Z", T, 0, 8 * T), tiles("Z", T, 8 * T, 16 * T)
        MT, MSQ = tiles("G", MEM, 0, 2048), tiles("G", MEM, 2048, 4096)
        MN = tiles("XD", MEM, 0, 2048)
        RSM = tiles("G", MEM, 4096, 5120)
        NEWC = at("G", 0, 27 * CONV_T).rearrange("p (j k) -> p j k", k=27)
        HIST = at("G", 648, 648 + 24 * CONV_T).rearrange("p (j b k) -> p j b k", b=BATCH_S, k=3)
        CB = tiles("G", 3 * P, 1224, 2760)
        KSQ, QSQ = tiles("G", T, 2760, 3816), tiles("G", T, 3816, 5928)
        DTX, DAX = at("Z", 0, 2048, 8), at("Z", 2048, 4096, 8)
        SBC = at("X", 4096, 5120, 8)
        HS = [at("X", 2048 * i, 2048 * (i + 1)).rearrange("p (j n) -> p j n", n=STATE) for i in range(2)]
        T2 = at("S", 0, 2048)
        BB = at("S", 2048, 3072)
        SM, PTs = at("XD", 0, 1024), at("XD", 1024, 2048)
        RING = [at("C", 4224, 6272), at("XD", 2048, 4096)]
        SC, SC2 = at("G", 6336 - 64, 6336), at("G", 6336 - 192, 6336 - 64)

        X1 = HN
        mk_at = MAP["MK"][0]
        MERGED = M[:, mk_at:mk_at + 8 * T].rearrange("p (j w) -> p j w", w=T)
        HT = MERGED
        X1SQ = M[:, mk_at + 8 * T:mk_at + 16 * T].rearrange("p (j w) -> p j w", w=T)
        WR = at("S", 256, 256 + KT * ROUTES).rearrange("p (k n) -> p k n", n=ROUTES)
        COMB = at("S", 600, 600 + 96).rearrange("p (t e) -> p t e", e=EXPERTS)
        MASK, PLACE = (at("S", a, a + 96).rearrange("p (t e) -> p t e", e=EXPERTS) for a in (700, 800))
        ONE, ONEW = (at("S", a, a + 3 * P).rearrange("p (t j s) -> p t j s", t=3, s=SLOTS) for a in (1600, 2000))
        BACK = at("S", 2400, 2400 + T)
        HTOK = tiles("W", D_MODEL, 0, 3 * D_MODEL)
        HG = tiles("W", P, 3072, 4096)
        DOWNED = at("W", 4096, 5120)
        SG, ACTV = at("W", 5120, 5376), at("W", 5376, 5632)
        ACTT = tiles("W", P, 5632, 5888)
        worst = ctx.enter_context(nc.sbuf_tensor("worst", [P, 1], mybir.dt.int32))
        assert mk_at + 16 * T <= MAP["S"][0] + 256

        y_end = MAP["C"][0] + XS_T * T
        free1 = [y_end, y_end + 4 * PIECE, y_end + 5 * PIECE, MAP["X"][0] + XS_T * T]
        free2 = [MAP["Z"][0], MAP["Z"][0] + PIECE, y_end + PIECE, y_end + 2 * PIECE]
        free3 = [y_end + 3 * PIECE, MAP["X"][0], MAP["X"][0] + PIECE, MAP["C"][0]]
        free4 = [MAP["C"][0] + PIECE, MAP["G"][0], MAP["G"][0] + PIECE, MAP["G"][0] + 2 * PIECE]
        assert y_end + 6 * PIECE <= MAP["Z"][0] and MAP["X"][0] + XS_T * T + PIECE <= MAP["C"][0]

        def piece(kind, q, j):
            o = {"gate": (free1, free4)[q % 2], "up": free2, "down": free3}[kind][j]
            return M[:, o:o + PIECE].rearrange("p (k n) -> p k n", n=D_MODEL if kind == "down" else D_FF)

        w_in, w_mem = ins["w_in"], ins["w_mem_kv"]
        chunks = []

        def cols(w, c0, n=CW, k0=0):
            return w[k0:k0 + D_MODEL, c0:c0 + n].rearrange("(k p) n -> p k n", p=P)

        for i in range(8):
            chunks.append((("mem", i), [(cols(w_mem, CW * i), 0, CW)]))
        for i in range(12):
            chunks.append((("xbc", i), [(cols(w_in, OFF_XBC + CW * i), 0, CW)]))
        chunks.append((("dt", 0), [(cols(w_in, OFF_DT, SSM_HEADS), 0, SSM_HEADS)]))
        for i in range(2):
            chunks.append((("kd", i), [(cols(w_in, OFF_K + HD * (2 * i + g), HD), P * g + HD * twice, HD)
                                       for g in range(2) for twice in range(2)]))
        chunks.append((("v", 0), [(cols(w_in, OFF_V), 0, CW)]))
        for i in range(4):
            chunks.append((("q", i), [(cols(w_in, OFF_Q + CW * i), 0, CW)]))
        for i in range(4):
            chunks.append((("mq", i), [(cols(w_in, OFF_MQ + CW * i), 0, CW)]))
        for i in range(8):
            chunks.append((("z", i), [(cols(w_in, OFF_Z + CW * i), 0, CW)]))
        for i in range(12):
            chunks.append((("gate", i), [(cols(w_in, OFF_GATE + CW * i), 0, CW)]))
        for i in range(4):
            chunks.append((("swa", i), [(cols(ins["w_br_swa"], CW * i), 0, CW)]))
            chunks.append((("memb", i), [(cols(ins["w_br_mem"], CW * i), 0, CW)]))
        for i in range(4):
            chunks.append((("ssma", i), [(cols(ins["w_br_ssm"], CW * i), 0, CW)]))
            chunks.append((("ssmb", i), [(cols(ins["w_br_ssm"], CW * i, CW, D_MODEL), 0, CW)]))
        for i in range(4):
            chunks.append((("out", i), [(cols(ins["w_out"], CW * i), 0, CW)]))
        number = {name: n for n, (name, _) in enumerate(chunks)}
        chunk_in = [sem(f"chunk_in{i}") for i in range(WBUFS)]

        def chunk(n):
            return tiles("W", CW, CHUNK * (n % WBUFS), CHUNK * (n % WBUFS + 1))

        place, uses, last_use = {}, [0] * 8, {}
        gate_in = [sem(f"gate_in{b}") for b in range(2)]
        up_in, down_in = sem("up_in"), sem("down_in")

        def by_rounds(eng, experts):
            eng.wait_ge(sem("worst_ready"), 1)
            fullest = eng.value_load(worst[0:1, 0:1])
            with eng.If(fullest <= SLOTS):
                experts(1)
            with eng.Else():
                experts(ALL_ROUNDS)

        def steps(eng, rounds, body):
            with eng.Fori(0, QUADS // 2) as it:
                for b in range(2):
                    q = it * 2 + b
                    if rounds == 1:
                        body(b, q, q)
                    else:
                        with eng.Fori(0, rounds) as r:
                            body(b, q, q * rounds + r)

        def wait_filled(eng, name):
            bank, n = place[name]
            eng.wait_ge(filled[bank], n + 1)
            return psum[bank]

        def wait_drained(eng, name):
            bank, n = place[name]
            eng.wait_ge(drained[bank], n + 1)

        def drains(instruction, name):
            instruction.then_inc(drained[place[name][0]], 1)

        block = ctx.enter_context(nc.Block())

        @block.tensor
        def _(pe):
            ring = [0]
            at_chunk = [0]
            chunk_arrivals = {}

            def opened(name, bank):
                n = uses[bank]
                uses[bank] += 1
                place[name] = (bank, n)
                if n:
                    pe.wait_ge(drained[bank], n)
                return psum[bank]

            def full(mm, name):
                mm.then_inc(filled[place[name][0]], 1)

            def next_proj(name):
                ring[0] += 1
                return opened(name, (ring[0] - 1) % 3)

            def arrive(name):
                n = number[name]
                pe.wait_ge(chunk_in[n % WBUFS], chunk_value[n])
                return chunk(n)

            def feature_tile(name, w, c, x, n, chunk_name):
                bank = next_proj(name)
                for k in range(KT):
                    mm = pe.matmul(bank[:, 0:n], w[:, k, P * c:P * (c + 1)], x[:, k, 0:n],
                                   start=(k == 0), stop=(k == KT - 1))
                full(mm, name)
                last_use[chunk_name] = name

            chunk_value, seen = {}, [0] * WBUFS
            for n, (_, parts) in enumerate(chunks):
                seen[n % WBUFS] += 16 * len(parts)
                chunk_value[n] = seen[n % WBUFS]

            def squares(name, bank, sq, first, n_tiles, n, weights=None):
                b = opened(name, bank)
                for k in range(n_tiles):
                    mm = pe.matmul(b[:, 0:n], ones if weights is None else weights, sq[:, first + k, 0:n],
                                   start=(k == 0), stop=(k == n_tiles - 1))
                full(mm, name)

            pe.wait_ge(sem("tables_in"), 32)
            pe.wait_ge(sem("x_squared"), 1)
            squares("ss_x", 3, XSQ, 0, KT, T)
            pe.wait_ge(sem("mem_squared"), 1)
            squares("ss_mem", 4, MSQ, 0, KT, MEM)

            pe.wait_ge(sem("mem_normed"), 1)
            for i in range(4):
                w = arrive(("mem", i))
                for c in range(2):
                    feature_tile(("mk", 2 * i + c), w, c, MN, MEM, ("mem", i))
            for i in range(4):
                w = arrive(("mem", 4 + i))
                for mt in range(2):
                    name = ("mv", i, mt)
                    b = next_proj(name)
                    for k in range(KT):
                        mm = pe.matmul(b[:, 0:CW], MN[:, k, P * mt:P * (mt + 1)], w[:, k, :],
                                       start=(k == 0), stop=(k == KT - 1))
                    full(mm, name)
                    last_use[("mem", 4 + i)] = name
            pe.wait_ge(sem("mk_squared"), 1)
            for h in range(MEM_H):
                squares(("ss_mk", h), 3 + h, MSQ, 2 * h, 2, MEM)

            pe.wait_ge(sem("x_normed"), 1)
            for i in range(12):
                w = arrive(("xbc", i))
                for c in range(2):
                    feature_tile(("xbc", 2 * i + c), w, c, HN, T, ("xbc", i))
            arrive(("dt", 0))
            off = MAP["W"][0] + CHUNK * (number[("dt", 0)] % WBUFS)
            w = M[:, off:off + KT * SSM_HEADS].rearrange("p (k n) -> p k n", n=SSM_HEADS)
            b = next_proj("dt")
            for t, rows in enumerate((P, P, BATCH_S)):
                for k in range(KT):
                    mm = pe.matmul(b[0:rows, 32 * t:32 * t + 32], HN[:, k, P * t:P * t + rows], w[:, k, :],
                                   start=(k == 0), stop=(k == KT - 1))
            full(mm, "dt")
            last_use[("dt", 0)] = "dt"
            for i in range(2):
                w = arrive(("kd", i))
                for c in range(2):
                    feature_tile(("kd", 2 * i + c), w, c, HN, T, ("kd", i))
            w = arrive(("v", 0))
            for t, rows in enumerate((P, P, BATCH_S)):
                b = next_proj(("v", t))
                for k in range(KT):
                    mm = pe.matmul(b[0:rows, 0:CW], HN[:, k, P * t:P * t + rows], w[:, k, :],
                                   start=(k == 0), stop=(k == KT - 1))
                full(mm, ("v", t))
                last_use[("v", 0)] = ("v", t)
            for i in range(4):
                w = arrive(("q", i))
                for c in range(2):
                    feature_tile(("q", 2 * i + c), w, c, HN, T, ("q", i))
                if i == 1:
                    pe.wait_ge(sem("dta"), 1)
                    b = opened("acum", 3)
                    pe.matmul(b[:, 0:32], tab("causal")[:, 0:P], DTA[:, 0, :], start=True, stop=True)
                    pe.matmul(b[:, 32:64], ones, DTA[:, 0, :], start=True, stop=False)
                    pe.matmul(b[:, 32:64], tab("causal")[:, 0:P], DTA[:, 1, :], start=False, stop=True)
                    pe.matmul(b[:, 64:96], ones, DTA[:, 0, :], start=True, stop=False)
                    full(pe.matmul(b[:, 64:96], ones, DTA[:, 1, :], start=False, stop=True), "acum")
                    pe.wait_ge(sem("dt_expanded"), 1)
                    b = opened("ex", 4)
                    for a, src in enumerate((DTX, DAX)):
                        for j in range(XS_T):
                            c0 = (a * XS_T + j) * BATCH_S
                            mm = pe.matmul(b[:, c0:c0 + BATCH_S], src[:, P * j:P * (j + 1)], ident[0:8, 0:8],
                                           start=True, stop=True)
                    full(mm, "ex")

            for i in range(4):
                w = arrive(("mq", i))
                for c in range(2):
                    feature_tile(("mq", 2 * i + c), w, c, HN, T, ("mq", i))
                    j = 2 * i + c
                    if j == 0:
                        pe.wait_ge(sem("conv_active"), 3)
                    if j < 4:
                        for half in range(2):
                            b = opened(("xtok", half, j), 3 + half)
                            for q in range(4):
                                mm = pe.transpose(b[:, P * q:P * (q + 1)], C[:, 4 * j + q, P * half:P * (half + 1)],
                                                  ident)
                            full(mm, ("xtok", half, j))
                    if j == 4:
                        for half in range(2):
                            b = opened(("btok", half), 5 + half)
                            for q in range(4):
                                mm = pe.transpose(b[:, P * q:P * (q + 1)], C[:, XS_T + q, P * half:P * (half + 1)],
                                                  ident)
                            full(mm, ("btok", half))
                        for a in range(2):
                            b = opened(("sbc", a), 3 + a)
                            for q in range(4):
                                mm = pe.transpose(b[0:8, P * q:P * (q + 1)], C[:, XS_T + 4 * a + q, SEQ:T], ident)
                            full(mm, ("sbc", a))
                    if j == 5:
                        for g in range(4):
                            b = opened(("cb", g), 3 + g)
                            pe.matmul(b[:, 0:SEQ], C[:, XS_T + g, 0:P], C[:, XS_T + 4 + g, 0:SEQ],
                                      start=True, stop=True)
                            full(pe.matmul(b[:, SEQ:3 * P], C[:, XS_T + g, P:SEQ], C[:, XS_T + 4 + g, P:SEQ],
                                           start=True, stop=True), ("cb", g))

            def ssd_bcast(u):
                for a in range(2):
                    b = opened(("acb", u, a), 3 + a)
                    for q in range(2):
                        h = 4 * u + 2 * a + q
                        o = b[:, SEQ * q:SEQ * (q + 1)]
                        pe.matmul(o, DTA[:, 0, h:h + 1].to_broadcast([P, P]), tab("causal")[:, 0:SEQ],
                                  start=True, stop=False)
                        mm = pe.matmul(o[:, P:SEQ], DTA[:, 1, h:h + 1].to_broadcast([P, P]),
                                       tab("causal")[:, 0:P], start=False, stop=True)
                    full(mm, ("acb", u, a))

            def ssd_y(u):
                pe.wait_ge(sem("decay_ready"), u + 1)
                D = tiles("S", 3 * P, 1536 * (u % 2), 1536 * (u % 2 + 1))
                b = opened(("y", u), 5)
                for q in range(4):
                    h = 4 * u + q
                    o = b[64 * (q % 2):64 * (q % 2) + 64, SEQ * (q // 2):SEQ * (q // 2 + 1)]
                    pe.matmul(o, XD[:, 0, HEADDIM * h:HEADDIM * (h + 1)], D[:, q, 0:SEQ], start=True, stop=False)
                    mm = pe.matmul(o[:, P:SEQ], XD[:, 1, HEADDIM * h:HEADDIM * (h + 1)], D[:, q, SEQ:3 * P],
                                   start=False, stop=True)
                full(mm, ("y", u))

            def qk(j):
                src, sq = (Q[:, j, :], QSQ[:, j, :]) if j < 8 else (KD[:, j - 8, :], KSQ[:, j - 8, :])
                if j == 0:
                    pe.wait_ge(sem("qk_squared"), 2)
                    pe.wait_ge(sem("qk_scaled"), 2)
                b = opened(("qk_ss", j), 6)
                full(pe.matmul(b[:, 0:T], tab("half_ones"), sq, start=True, stop=True), ("qk_ss", j))
                b = opened(("qk_rot", j), 7)
                full(pe.matmul(b[:, 0:T], tab("rot"), src, start=True, stop=True), ("qk_rot", j))

            def state(g):
                if g == 0:
                    pe.wait_ge(sem("xd_weighed"), 1)
                b = opened(("state", g), 3 + g % 2)
                for q in range(4):
                    j = 4 * g + q
                    for half in range(2):
                        mm = pe.matmul(b[:, P * q:P * (q + 1)], XD[:, half, P * j:P * (j + 1)],
                                       BT[:, half, P * g:P * (g + 1)], start=(half == 0), stop=(half == 1))
                full(mm, ("state", g))

            def swa_scores(u):
                g, blk = u // 2, u % 2
                for hh in range(2):
                    b = opened(("s", u, hh), 3 + hh)
                    rows = slice(64 * hh, 64 * hh + 64)
                    for jj in range(2):
                        for back in range(blk + 1):
                            mm = pe.matmul(b[:, 256 * jj + P * back:256 * jj + P * (back + 1)],
                                           Q[rows, 2 * g + jj, P * blk:P * (blk + 1)],
                                           KD[rows, g, P * (blk - back):P * (blk - back + 1)],
                                           start=True, stop=True)
                    full(mm, ("s", u, hh))

            def swa_turn(u):
                pe.wait_ge(sem("probs"), u + 1)
                p = SM.rearrange("p (k w) -> p k w", w=256)
                for back in range(u % 2 + 1):
                    b = opened(("pt", u, back), 5 + back)
                    for hh in range(2):
                        for jj in range(2):
                            mm = pe.transpose(b[:, P * (2 * hh + jj):P * (2 * hh + jj + 1)],
                                              p[:, 2 * jj + hh, P * back:P * (back + 1)], ident)
                    full(mm, ("pt", u, back))

            def swa_out(u):
                g, blk = u // 2, u % 2
                for back in range(blk + 1):
                    wait_drained(pe, ("pt", u, back))
                b = opened(("o", u), 7)
                for hh in range(2):
                    for back in range(blk + 1):
                        mm = pe.matmul(b[64 * hh:64 * hh + 64, 0:256], VT[:, blk - back, HD * g:HD * (g + 1)],
                                       PTs[:, 512 * back + 256 * hh:512 * back + 256 * (hh + 1)],
                                       start=(back == 0), stop=(back == blk))
                full(mm, ("o", u))

            def mem_scores(h):
                b = opened(("ms", h), 3)
                for qb in range(2):
                    for dt in range(2):
                        mm = pe.matmul(b[:, MEM * qb:MEM * (qb + 1)], MQ[:, 2 * h + dt, P * qb:P * (qb + 1)],
                                       MK[:, 2 * h + dt, :], start=(dt == 0), stop=(dt == 1))
                full(mm, ("ms", h))

            def mem_turn(h):
                pe.wait_ge(sem("probs"), 8 + h + 1)
                b = opened(("mpt", h), 5)
                for mt in range(2):
                    for qb in range(2):
                        mm = pe.transpose(b[:, P * (2 * mt + qb):P * (2 * mt + qb + 1)],
                                          SM[:, MEM * qb + P * mt:MEM * qb + P * (mt + 1)], ident)
                full(mm, ("mpt", h))

            def mem_out(h):
                wait_drained(pe, ("mpt", h))
                b = opened(("mo", h), 7)
                for dt in range(2):
                    for mt in range(2):
                        mm = pe.matmul(b[:, 256 * dt:256 * (dt + 1)],
                                       MV[:, mt, MEM_D * h + P * dt:MEM_D * h + P * (dt + 1)],
                                       PTs[:, 256 * mt:256 * (mt + 1)], start=(mt == 0), stop=(mt == 1))
                full(mm, ("mo", h))

            def sample_bc(b_):
                for a in range(2):
                    name = ("bb", b_, a)
                    b = opened(name, 3 + a)
                    full(pe.matmul(b[:, :], ident[0:8, b_:b_ + 1].to_broadcast([8, P]),
                                   SBC[:, 512 * a:512 * (a + 1)], start=True, stop=True), name)

            def ring_arrives(r):
                pe.wait_ge(sem(f"ring_in{r % 2}"), 16 * (r // 2 + 1) + 16 * BATCH_S * (r == 18))
                return RING[r % 2]

            def sample_mem_scores(b_):
                kc = ring_arrives(b_).rearrange("p (h dt m) -> p h dt m", dt=2, m=MEM)
                b = opened(("sms", b_), 6)
                for mt in range(2):
                    for h in range(MEM_H):
                        for dt in range(2):
                            mm = pe.matmul(b[:, 4 * mt + h:4 * mt + h + 1], kc[:, h, dt, P * mt:P * (mt + 1)],
                                           MQ[:, 2 * h + dt, SEQ + b_:SEQ + b_ + 1],
                                           start=(dt == 0), stop=(dt == 1))
                full(mm, ("sms", b_))

            def sample_swa_scores(part):
                ring_arrives(8 + part)
                pe.wait_ge(sem("new_key"), part + 1)
                kc = RING[part].rearrange("p (g b m) -> p g b m", b=4, m=P)
                for hh in range(2):
                    rows = slice(64 * hh, 64 * hh + 64)
                    b = opened(("sss", part, hh), 6 + hh)
                    for b_ in range(4):
                        for g in range(KV):
                            c0 = 8 * b_ + 2 * g
                            mm = pe.matmul(b[:, c0:c0 + 2], kc[rows, g, b_, :],
                                           Q[rows, 2 * g:2 * g + 2, SEQ + 4 * part + b_], start=True, stop=True)
                    full(mm, ("sss", part, hh))

            def sample_turn():
                wait_drained(pe, ("sms", BATCH_S - 1))
                b = opened("sct", 3)
                for mt in range(2):
                    mm = pe.transpose(b[0:32, P * mt:P * (mt + 1)], SC[:, 32 * mt:32 * (mt + 1)], ident)
                wait_drained(pe, ("sss", 1, 0))
                wait_drained(pe, ("sss", 1, 1))
                full(pe.transpose(b[:, 256:384], SC2, ident), "sct")

            def sample_back():
                pe.wait_ge(sem("sample_probs"), 2)
                b = opened("spt", 4)
                for mt in range(2):
                    pe.transpose(b[:, 32 * mt:32 * (mt + 1)], SM[0:32, P * mt:P * (mt + 1)], ident[0:32, 0:32])
                full(pe.transpose(b[:, 64:192], SM[:, 256:384], ident), "spt")

            def sample_mem_out(b_):
                vc = ring_arrives(10 + b_).rearrange("p (mt n) -> p mt n", mt=2)
                if b_ == 0:
                    wait_drained(pe, "spt")
                b = opened(("smo", b_), 5)
                for h in range(MEM_H):
                    for dt in range(2):
                        c = 2 * h + dt
                        for mt in range(2):
                            mm = pe.matmul(b[:, c:c + 1], vc[:, mt, P * c:P * (c + 1)],
                                           PTs[:, 32 * mt + 4 * b_ + h:32 * mt + 4 * b_ + h + 1],
                                           start=(mt == 0), stop=(mt == 1))
                full(mm, ("smo", b_))

            def sample_swa_out():
                vc = ring_arrives(18).rearrange("p (b n) -> p b n", b=BATCH_S)
                b = opened("sso", 6)
                for b_ in range(BATCH_S):
                    for g in range(KV):
                        for hh in range(2):
                            c0 = 64 + 16 * b_ + 4 * g + 2 * hh
                            mm = pe.matmul(b[64 * hh:64 * hh + 64, 8 * b_ + 2 * g:8 * b_ + 2 * g + 2],
                                           vc[:, b_, HD * g:HD * (g + 1)], PTs[:, c0:c0 + 2],
                                           start=True, stop=True)
                full(mm, "sso")

            for i in range(40):
                name = ("z", i // 2) if i < 16 else ("gate", (i - 16) // 2)
                w = arrive(name)
                feature_tile(("zg", i), w, i % 2, HN, T, name)
                if i < 8:
                    ssd_bcast(i)
                if 1 <= i < 9:
                    ssd_y(i - 1)
                if i < 12:
                    qk(i)
                if 10 <= i < 14:
                    state(i - 10)
                if i in (12, 13):
                    for h in (2 * i - 24, 2 * i - 23):
                        if h == 0:
                            pe.wait_ge(sem("mq_squared"), 1)
                        squares(("ss_mq", h), 6 + h % 2, QSQ, 2 * h, 2, T)
                if i == 14:
                    pe.wait_ge(sem("qk_ready"), 12)
                if 14 <= i < 22:
                    swa_scores(i - 14)
                if 15 <= i < 23:
                    swa_turn(i - 15)
                if 16 <= i < 24:
                    swa_out(i - 16)
                if i == 23:
                    pe.wait_ge(sem("mq_ready"), 1)
                    pe.wait_ge(sem("mk_ready"), 1)
                if 23 <= i < 27:
                    mem_scores(i - 23)
                if 24 <= i < 28:
                    mem_turn(i - 24)
                if 25 <= i < 29:
                    mem_out(i - 25)
                if 14 <= i < 38 and (i - 14) % 3 == 0:
                    sample_bc((i - 14) // 3)
                if 24 <= i < 32:
                    sample_mem_scores(i - 24)
                if i in (32, 33):
                    sample_swa_scores(i - 32)
                if i == 35:
                    sample_turn()
                if i == 37:
                    sample_back()
                if 38 <= i:
                    sample_mem_out(2 * (i - 38))
                    sample_mem_out(2 * (i - 38) + 1)
            for b_ in range(4, BATCH_S):
                sample_mem_out(b_)
            sample_swa_out()

            wait_drained(pe, ("mo", 3))
            wait_drained(pe, ("smo", BATCH_S - 1))
            wait_drained(pe, "sso")
            for i in range(4):
                for kind, x in (("swa", Q), ("memb", MQ)):
                    w = arrive((kind, i))
                    for c in range(2):
                        feature_tile((kind, 2 * i + c), w, c, x, T, (kind, i))
            pe.wait_ge(sem("y_squared"), 1)
            squares("ss_y", 3, X, 0, XS_T, T)
            pe.wait_ge(sem("y_ready"), 1)
            for i in range(4):
                wa = arrive(("ssma", i))
                wb = arrive(("ssmb", i))
                for c in range(2):
                    name = ("ssm", 2 * i + c)
                    b = next_proj(name)
                    for k in range(XS_T):
                        w = wa if k < KT else wb
                        mm = pe.matmul(b[:, 0:T], w[:, k % KT, P * c:P * (c + 1)], C[:, k, :],
                                       start=(k == 0), stop=(k == XS_T - 1))
                    full(mm, name)
                    last_use[("ssma", i)] = last_use[("ssmb", i)] = name
            pe.wait_ge(sem("merged"), 8)
            for i in range(4):
                w = arrive(("out", i))
                for c in range(2):
                    feature_tile(("out", 2 * i + c), w, c, MERGED, T, ("out", i))
            pe.wait_ge(sem("x1_squared"), 1)
            squares("ss_x1", 4, X1SQ, 0, KT, T)
            pe.wait_ge(sem("h_ready"), 1)
            pe.wait_ge(sem("router_in"), 16)
            b = opened("route", 5)
            for t, rows in enumerate((P, P, BATCH_S)):
                for k in range(KT):
                    mm = pe.matmul(b[0:rows, 64 * t:64 * t + ROUTES], HT[:, k, P * t:P * t + rows],
                                   WR[:, k, :], start=(k == 0), stop=(k == KT - 1))
            full(mm, "route")
            for t, rows in enumerate((P, P, BATCH_S)):
                for half in range(2):
                    name = ("htok", t, half)
                    b = opened(name, (6, 7, 3, 4)[(2 * t + half) % 4])
                    for q in range(4):
                        mm = pe.transpose(b[0:rows, P * q:P * (q + 1)], HT[:, 4 * half + q, P * t:P * t + rows], ident)
                    full(mm, name)
            pe.wait_ge(sem("chosen"), 1)
            b = opened("count", 5)
            causal = tab("causal")
            pe.matmul(b[:, 0:32], causal[:, 0:P], MASK[:, 0, :], start=True, stop=True)
            pe.matmul(b[:, 32:64], ones, MASK[:, 0, :], start=True, stop=False)
            pe.matmul(b[:, 32:64], causal[:, 0:P], MASK[:, 1, :], start=False, stop=True)
            pe.matmul(b[0:8, 64:96], ones[:, 0:8], MASK[:, 0, :], start=True, stop=False)
            pe.matmul(b[0:8, 64:96], ones[:, 0:8], MASK[:, 1, :], start=False, stop=False)
            pe.matmul(b[0:8, 64:96], causal[0:8, 0:8], MASK[0:8, 2, :], start=False, stop=True)
            pe.matmul(b[:, 96:128], ones, MASK[:, 0, :], start=True, stop=False)
            pe.matmul(b[:, 96:128], ones, MASK[:, 1, :], start=False, stop=False)
            full(pe.matmul(b[:, 96:128], ones[0:8, :], MASK[0:8, 2, :], start=False, stop=True), "count")

            for b in range(8):
                if uses[b]:
                    pe.wait_ge(drained[b], uses[b])

            def experts(rounds):
                def body(buf, q, n):
                    pe.wait_ge(sem("slots_ready"), n + 1)
                    for k in range(KT):
                        for t, rows in enumerate((P, P, BATCH_S)):
                            mm = pe.matmul(psum[4 + k // 4][:, P * (k % 4):P * (k % 4 + 1)],
                                           HTOK[0:rows, t, P * k:P * (k + 1)],
                                           ONE[0:rows, t].rearrange("p j s -> p (j s)"), start=(t == 0), stop=(t == 2))
                        if k % 4 == 3:
                            mm.then_inc(sem(f"gathered{k // 4}"), 1)
                    pe.wait_ge(sem("tile_added"), n * KT + 2)
                    for t, rows in enumerate((P, P, BATCH_S)):
                        mm = pe.transpose(psum[6][:, P * t:P * t + rows],
                                          ONEW[0:rows, t].rearrange("p j s -> p (j s)"), ident[0:rows, 0:rows])
                    mm.then_inc(sem("back_filled"), 1)
                    pe.wait_ge(sem("gathered_stored"), n * 2 + 2)
                    for bank, kind in enumerate(("gate", "up")):
                        if kind == "gate":
                            pe.wait_ge(gate_in[buf], (q - buf) * (16 * QUAD // 2) + 16 * QUAD)
                        else:
                            pe.wait_ge(up_in, q * (16 * QUAD) + 16 * QUAD)
                        for k in range(KT):
                            for j in range(QUAD):
                                mm = pe.matmul(psum[bank][SLOTS * j:SLOTS * (j + 1), 0:D_FF],
                                               HG[:, k, SLOTS * j:SLOTS * (j + 1)], piece(kind, buf, j)[:, k, :],
                                               start=(k == 0), stop=(k == KT - 1))
                        mm.then_inc(sem(f"{kind}_filled"), 1)
                    pe.wait_ge(sem("act_ready"), n + 1)
                    for f in range(FF_T):
                        mm = pe.transpose(psum[4][:, P * f:P * (f + 1)], ACTV[:, P * f:P * (f + 1)], ident)
                    mm.then_inc(sem("act_turned"), 1)
                    pe.wait_ge(down_in, q * (16 * QUAD) + 16 * QUAD)
                    pe.wait_ge(sem("actT_ready"), n + 1)
                    for half in range(2):
                        for f in range(FF_T):
                            for j in range(QUAD):
                                mm = pe.matmul(psum[2 + half][SLOTS * j:SLOTS * (j + 1), :],
                                               ACTT[:, f, SLOTS * j:SLOTS * (j + 1)],
                                               piece("down", buf, j)[:, f, 512 * half:512 * (half + 1)],
                                               start=(f == 0), stop=(f == 1))
                        mm.then_inc(sem(f"down_filled{half}"), 1)
                    pe.wait_ge(sem("back_ready"), n + 1)
                    for m in range(KT):
                        if m % 4 == 0:
                            pe.wait_ge(sem(f"down_stored{m // 4}"), n + 1)
                        pe.wait_ge(sem("tile_added"), n * KT + (m + 1))
                        pe.matmul(psum[6 + m % 2][:, 0:T], DOWNED[:, P * m:P * (m + 1)], BACK,
                                  start=True, stop=True).then_inc(sem("tile_filled"), 1)

                steps(pe, rounds, body)

            by_rounds(pe, experts)

        @block.sync
        def _(sp):
            sp.dma_start(at("tab"), ins["tables"]).then_inc(sem("tables_in"), 16)
            sp.dma_start(at("vec"), ins["vectors"]).then_inc(sem("tables_in"), 16)
            sp.dma_start(XT, ins["xT"]).then_inc(sem("x_in"), 16)
            sp.dma_start(MT, ins["memT"]).then_inc(sem("mem_in"), 16)

            def load_chunk(n):
                name, parts = chunks[n]
                if n >= WBUFS:
                    wait_filled(sp, last_use[chunks[n - WBUFS][0]])
                for src, c0, width in parts:
                    if name == ("dt", 0):
                        off = MAP["W"][0] + CHUNK * (n % WBUFS)
                        dst = M[:, off:off + KT * width].rearrange("p (k n) -> p k n", n=width)
                    else:
                        dst = chunk(n)[:, :, c0:c0 + width]
                    sp.dma_start(dst, src).then_inc(chunk_in[n % WBUFS], 16)

            def load_ring(r):
                dst = RING[r % 2]
                if r == 0:
                    for g in range(4):
                        wait_filled(sp, ("cb", g))
                    for a in range(2):
                        wait_filled(sp, ("sbc", a))
                        wait_filled(sp, ("btok", a))
                elif r == 1:
                    wait_filled(sp, ("state", 3))
                elif r < 10:
                    wait_filled(sp, ("sms", r - 2))
                elif r < 12:
                    wait_filled(sp, ("sss", r - 10, 1))
                    sp.wait_ge(sem(f"s_k_out{r - 10}"), 16)
                else:
                    wait_filled(sp, ("smo", r - 12))
                if r < 8:
                    src = ins["mem_kT"][r]
                elif r < 10:
                    src = ins["swa_kT"][r - 8]
                elif r < 18:
                    src = ins["mem_v"][r - 10]
                else:
                    src = ins["swa_v"]
                sp.dma_start(dst, src).then_inc(sem(f"ring_in{r % 2}"), 16)
                if r == 18:
                    sp.wait_ge(sem("ring_in0"), 160)
                    wait_drained(sp, ("v", 2))
                    for b_ in range(BATCH_S):
                        sp.dma_start(dst[0:1, 256 * b_:256 * (b_ + 1)], VT[b_:b_ + 1, 2, :]
                                     ).then_inc(sem("ring_in0"), 16)

            first_z = number[("z", 0)]
            r = 0
            for n in range(number[("swa", 0)]):
                load_chunk(n)
                m = n - first_z
                while r < 12 and m >= 0 and m >= (27 + r) / 2 - (5 if r < 2 else 0):
                    load_ring(r)
                    r += 1
            while r < 19:
                load_ring(r)
                r += 1

            def load_piece(kind, e, q, j):
                src = ins[f"w_exp_{kind}"][e].rearrange("(k p) f -> p k f", p=P)
                sp.dma_start(piece(kind, q, j), src).then_inc(
                    {"gate": gate_in[q % 2], "up": up_in, "down": down_in}[kind], 16)

            for n in range(number[("swa", 0)], len(chunks)):
                name = chunks[n][0]
                load_chunk(n)
                if name == ("memb", 0):
                    wait_filled(sp, "sso")
                    wait_filled(sp, ("smo", BATCH_S - 1))
                    wait_drained(sp, "sso")
                    sp.wait_ge(sem("s_v_out"), 16)
                    sp.wait_ge(sem("samples_done"), 1)
                    load_piece("gate", 0, 0, 0)
                    load_piece("gate", 1, 0, 1)
                elif name == ("swa", 1):
                    load_piece("gate", 2, 0, 2)
                    sp.dma_start(HN, ins["xT"]).then_inc(sem("x_again"), 16)
                elif name == ("memb", 1):
                    load_piece("gate", 3, 0, 3)
                elif name == ("memb", 2):
                    sp.wait_ge(sem("y_gated"), 1)
                    load_piece("up", 0, 0, 0)
                elif name == ("memb", 3):
                    load_piece("up", 1, 0, 1)
                elif name == ("ssmb", 1):
                    wait_filled(sp, ("swa", 7))
                    wait_filled(sp, ("memb", 7))
                    load_piece("up", 2, 0, 2)
                    load_piece("up", 3, 0, 3)
                elif name == ("ssmb", 2):
                    load_piece("down", 0, 0, 0)
                    wait_filled(sp, "ss_y")
                    load_piece("down", 1, 0, 1)
                elif name == ("ssmb", 3):
                    load_piece("down", 2, 0, 2)
            sp.wait_ge(sem("merged"), 8)
            load_piece("down", 3, 0, 3)
            for j in range(QUAD):
                load_piece("gate", QUAD + j, 1, j)

            def experts(rounds):
                def up_down(q, buf):
                    sp.wait_ge(sem("up_filled"), q * rounds)
                    for j in range(QUAD):
                        load_piece("up", q * QUAD + j, buf, j)
                    sp.wait_ge(sem("down_filled1"), q * rounds)
                    for j in range(QUAD):
                        load_piece("down", q * QUAD + j, buf, j)

                with sp.Fori(0, QUADS // 2 - 1) as it:
                    for b in range(1, 3):
                        q = it * 2 + b
                        up_down(q, b % 2)
                        sp.wait_ge(sem("gate_filled"), q * rounds)
                        for j in range(QUAD):
                            load_piece("gate", (q + 1) * QUAD + j, b + 1, j)
                up_down(QUADS - 1, 1)
                sp.wait_ge(sem("tile_added"), 2 + KT * QUADS * rounds)

            by_rounds(sp, experts)
            sp.dma_start(outs["yT"], X1).then_inc(sem("y_out"), 16)
            sp.wait_ge(sem("y_out"), 16)

        @block.gpsimd
        def _(pool):
            pool.wait_ge(sem("mk_ready"), 1)
            pool.dma_start(outs["p_mem_kT"], MK).then_inc(sem("p_mem_out"), 16)
            pool.dma_start(HIST, ins["histT"]).then_inc(sem("hist_in"), 16)
            for i in range(4):
                for mt in range(2):
                    wait_drained(pool, ("mv", i, mt))
            pool.dma_start(outs["p_mem_v"], MV).then_inc(sem("p_mem_out"), 16)
            for t in range(3):
                wait_drained(pool, ("v", t))
            pool.dma_start(outs["p_swa_v"], VT[:, 1, :]).then_inc(sem("p_v_out"), 16)
            pool.wait_ge(sem("new_conv"), 1)
            pool.dma_start(outs["newconvT"], NEWC).then_inc(sem("conv_out"), 16)

            def load_state(b):
                if b >= 2:
                    pool.wait_ge(sem(f"s_ssm_out{b % 2}"), 16 * (b // 2))
                pool.dma_start(HS[b % 2], ins["state_ssm"][b].rearrange("(j p) n -> p j n", p=P)
                               ).then_inc(sem(f"state_in{b % 2}"), 16)

            pool.wait_ge(sem("conv_active"), 3)
            load_state(0)
            load_state(1)
            pool.wait_ge(sem("qk_ready"), 12)
            pool.dma_start(outs["p_swa_kT"], KD[0:64, :, P:SEQ]).then_inc(sem("p_k_out"), 16)
            for g in range(4):
                wait_drained(pool, ("state", g))
            pool.dma_start(outs["p_ssm"].rearrange("(j p) n -> p j n", p=P),
                           at("S", 0, 2048).rearrange("p (j n) -> p j n", n=STATE)).then_inc(sem("p_ssm_out"), 16)

            def store_state(b):
                pool.wait_ge(sem("state_new"), b + 1)
                pool.dma_start(outs["s_ssm"][b].rearrange("(j p) n -> p j n", p=P), HS[b % 2]
                               ).then_inc(sem(f"s_ssm_out{b % 2}"), 16)

            for b in range(BATCH_S):
                store_state(b)
                if b + 2 < BATCH_S:
                    pool.wait_ge(sem("sample_y"), b + 1)
                    load_state(b + 2)
                if b == 5:
                    for part in range(2):
                        pool.wait_ge(sem("new_key"), part + 1)
                        pool.dma_start(outs["s_swa_kT"][part], RING[part][0:64, :]).then_inc(sem(f"s_k_out{part}"), 16)
            pool.wait_ge(sem("ring_in0"), 160 + 16 * BATCH_S)
            pool.dma_start(outs["s_swa_v"], RING[0]).then_inc(sem("s_v_out"), 16)
            pool.wait_ge(sem("samples_done"), 1)
            pool.dma_start(WR, ins["w_router"].rearrange("(k p) n -> p k n", p=P)).then_inc(sem("router_in"), 16)
            for name, n in (("p_mem_out", 32), ("p_v_out", 16), ("conv_out", 16), ("p_k_out", 16), ("p_ssm_out", 16),
                            ("s_ssm_out0", 64), ("s_ssm_out1", 64), ("s_k_out0", 16), ("s_k_out1", 16), ("s_v_out", 16)):
                pool.wait_ge(sem(name), n)

        @block.scalar
        def _(act):
            a = nc.scalar

            def evac(name, dst, n, rows=P, src=None):
                b = wait_filled(act, name)
                drains(a.activation(dst, b[0:rows, 0:n] if src is None else src(b), ACT.Copy), name)

            def rstd(name, dst, width, n):
                b = wait_filled(act, name)
                a.preload_act_table_set("natural_log_exp_and_others")
                drains(a.activation(dst, b[:, 0:n], ACT.Ln, scale=1.0 / width, bias=EPS), name)
                wait_drained(act, name)
                done(act, a.activation(dst, dst, ACT.Exp, scale=-0.5), "rstd")

            act.wait_ge(sem("x_in"), 16)
            a.activation(XSQ, XT, ACT.Square).then_inc(sem("x_squared"), 1)
            act.wait_ge(sem("mem_in"), 16)
            a.activation(MSQ, MT, ACT.Square).then_inc(sem("mem_squared"), 1)
            rstd("ss_x", RS, D_MODEL, T)
            rstd("ss_mem", TQ[:, 0:MEM], D_MODEL, MEM)
            for j in range(8):
                evac(("mk", j), MK[:, j, :], MEM)
            wait_drained(act, ("mk", 7))
            a.activation(MSQ, MK, ACT.Square).then_inc(sem("mk_squared"), 1)
            for i in range(4):
                for mt in range(2):
                    evac(("mv", i, mt), MV[:, mt, CW * i:CW * (i + 1)], CW)
            for h in range(MEM_H):
                rstd(("ss_mk", h), RSM[:, h, :], MEM_D, MEM)

            def silu_conv(batch):
                act.wait_ge(sem("convolved"), batch + 1)
                v = C[:, 8 * batch:8 * (batch + 1), :]
                a.activation(v, v, ACT.Silu).then_inc(sem("conv_active"), 1)

            for j in range(CONV_T):
                evac(("xbc", j), X[:, j, :], T)
                if j == 13:
                    silu_conv(0)
                if j == 21:
                    silu_conv(1)
            for j in range(KV):
                evac(("kd", j), KD[:, j, :], T)
            wait_drained(act, ("kd", 3))
            a.activation(KSQ, KD, ACT.Square).then_inc(sem("qk_squared"), 1)
            for t, rows in enumerate((P, P, BATCH_S)):
                evac(("v", t), VT[0:rows, t, :], CW, rows)
            act.wait_ge(sem("dt_minus_abs"), 1)
            a.preload_act_table_set("natural_log_exp_and_others")
            E1, U1, L1 = (at("S", 96 * i, 96 * (i + 1)) for i in range(1, 4))
            done(act, a.activation(E1, E1, ACT.Exp), "dt_exp")
            act.wait_ge(sem("dt_one_plus"), 1)
            done(act, a.activation(L1, U1, ACT.Ln), "dt_ln")
            a.activation(at("S", 384, 384 + 32), vec("a_log"), ACT.Exp).then_inc(sem("a_exp"), 1)
            act.wait_ge(sem("dta"), 1)
            a.activation(at("S", 416, 448, 8), DTA[0:8, 2, :], ACT.Exp).then_inc(sem("da_exp"), 1)
            for j in range(8):
                evac(("q", j), Q[:, j, :], T)
                if j == 1:
                    silu_conv(2)
            wait_drained(act, ("q", 7))
            a.activation(QSQ, Q, ACT.Square).then_inc(sem("qk_squared"), 1)
            act.wait_ge(sem("to_end"), 1)
            a.activation(WE, WE, ACT.Exp).then_inc(sem("end_decay"), 1)
            for j in range(8):
                evac(("mq", j), MQ[:, j, :], T)
                if j == 4:
                    for half in range(2):
                        evac(("btok", half), BT[:, half, :], 512)
                    for k in range(2):
                        evac(("sbc", k), SBC[:, 512 * k:512 * (k + 1)], 512, 8)

            for i in range(42):
                if i < 40:
                    evac(("zg", i), Z[:, i, :] if i < 16 else G[:, i - 16, :], T)
                if i < 8:
                    act.wait_ge(sem("segments"), i + 1)
                    D = at("S", 1536 * (i % 2), 1536 * (i % 2 + 1))
                    a.activation(D, D, ACT.Exp).then_inc(sem("decay_exp"), 1)
                if i < 12:
                    if i:
                        act.wait_ge(sem("qk_ready"), i)
                    rstd(("qk_ss", i), RS, HD, T)
                if i == 9:
                    wait_filled(act, ("qk_ss", 7))
                    wait_drained(act, ("mq", 7))
                    a.activation(QSQ, MQ, ACT.Square).then_inc(sem("mq_squared"), 1)
                if 10 <= i < 14:
                    if i == 10:
                        wait_filled(act, ("y", 7))
                    g = i - 10
                    evac(("state", g), at("S", 512 * g, 512 * (g + 1)), 512)
                if i in (12, 13):
                    for h in (2 * i - 24, 2 * i - 23):
                        if h == 0:
                            act.wait_ge(sem("qk_ready"), 12)
                        else:
                            act.wait_ge(sem("mq_scaled"), h)
                        rstd(("ss_mq", h), RS, MEM_D, T)
                if 16 <= i < 24:
                    u = i - 16
                    g, blk = u // 2, u % 2
                    evac(("o", u), Q[:, 2 * g:2 * g + 2, P * blk:P * (blk + 1)], 256,
                         src=lambda b: b[:, 0:256].rearrange("p (j q) -> p j q", j=2))
                if 25 <= i < 29:
                    h = i - 25
                    evac(("mo", h), MQ[:, 2 * h:2 * h + 2, 0:SEQ], 512,
                         src=lambda b: b[:, :].rearrange("p (j q) -> p j q", j=2))
                if 14 <= i < 22:
                    u = i - 14
                    width = P * (u % 2 + 1)
                    act.wait_ge(sem("swa_max"), u + 1)
                    for k in range(4):
                        p = SM[:, 256 * k:256 * k + width]
                        a.activation(p, p, ACT.Exp, bias=at("ST", 4 + k, 5 + k), accum_out=at("ST", 8 + k, 9 + k))
                    a.activation(at("ST", 12, 16), at("ST", 12, 16), ACT.Exp).then_inc(sem("exps"), 1)
                if 23 <= i < 27:
                    h = i - 23
                    act.wait_ge(sem("mem_max"), h + 1)
                    if h:
                        wait_filled(act, ("mpt", h - 1))
                    else:
                        wait_filled(act, ("pt", 7, 1))
                    b = wait_filled(act, ("ms", h))
                    a.activation(SM[:, 0:MEM], b[:, 0:MEM], ACT.Exp, bias=at("ST", 20, 21), scale=MEM_D ** -0.5,
                                 accum_out=at("ST", 24, 25)).then_inc(sem("mem_exp0"), 1)
                    done(act, a.activation(SM[:, MEM:2 * MEM], b[:, MEM:2 * MEM], ACT.Exp, bias=at("ST", 21, 22),
                                           scale=MEM_D ** -0.5, accum_out=at("ST", 25, 26)), "exps")
                if 14 <= i < 38 and (i - 14) % 3 == 0:
                    b_ = (i - 14) // 3
                    if b_ == 0:
                        act.wait_ge(sem("p_ssm_out"), 16)
                    else:
                        act.wait_ge(sem("sample_y"), b_)
                    for k in range(2):
                        evac(("bb", b_, k), BB[:, 512 * k:512 * (k + 1)], 512)
                if 24 <= i < 32:
                    b_ = i - 24
                    evac(("sms", b_), SC.rearrange("p (mt b h) -> p mt b h", mt=2, h=MEM_H)[:, :, b_, :], 8,
                         src=lambda b: b[:, 0:8].rearrange("p (mt h) -> p mt h", mt=2))
                if i in (32, 33):
                    for hh in range(2):
                        dst = SC2[:, 64 * (i - 32):64 * (i - 31)].rearrange("p (bg hh jj) -> p bg hh jj", hh=2, jj=2)
                        evac(("sss", i - 32, hh), dst[:, :, hh, :], 32,
                             src=lambda b: b[:, 0:32].rearrange("p (bg jj) -> p bg jj", jj=2))
                if i == 36:
                    act.wait_ge(sem("sample_max"), 1)
                    b = wait_filled(act, "sct")
                    wait_filled(act, ("mpt", 3))
                    a.activation(SM[0:32, 0:MEM], b[0:32, 0:MEM], ACT.Exp, bias=at("ST", 32, 33, 32),
                                 scale=MEM_D ** -0.5, accum_out=at("ST", 34, 35, 32)).then_inc(sem("sexp0"), 1)
                    a.activation(SM[:, 256:384], b[:, 256:384], ACT.Exp, bias=at("ST", 33, 34),
                                 scale=HD ** -0.5, accum_out=at("ST", 35, 36)).then_inc(sem("sexp1"), 1)
                    a.activation(at("ST", 36, 37), at("ST", 36, 37), ACT.Exp).then_inc(sem("sample_exps"), 1)
                if i in (38, 39):
                    for b_ in (2 * (i - 38), 2 * (i - 38) + 1):
                        evac(("smo", b_), MQ[:, 0:8, SEQ + b_], 8)
            for b_ in range(4, BATCH_S):
                evac(("smo", b_), MQ[:, 0:8, SEQ + b_], 8)
            evac("sso", Q[:, 0:8, SEQ:T].rearrange("p t b -> p b t"), 64,
                 src=lambda b: b[:, 0:64].rearrange("p (b t) -> p b t", b=BATCH_S))
            wait_drained(act, ("zg", 39))
            wait_drained(act, ("zg", 38))
            wait_drained(act, ("zg", 37))
            a.activation(at("Z"), at("Z"), ACT.Silu).then_inc(sem("z_active"), 1)
            a.activation(at("G"), at("G"), ACT.Sigmoid).then_inc(sem("gates_active"), 1)
            act.wait_ge(sem("y_gated"), 1)
            act.wait_ge(sem("s_ssm_out0"), 64)
            act.wait_ge(sem("s_ssm_out1"), 64)
            a.activation(X[:, 0:XS_T, :], C[:, 0:XS_T, :], ACT.Square).then_inc(sem("y_squared"), 1)
            rstd("ss_y", RS, D_INNER, T)
            act.wait_ge(sem("x1_made"), 1)
            act.wait_ge(sem("p_mem_out"), 32)
            a.activation(X1SQ, X1, ACT.Square).then_inc(sem("x1_squared"), 1)
            rstd("ss_x1", RS, D_MODEL, T)
            for t, rows in enumerate((P, P, BATCH_S)):
                for half in range(2):
                    evac(("htok", t, half), HTOK[0:rows, t, 512 * half:512 * (half + 1)], 512, rows)
            act.wait_ge(sem("route_args"), 1)
            done(act, a.activation(at("S", 1100, 1112), at("S", 1100, 1112), ACT.Exp), "route_exp")
            done(act, a.activation(at("S", 1112, 1115), at("S", 1112, 1115), ACT.Exp), "route_exp")

            def experts(rounds):
                def body(buf, q, n):
                    act.wait_ge(sem("gathered0"), n + 1)
                    a.activation(HG[:, 0:4, :].rearrange("p k s -> p (k s)"), psum[4][:, :], ACT.Copy
                                 ).then_inc(sem("gathered_stored"), 1)
                    act.wait_ge(sem("gate_filled"), n + 1)
                    a.activation(SG, psum[0][:, 0:D_FF], ACT.Silu).then_inc(sem("silu"), 1)
                    act.wait_ge(sem("down_filled0"), n + 1)
                    a.activation(DOWNED[:, 0:512], psum[2][:, :], ACT.Copy).then_inc(sem("down_stored0"), 1)

                steps(act, rounds, body)

            by_rounds(act, experts)

        @block.vector
        def _(dve):
            v = nc.vector

            def link(ins_):
                done(dve, ins_, "vector_chain")

            dve.wait_ge(sem("tables_in"), 32)
            dve.wait_ge(sem("x_in"), 16)
            dve.wait_ge(sem("rstd"), 1)
            link(v.tensor_tensor(HN, XT, each(RS, KT), ALU.mult))
            v.tensor_tensor(HN, HN, over(vec("g1"), T), ALU.mult).then_inc(sem("x_normed"), 1)
            dve.wait_ge(sem("mem_in"), 16)
            dve.wait_ge(sem("rstd"), 2)
            link(v.tensor_tensor(MN, MT, each(TQ[:, 0:MEM], KT), ALU.mult))
            v.tensor_tensor(MN, MN, over(vec("gmem"), MEM), ALU.mult).then_inc(sem("mem_normed"), 1)
            for h in range(MEM_H):
                dve.wait_ge(sem("rstd"), 3 + h)
                for dt in range(2):
                    t = MK[:, 2 * h + dt, :]
                    last = v.scalar_tensor_tensor(t, t, vec("gmk", dt, dt + 1), RSM[:, h, :], ALU.mult, ALU.mult)
            last.then_inc(sem("mk_ready"), 1)

            def tap(j, k):
                a_, _n = VEC["conv_w"]
                return at("vec", a_ + CONV_T * k + j, a_ + CONV_T * k + j + 1)

            def conv(batch):
                js = range(8 * batch, 8 * (batch + 1))
                wait_drained(dve, ("xbc", js[-1]))
                wait_drained(dve, ("xbc", js[-2]))
                wait_drained(dve, ("xbc", js[-3]))
                for j in js:
                    last = v.tensor_scalar(C[:, j, 0:SEQ], X[:, j, 0:SEQ], tap(j, 3), vec("conv_b", j, j + 1),
                                           ALU.mult, ALU.add)
                link(last)
                for back in range(1, CONV_TAPS):
                    for j in js:
                        last = v.scalar_tensor_tensor(C[:, j, back:SEQ], X[:, j, 0:SEQ - back], tap(j, 3 - back),
                                                      C[:, j, back:SEQ], ALU.mult, ALU.add)
                    link(last)
                cs, xs_ = C[:, js[0]:js[-1] + 1, SEQ:T], X[:, js[0]:js[-1] + 1, SEQ:T]
                tmp = at("S", 512, 512 + 64).rearrange("p (j b) -> p j b", b=BATCH_S)

                def w(k):
                    return over(vec("conv_w", CONV_T * k + js[0], CONV_T * k + js[-1] + 1), BATCH_S)

                link(v.tensor_tensor(cs, xs_, w(3), ALU.mult))
                dve.wait_ge(sem("hist_in"), 16)
                for k in range(3):
                    link(v.tensor_tensor(tmp, HIST[:, js[0]:js[-1] + 1, :, k], w(k), ALU.mult))
                    link(v.tensor_tensor(cs, cs, tmp, ALU.add))
                done(dve, v.tensor_tensor(cs, cs, over(vec("conv_b", js[0], js[-1] + 1), BATCH_S), ALU.add),
                     "convolved")

            conv(0)
            conv(1)
            conv(2)
            new = NEWC[:, :, 0:24].rearrange("p j (b k) -> p j b k", k=3)
            link(v.tensor_copy(new[:, :, :, 0:2], HIST[:, :, :, 1:3]))
            link(v.tensor_copy(new[:, :, :, 2], X[:, :, SEQ:T]))
            done(dve, v.tensor_copy(NEWC[:, :, 24:27], X[:, :, SEQ - 3:SEQ]), "new_conv")

            R0, E1, U1, L1 = (at("S", 96 * i, 96 * (i + 1)) for i in range(4))
            AEXP, DAS = at("S", 384, 416), at("S", 416, 448, 8)
            R3 = R0.rearrange("p (t h) -> p t h", t=3)
            link(v.memset(R0, 0.0))
            b = wait_filled(dve, "dt")
            link(v.tensor_tensor(R3[:, 0:2, :], b[:, 0:64].rearrange("p (t h) -> p t h", t=2),
                                 each(vec("dt_bias"), 2), ALU.add))
            drains(v.tensor_tensor(R3[0:8, 2, :], b[0:8, 64:96], vec("dt_bias", rows=8), ALU.add), "dt")
            wait_drained(dve, "dt")
            link(v.tensor_scalar(E1, R0, -1.0, None, ALU.mult))
            done(dve, v.tensor_tensor(E1, E1, R0, ALU.min), "dt_minus_abs")
            dve.wait_ge(sem("dt_exp"), 1)
            done(dve, v.tensor_scalar(U1, E1, 1.0, None, ALU.add), "dt_one_plus")
            link(v.tensor_scalar(at("S", 448, 544), U1, -1.0, None, ALU.add))
            link(v.tensor_scalar(at("S", 544, 640), at("S", 448, 544), 0.0, None, ALU.is_equal))
            link(v.tensor_tensor(at("S", 448, 544), at("S", 448, 544), at("S", 544, 640), ALU.add))
            link(v.reciprocal(at("S", 448, 544), at("S", 448, 544)))
            dve.wait_ge(sem("dt_ln"), 1)
            link(v.tensor_tensor(L1, L1, at("S", 544, 640), ALU.add))
            link(v.tensor_tensor(L1, L1, E1, ALU.mult))
            link(v.tensor_tensor(L1, L1, at("S", 448, 544), ALU.mult))
            link(v.tensor_scalar(R0, R0, 0.0, None, ALU.max))
            link(v.tensor_tensor(at("DT"), R0, L1, ALU.add))
            dve.wait_ge(sem("a_exp"), 1)
            link(v.tensor_tensor(DTA, DT, each(AEXP, 3), ALU.mult))
            done(dve, v.tensor_scalar(at("DTA"), at("DTA"), -1.0, None, ALU.mult), "dta")
            dve.wait_ge(sem("da_exp"), 1)
            link(v.tensor_copy(DTX.rearrange("p (h d) -> p h d", d=HEADDIM), over(DT[0:8, 2, :], HEADDIM)))
            done(dve, v.tensor_copy(DAX.rearrange("p (h d) -> p h d", d=HEADDIM), over(DAS, HEADDIM)), "dt_expanded")
            b = wait_filled(dve, "acum")
            link(v.tensor_copy(at("AC"), b[:, 0:64]))
            drains(v.tensor_tensor(WE, each(b[:, 64:96], 2), AC, ALU.subtract), "acum")
            wait_drained(dve, "acum")
            done(dve, v.tensor_scalar(at("WE"), at("WE"), 0.0, None, ALU.min), "to_end")
            b = wait_filled(dve, "ex")
            drains(v.tensor_copy(at("EX"), b[:, 0:256]), "ex")
            wait_drained(dve, "ex")
            dve.wait_ge(sem("qk_squared"), 2)
            done(dve, v.tensor_scalar(at("KD"), at("KD"), vec("gk"), None, ALU.mult), "qk_scaled")
            done(dve, v.tensor_scalar(at("Q"), at("Q"), vec("gq"), None, ALU.mult), "qk_scaled")
            dve.wait_ge(sem("conv_active"), 3)
            link(v.tensor_tensor(XS, C[:, 0:XS_T, SEQ:T], EX[:, 0, :, :], ALU.mult))
            for j in range(4):
                for half in range(2):
                    b = wait_filled(dve, ("xtok", half, j))
                    drains(v.tensor_tensor(XD[:, half, 512 * j:512 * (j + 1)].rearrange("p (h d) -> p h d", d=HEADDIM),
                                           b[:, :].rearrange("p (h d) -> p h d", d=HEADDIM),
                                           over(DT[:, half, 8 * j:8 * (j + 1)], HEADDIM), ALU.mult),
                           ("xtok", half, j))
            for g in range(4):
                b = wait_filled(dve, ("cb", g))
                drains(v.tensor_tensor(CB[:, g, :], b[:, 0:3 * P], tab("causal"), ALU.mult), ("cb", g))
                wait_drained(dve, ("cb", g))

            def segments(u):
                if u >= 2:
                    wait_filled(dve, ("y", u - 2))
                D = tiles("S", 3 * P, 1536 * (u % 2), 1536 * (u % 2 + 1))
                for a_ in range(2):
                    b = wait_filled(dve, ("acb", u, a_))
                    for q in range(2):
                        h = 4 * u + 2 * a_ + q
                        o = b[:, SEQ * q:SEQ * (q + 1)]
                        v.tensor_scalar(D[:, 2 * a_ + q, 0:SEQ], o, AC[:, 0, h:h + 1], 0.0,
                                        ALU.subtract, ALU.min)
                        last = v.tensor_scalar(D[:, 2 * a_ + q, SEQ:3 * P], o[:, P:SEQ], AC[:, 1, h:h + 1], 0.0,
                                               ALU.subtract, ALU.min)
                    if a_ == 0:
                        drains(last, ("acb", u, 0))
                drains(last, ("acb", u, 1))
                wait_drained(dve, ("acb", u, 1))
                done(dve, v.tensor_scalar(at("ST", 60, 61), AC[:, 0, 0:1], 0.0, None, ALU.mult), "segments")

            def decays(u):
                dve.wait_ge(sem("decay_exp"), u + 1)
                D = tiles("S", 3 * P, 1536 * (u % 2), 1536 * (u % 2 + 1))
                done(dve, v.tensor_tensor(D, D, each(CB[:, u // 2, :], 4), ALU.mult), "decay_ready")

            def y_add(u):
                b = wait_filled(dve, ("y", u))
                for q in range(2):
                    j = 2 * u + q
                    last = v.scalar_tensor_tensor(C[:, j, 0:SEQ], C[:, j, 0:SEQ], vec("ssm_d", j, j + 1),
                                                  b[:, SEQ * q:SEQ * (q + 1)], ALU.mult, ALU.add)
                drains(last, ("y", u))

            def rotate(j):
                src = Q[:, j, :] if j < 8 else KD[:, j - 8, :]
                b = wait_filled(dve, ("qk_rot", j))
                drains(v.tensor_tensor(TQ, b[:, 0:T], tab("sin"), ALU.mult), ("qk_rot", j))
                wait_drained(dve, ("qk_rot", j))
                link(v.tensor_tensor(src, src, tab("cos"), ALU.mult))
                link(v.tensor_tensor(src, src, TQ, ALU.add))
                dve.wait_ge(sem("rstd"), 7 + j)
                done(dve, v.tensor_tensor(src, src, RS, ALU.mult), "qk_ready")

            def swa_max(u):
                g, blk = u // 2, u % 2
                width = P * (blk + 1)
                if u:
                    for back in range((u - 1) % 2 + 1):
                        wait_filled(dve, ("pt", u - 1, back))
                for hh in range(2):
                    b = wait_filled(dve, ("s", u, hh))
                    for jj in range(2):
                        k = 2 * jj + hh
                        h = 4 * g + k
                        last = v.tensor_tensor_reduce(SM[:, 256 * k:256 * k + width],
                                                      b[:, 256 * jj:256 * jj + width],
                                                      tab("window")[:, 0:width], HD ** -0.5, vec("sink", h, h + 1),
                                                      ALU.add, ALU.max, at("ST", k, k + 1))
                    drains(last, ("s", u, hh))
                    wait_drained(dve, ("s", u, hh))
                link(v.tensor_scalar(at("ST", 4, 8), at("ST", 0, 4), -1.0, None, ALU.mult))
                done(dve, v.tensor_tensor(at("ST", 12, 16), vec("sink", 4 * g, 4 * g + 4), at("ST", 0, 4),
                                          ALU.subtract), "swa_max")

            def swa_probs(u):
                width = P * (u % 2 + 1)
                dve.wait_ge(sem("exps"), u + 1)
                link(v.tensor_tensor(at("ST", 8, 12), at("ST", 8, 12), at("ST", 12, 16), ALU.add))
                link(v.reciprocal(at("ST", 8, 12), at("ST", 8, 12)))
                p = SM.rearrange("p (k w) -> p k w", w=256)[:, :, 0:width]
                done(dve, v.tensor_tensor(p, p, over(at("ST", 8, 12), width), ALU.mult), "probs")

            def swa_turned(u):
                if u:
                    wait_filled(dve, ("o", u - 1))
                for back in range(u % 2 + 1):
                    b = wait_filled(dve, ("pt", u, back))
                    drains(v.tensor_copy(PTs[:, 512 * back:512 * (back + 1)], b[:, :]), ("pt", u, back))

            def mem_max(h):
                b = wait_filled(dve, ("ms", h))
                link(v.tensor_reduce(at("ST", 18, 20), b[:, :].rearrange("p (q m) -> p q m", q=2), AX.X, ALU.max))
                done(dve, v.tensor_scalar(at("ST", 20, 22), at("ST", 18, 20), -(MEM_D ** -0.5), None, ALU.mult),
                     "mem_max")
                dve.wait_ge(sem("exps"), 8 + h + 1)
                drains(v.reciprocal(at("ST", 24, 26), at("ST", 24, 26)), ("ms", h))
                wait_drained(dve, ("ms", h))
                p = SM[:, 0:2 * MEM].rearrange("p (q m) -> p q m", q=2)
                done(dve, v.tensor_tensor(p, p, over(at("ST", 24, 26), MEM), ALU.mult), "probs")

            def mem_turned(h):
                wait_filled(dve, ("mo", h - 1) if h else ("o", 7))
                b = wait_filled(dve, ("mpt", h))
                drains(v.tensor_copy(PTs[:, 0:512], b[:, :]), ("mpt", h))

            def sample(b_, piece):
                H = HS[b_ % 2]
                if piece == 0:
                    dve.wait_ge(sem(f"state_in{b_ % 2}"), 16 * (b_ // 2 + 1))
                    link(v.tensor_tensor(H, H, over(EX[:, 1, :, b_], STATE), ALU.mult))
                elif piece == 1:
                    if b_ == 0:
                        dve.wait_ge(sem("p_ssm_out"), 16)
                    wait_drained(dve, ("bb", b_, 0))
                    t2 = T2.rearrange("p (g j n) -> p g j n", g=4, n=STATE)
                    bcast = BB[:, 0:512].rearrange("p (g n) -> p g n", g=4).unsqueeze(2).to_broadcast([P, 4, 4, STATE])
                    xdt = XS[:, :, b_].rearrange("p (g j) -> p g j", g=4).unsqueeze(3).to_broadcast([P, 4, 4, STATE])
                    link(v.tensor_tensor(t2, bcast, xdt, ALU.mult))
                    h2 = H.rearrange("p j n -> p (j n)")
                    done(dve, v.tensor_tensor(h2, h2, T2, ALU.add), "state_new")
                else:
                    wait_drained(dve, ("bb", b_, 1))
                    t2 = T2.rearrange("p (g j n) -> p g j n", g=4, n=STATE)
                    bcast = BB[:, 512:1024].rearrange("p (g n) -> p g n", g=4).unsqueeze(2).to_broadcast(
                        [P, 4, 4, STATE])
                    h4 = H.rearrange("p (g j) n -> p g j n", g=4)
                    link(v.tensor_tensor(t2, h4, bcast, ALU.mult))
                    done(dve, v.tensor_reduce(EX[:, 0, :, b_], T2.rearrange("p (j n) -> p j n", n=STATE), AX.X,
                                              ALU.add), "sample_y")

            for i in range(40):
                if 1 <= i < 9:
                    decays(i - 1)
                if i < 8:
                    segments(i)
                if 1 <= i < 9:
                    y_add(i - 1)
                if i < 12:
                    rotate(i)
                if i == 9:
                    dve.wait_ge(sem("end_decay"), 1)
                    x3 = at("XD").rearrange("p (h d) -> p h d", d=HEADDIM)
                    done(dve, v.tensor_tensor(x3, x3, over(at("WE"), HEADDIM), ALU.mult), "xd_weighed")
                if i in (12, 13):
                    for h in (2 * i - 24, 2 * i - 23):
                        dve.wait_ge(sem("rstd"), 19 + h)
                        for dt in range(2):
                            t = MQ[:, 2 * h + dt, :]
                            last = v.scalar_tensor_tensor(t, t, vec("gmq", dt, dt + 1), RS, ALU.mult, ALU.mult)
                        done(dve, last, "mq_scaled")
                    if i == 13:
                        done(dve, v.tensor_scalar(at("ST", 61, 62), RS[:, 0:1], 0.0, None, ALU.mult), "mq_ready")
                        wait_filled(dve, ("state", 3))
                if 15 <= i < 23:
                    swa_probs(i - 15)
                    swa_turned(i - 15)
                if 24 <= i < 28:
                    mem_turned(i - 24)
                if 14 <= i < 22:
                    swa_max(i - 14)
                if 23 <= i < 27:
                    mem_max(i - 23)
                if 14 <= i < 38:
                    sample((i - 14) // 3, (i - 14) % 3)
                if i in (31, 32):
                    part = i - 31
                    dve.wait_ge(sem(f"ring_in{part}"), 16 * 5)
                    kc = RING[part].rearrange("p (g b m) -> p g b m", b=4, m=P)
                    done(dve, v.tensor_copy(kc[:, :, :, 0], KD[:, :, SEQ + 4 * part:SEQ + 4 * (part + 1)]), "new_key")
                if i == 36:
                    b = wait_filled(dve, "sct")
                    link(v.tensor_reduce(at("ST", 32, 33, 32), b[0:32, 0:MEM], AX.X, ALU.max))
                    link(v.tensor_scalar(at("ST", 32, 33, 32), at("ST", 32, 33, 32), -(MEM_D ** -0.5), None, ALU.mult))
                    link(v.tensor_reduce(at("ST", 33, 34), b[:, 256:384], AX.X, ALU.max))
                    link(v.tensor_scalar(at("ST", 33, 34), at("ST", 33, 34), HD ** -0.5, vec("sink_col"),
                                         ALU.mult, ALU.max))
                    link(v.tensor_tensor(at("ST", 36, 37), vec("sink_col"), at("ST", 33, 34), ALU.subtract))
                    done(dve, v.tensor_scalar(at("ST", 33, 34), at("ST", 33, 34), -1.0, None, ALU.mult), "sample_max")
                    dve.wait_ge(sem("sample_exps"), 1)
                    drains(v.tensor_tensor(at("ST", 35, 36), at("ST", 35, 36), at("ST", 36, 37), ALU.add), "sct")
                    wait_drained(dve, "sct")
                    link(v.reciprocal(at("ST", 34, 35, 32), at("ST", 34, 35, 32)))
                    link(v.reciprocal(at("ST", 35, 36), at("ST", 35, 36)))
                    done(dve, v.tensor_scalar(SM[0:32, 0:MEM], SM[0:32, 0:MEM], at("ST", 34, 35, 32), None, ALU.mult),
                         "sample_probs")
                    done(dve, v.tensor_scalar(SM[:, 256:384], SM[:, 256:384], at("ST", 35, 36), None, ALU.mult),
                         "sample_probs")
                if i == 37:
                    wait_filled(dve, ("mo", 3))
                    b = wait_filled(dve, "spt")
                    drains(v.tensor_copy(PTs[:, 0:192], b[:, 0:192]), "spt")
            ys = C[:, 0:XS_T, SEQ:T]
            link(v.tensor_tensor(ys, ys, over(vec("ssm_d"), BATCH_S), ALU.mult))
            done(dve, v.tensor_tensor(ys, ys, EX[:, 0, :, :], ALU.add), "samples_done")
            dve.wait_ge(sem("z_active"), 1)
            y_all = C[:, 0:XS_T, :]
            done(dve, v.tensor_tensor(y_all, y_all, Z, ALU.mult), "y_gated")
            dve.wait_ge(sem("y_squared"), 1)
            done(dve, v.tensor_tensor(y_all, y_all, over(vec("ssm_g"), T), ALU.mult), "y_ready")
            dve.wait_ge(sem("gates_active"), 1)
            dve.wait_ge(sem("p_mem_out"), 32)
            wait_filled(dve, ("mo", 3))
            for i in range(4):
                for c in range(2):
                    m = 2 * i + c
                    b = wait_filled(dve, ("swa", m))
                    drains(v.tensor_tensor(MERGED[:, m, :], b[:, 0:T], G[:, 8 + m, :], ALU.mult), ("swa", m))
                for c in range(2):
                    m = 2 * i + c
                    b = wait_filled(dve, ("memb", m))
                    drains(v.tensor_tensor(TQ, b[:, 0:T], G[:, 16 + m, :], ALU.mult), ("memb", m))
                    wait_drained(dve, ("memb", m))
                    link(v.tensor_tensor(MERGED[:, m, :], MERGED[:, m, :], TQ, ALU.add))
            dve.wait_ge(sem("rstd"), 23)
            for m in range(8):
                b = wait_filled(dve, ("ssm", m))
                drains(v.tensor_tensor(TQ, b[:, 0:T], RS, ALU.mult), ("ssm", m))
                wait_drained(dve, ("ssm", m))
                link(v.tensor_tensor(TQ, TQ, G[:, m, :], ALU.mult))
                done(dve, v.tensor_tensor(MERGED[:, m, :], MERGED[:, m, :], TQ, ALU.add), "merged")
            dve.wait_ge(sem("x_again"), 16)
            for m in range(8):
                b = wait_filled(dve, ("out", m))
                drains(v.tensor_tensor(X1[:, m, :], X1[:, m, :], b[:, 0:T], ALU.add), ("out", m))
                wait_drained(dve, ("out", m))
            done(dve, v.tensor_scalar(at("ST", 62, 63), vec("gq"), 0.0, None, ALU.mult), "x1_made")
            dve.wait_ge(sem("rstd"), 24)
            link(v.tensor_tensor(HT, X1, each(RS, KT), ALU.mult))
            done(dve, v.tensor_tensor(HT, HT, over(vec("g2"), T), ALU.mult), "h_ready")

            link(v.memset(PLACE, -1.0))

            def r(a_, n, w=None):
                ap = at("S", 1100 + a_, 1100 + a_ + n)
                return ap if w is None else ap.rearrange("p (t e) -> p t e", e=w)

            D4, M2, D8, O8, OG, SEL, LG = (r(0, 12, 4), r(12, 3), r(16, 24, 8), r(40, 24, 8), r(64, 12, 4),
                                           r(80, 96), r(176, 108, ROUTES))
            T12, T24, MX, OH2, ZS = r(300, 12, 4), r(320, 24, 8), r(344, 3), r(350, 24, 8), r(380, 24, 8)
            W1, W2 = r(404, 3), r(407, 3)
            dve.wait_ge(sem("router_in"), 16)
            link(v.memset(r(176, 108), 0.0))
            b = wait_filled(dve, "route")
            for t, rows in enumerate((P, P, BATCH_S)):
                last = v.tensor_tensor(LG[0:rows, t, :], b[0:rows, 64 * t:64 * t + ROUTES],
                                       vec("route_b", rows=rows), ALU.add)
            drains(last, "route")
            wait_drained(dve, "route")

            def first_best(src, width, order, mx, eq, out):
                link(v.tensor_reduce(mx, src, AX.X, ALU.max))
                link(v.tensor_tensor(eq, src, over(mx, width), ALU.is_equal))
                link(v.tensor_tensor(eq, eq, each(tab(order), 3), ALU.mult))
                link(v.tensor_reduce(MX2, eq, AX.X, ALU.max))
                link(v.tensor_tensor(out, eq, over(MX2, width), ALU.is_equal))

            MX2 = r(347, 3)
            first_best(LG[:, :, 0:GROUPS], GROUPS, "first_g", MX, T12, OG)
            link(v.tensor_tensor(D4, LG[:, :, 0:GROUPS], over(MX, GROUPS), ALU.subtract))
            for t in range(3):
                last = v.tensor_tensor(SEL[:, 32 * t:32 * (t + 1)].rearrange("p (g e) -> p g e", g=GROUPS),
                                       LG[:, t, GROUPS:ROUTES].rearrange("p (g e) -> p g e", g=GROUPS),
                                       over(OG[:, t, :], PER_GROUP), ALU.mult)
            link(last)
            link(v.tensor_reduce(ZS, SEL.rearrange("p (t g e) -> p t e g", t=3, g=GROUPS), AX.X, ALU.add))
            first_best(ZS, PER_GROUP, "first_e", MX, T24, O8)
            link(v.tensor_tensor(D8, ZS, over(MX, PER_GROUP), ALU.subtract))
            link(v.scalar_tensor_tensor(D8, O8, -1e30, D8, ALU.mult, ALU.add))
            first_best(D8, PER_GROUP, "first_e", M2, T24, OH2)
            done(dve, v.tensor_scalar(r(410, 3), M2, 1.0, None, ALU.mult), "route_args")
            link(v.tensor_tensor(T24, O8, OH2, ALU.add))
            for t in range(3):
                last = v.tensor_tensor(MASK[:, t, :].rearrange("p (g e) -> p g e", g=GROUPS),
                                       over(OG[:, t, :], PER_GROUP), each(T24[:, t, :], GROUPS), ALU.mult)
            done(dve, last, "chosen")
            dve.wait_ge(sem("route_exp"), 2)
            link(v.tensor_reduce(W1, D4, AX.X, ALU.add))
            link(v.reciprocal(W1, W1))
            link(v.tensor_scalar(W2, M2, 1.0, None, ALU.add))
            link(v.reciprocal(W2, W2))
            link(v.tensor_tensor(W1, W1, W2, ALU.mult))
            link(v.tensor_tensor(W2, W1, M2, ALU.mult))
            link(v.tensor_tensor(O8, O8, over(W1, PER_GROUP), ALU.mult))
            link(v.tensor_tensor(OH2, OH2, over(W2, PER_GROUP), ALU.mult))
            link(v.tensor_tensor(O8, O8, OH2, ALU.add))
            for t in range(3):
                last = v.tensor_tensor(COMB[:, t, :].rearrange("p (g e) -> p g e", g=GROUPS),
                                       over(OG[:, t, :], PER_GROUP), each(O8[:, t, :], GROUPS), ALU.mult)
            done(dve, last, "comb")
            b = wait_filled(dve, "count")
            link(v.tensor_reduce(MX2[:, 0:1], b[:, 96:128], AX.X, ALU.max))
            v.tensor_copy(worst[:, :], MX2[:, 0:1]).then_inc(sem("worst_ready"), 1)
            b3 = b[:, 0:64].rearrange("p (t e) -> p t e", t=2)
            link(v.tensor_tensor(PLACE[:, 0:2, :], b3, MASK[:, 0:2, :], ALU.mult))
            drains(v.tensor_tensor(PLACE[0:8, 2, :], b[0:8, 64:96], MASK[0:8, 2, :], ALU.mult), "count")
            wait_drained(dve, "count")
            link(v.tensor_scalar(PLACE[:, 0:2, :], PLACE[:, 0:2, :], -1.0, None, ALU.add))
            link(v.tensor_scalar(PLACE[0:8, 2, :], PLACE[0:8, 2, :], -1.0, None, ALU.add))

            dve.sem_inc(sem("tile_added"), 2)

            def experts(rounds):
                def body(buf, q, n):
                    mine = PLACE[:, :, bass.ds(q * QUAD, QUAD)]
                    slots = tab("slots").unsqueeze(1).unsqueeze(1).to_broadcast([P, 3, QUAD, SLOTS])
                    v.tensor_tensor(ONE, mine.unsqueeze(3).to_broadcast([P, 3, QUAD, SLOTS]), slots, ALU.is_equal
                                    ).then_inc(sem("slots_found"), 1)
                    dve.wait_ge(sem("slots_found"), n + 1)
                    v.tensor_tensor(ONEW, ONE,
                                    COMB[:, :, bass.ds(q * QUAD, QUAD)].unsqueeze(3).to_broadcast([P, 3, QUAD, SLOTS]),
                                    ALU.mult).then_inc(sem("slots_ready"), 1)
                    if rounds > 1:
                        v.tensor_scalar(mine, mine, -float(SLOTS), None, ALU.add).then_inc(sem("place_moved"), 1)
                        dve.wait_ge(sem("place_moved"), n + 1)
                    dve.wait_ge(sem("gathered1"), n + 1)
                    v.tensor_copy(HG[:, 4:8, :].rearrange("p k s -> p (k s)"), psum[5][:, :]
                                  ).then_inc(sem("gathered_stored"), 1)
                    dve.wait_ge(sem("back_filled"), n + 1)
                    v.tensor_copy(BACK, psum[6][:, 0:T]).then_inc(sem("back_ready"), 1)
                    dve.wait_ge(sem("silu"), n + 1)
                    dve.wait_ge(sem("up_filled"), n + 1)
                    v.tensor_tensor(ACTV, psum[1][:, 0:D_FF], SG, ALU.mult).then_inc(sem("act_ready"), 1)
                    dve.wait_ge(sem("act_turned"), n + 1)
                    v.tensor_copy(ACTT.rearrange("p f s -> p (f s)"), psum[4][:, 0:D_FF]
                                  ).then_inc(sem("actT_ready"), 1)
                    dve.wait_ge(sem("down_filled1"), n + 1)
                    v.tensor_copy(DOWNED[:, 512:1024], psum[3][:, :]).then_inc(sem("down_stored1"), 1)
                    for m in range(KT):
                        dve.wait_ge(sem("tile_filled"), n * KT + (m + 1))
                        v.tensor_tensor(X1[:, m, :], X1[:, m, :], psum[6 + m % 2][:, 0:T], ALU.add
                                        ).then_inc(sem("tile_added"), 1)

                steps(dve, rounds, body)

            by_rounds(dve, experts)


def _tables():
    t = np.zeros((P, TAB_W), np.float32)

    def put(name, a):
        o, n = TAB[name]
        t[:, o:o + n] = a

    s, u = np.arange(P)[:, None], np.arange(P)[None, :]
    causal = (s <= u).astype(np.float32)
    put("ident", np.eye(P, dtype=np.float32))
    put("causal", np.concatenate([causal, np.ones((P, P), np.float32), causal], 1))
    rot = np.zeros((P, P), np.float32)
    for m in range(P):
        if m % 64 < 32:
            rot[m + 32, m] = -1.0
        else:
            rot[m - 32, m] = 1.0
    put("rot", rot)
    put("half_ones", (s // 64 == u // 64).astype(np.float32))
    put("ones", np.ones((P, P), np.float32))
    put("window", np.concatenate([np.where(u <= s, 0, -1e30), np.where(u > s, 0, -1e30)], 1))
    inv = np.float32(10000.0) ** (-np.arange(32, dtype=np.float32) / np.float32(32))
    pos = np.concatenate([np.arange(SEQ), np.full(BATCH_S, PAST_LEN)]).astype(np.float32)
    ang = (pos[None, :] * inv[:, None]).astype(np.float32)
    put("cos", np.tile(np.cos(ang), (4, 1)))
    put("sin", np.tile(np.sin(ang), (4, 1)))
    put("first_g", np.arange(GROUPS, 0, -1)[None, :])
    put("first_e", np.arange(PER_GROUP, 0, -1)[None, :])
    put("slots", np.arange(SLOTS)[None, :])
    return t


def _layout(inp):
    c = np.ascontiguousarray

    def feat(a):
        return a.reshape(-1, P).T

    def rows(a):
        return np.broadcast_to(a.reshape(1, -1), (P, a.size))

    i = {k: np.asarray(a) for k, a in inp.items()}
    xt = np.concatenate([i["x_prompt"][0], i["x_sample"][:, 0]], 0)
    sink = i["att_sink"][0]
    sink_col = np.tile(sink.reshape(KV, 2, 2).transpose(0, 2, 1).reshape(-1), BATCH_S)[:, None]
    parts = {
        "g1": feat(i["norm1_g"][0]), "gmem": feat(i["mem_norm_g"][0]),
        "conv_w": np.concatenate([feat(i["ssm_conv_w"][0, k]) for k in range(CONV_TAPS)], 1),
        "conv_b": feat(i["ssm_conv_b"][0]), "ssm_g": feat(i["ssm_norm_g"][0]),
        "ssm_d": feat(np.repeat(i["ssm_d"][0], HEADDIM)),
        "gq": np.tile(i["att_q_norm_g"][0], 2)[:, None], "gk": np.tile(i["att_k_norm_g"][0], 2)[:, None],
        "gmq": feat(i["mem_q_norm_g"][0]), "gmk": feat(i["mem_k_norm_g"][0]), "g2": feat(i["norm2_g"][0]),
        "sink_col": sink_col, "dt_bias": rows(i["ssm_dt_bias"][0]), "a_log": rows(i["ssm_a_log"][0]),
        "route_b": rows(np.concatenate([i["b_router_group"][0], i["b_router_expert"][0]])), "sink": rows(sink),
    }

    def tiled(a):
        return c(a.T.reshape(-1, P, a.shape[0]).transpose(1, 0, 2))

    kt = i["cache_swa_k"][0].transpose(3, 2, 0, 1).reshape(HD, KV, 2, 4, P)
    kt = np.concatenate([kt, kt], 0).transpose(2, 0, 1, 3, 4)
    return {
        "tables": _tables(),
        "vectors": c(np.concatenate([parts[n] for n in VEC], 1)),
        "xT": tiled(xt),
        "memT": tiled(i["mem_prompt"][0]),
        "histT": c(i["state_conv"][0].transpose(2, 0, 1).reshape(CONV_T, P, BATCH_S, 3).transpose(1, 0, 2, 3)),
        "w_in": i["w_in"][0], "w_mem_kv": i["w_mem_kv"][0], "w_br_ssm": i["w_br_ssm"][0],
        "w_br_swa": i["w_br_swa"][0], "w_br_mem": i["w_br_mem"][0], "w_out": i["w_out"][0],
        "w_router": c(np.concatenate([i["w_router_group"][0], i["w_router_expert"][0]], 1)),
        "w_exp_gate": i["w_exp_gate"][0], "w_exp_up": i["w_exp_up"][0], "w_exp_down": i["w_exp_down"][0],
        "state_ssm": i["state_ssm"][0].reshape(BATCH_S, D_INNER, STATE),
        "mem_kT": c(i["cache_mem_k"][0].reshape(BATCH_S, MEM, MEM_H, 2, P).transpose(0, 4, 2, 3, 1)
                    .reshape(BATCH_S, P, 2048)),
        "mem_v": c(i["cache_mem_v"][0].reshape(BATCH_S, 2, P, D_MODEL).transpose(0, 2, 1, 3).reshape(BATCH_S, P, 2048)),
        "swa_kT": c(kt.reshape(2, P, 2048)),
        "swa_v": c(i["cache_swa_v"][0].reshape(BATCH_S, P, KV * HD).transpose(1, 0, 2).reshape(P, 2048)),
    }


_OUTS = {
    "yT": (P, KT, T), "p_mem_kT": (P, 8, MEM), "p_mem_v": (P, 2, D_MODEL), "p_swa_v": (P, KV * HD),
    "newconvT": (P, CONV_T, 27), "p_swa_kT": (64, KV, P), "p_ssm": (D_INNER, STATE),
    "s_ssm": (BATCH_S, D_INNER, STATE), "s_swa_kT": (2, 64, 2048), "s_swa_v": (P, 2048),
}


def _results(o):
    c = np.ascontiguousarray
    y = o["yT"].transpose(1, 0, 2).reshape(D_MODEL, T).T
    conv = o["newconvT"].transpose(1, 0, 2).reshape(CONV_CH, 27)
    roll = list(range(1, P)) + [0]
    sk = o["s_swa_kT"].reshape(2, HD, KV, 4, P).transpose(0, 3, 4, 2, 1).reshape(BATCH_S, P, KV, HD)[:, roll]
    sv = o["s_swa_v"].reshape(P, BATCH_S, KV, HD).transpose(1, 0, 2, 3)[:, roll]
    return (
        c(y[:SEQ])[None], c(y[SEQ:])[:, None],
        c(conv[:, 24:27].T)[None, None],
        o["p_ssm"].reshape(1, 1, SSM_HEADS, HEADDIM, STATE),
        c(o["p_swa_kT"].transpose(2, 1, 0))[None, None],
        o["p_swa_v"].reshape(1, 1, P, KV, HD),
        c(o["p_mem_kT"].transpose(2, 1, 0).reshape(MEM, MEM_H, MEM_D))[None, None],
        c(o["p_mem_v"].transpose(1, 0, 2).reshape(MEM, MEM_H, MEM_D))[None, None],
        c(conv[:, 0:24].reshape(CONV_CH, BATCH_S, 3).transpose(1, 2, 0))[None],
        o["s_ssm"].reshape(1, BATCH_S, SSM_HEADS, HEADDIM, STATE),
        c(sk)[None], c(sv)[None],
    )


def kernel(**inputs):
    import concourse.bacc as bacc
    from concourse.bass_utils import run_bass_kernel_spmd

    nc = bacc.Bacc("TRN2", target_bir_lowering=False, num_devices=1)
    arrays = _layout(inputs)
    ins = {n: nc.dram_tensor(f"in_{n}", a.shape, mybir.dt.from_np(a.dtype), kind="ExternalInput").ap()
           for n, a in arrays.items()}
    outs = {n: nc.dram_tensor(f"out_{n}", s, F32, kind="ExternalOutput").ap() for n, s in _OUTS.items()}
    build_program(nc, ins, outs)
    got = run_bass_kernel_spmd(nc, [{f"in_{n}": a for n, a in arrays.items()}], core_ids=[0])
    return _results({n: got.results[0][f"out_{n}"] for n in _OUTS})
```

```python
from contextlib import ExitStack

import numpy as np

import concourse.bass as bass
from concourse import mybir

P = 128
D_MODEL = 1024
SEQ = 256
BATCH_S = 8
PAST_LEN = 2048
T = SEQ + BATCH_S
KT = D_MODEL // P
D_INNER = 2048
HEADDIM = 64
SSM_HEADS = 32
SSM_GROUPS = 4
STATE = 128
CONV_TAPS = 4
CONV_CH = D_INNER + 2 * SSM_GROUPS * STATE
CONV_T = CONV_CH // P
XS_T = D_INNER // P
KV = 4
HD = 64
WINDOW = 128
MEM = 256
MEM_H = 4
MEM_D = 256
GROUPS = 4
PER_GROUP = 8
EXPERTS = GROUPS * PER_GROUP
D_FF = 256
FF_T = D_FF // P
EPS = 1e-6
OFF_GATE, OFF_Z = 0, 3 * D_MODEL
OFF_XBC = OFF_Z + D_INNER
OFF_DT = OFF_XBC + CONV_CH
OFF_Q = OFF_DT + SSM_HEADS
OFF_K = OFF_Q + 1024
OFF_V = OFF_K + KV * HD
OFF_MQ = OFF_V + KV * HD
ROUTES = GROUPS + EXPERTS

CW = 256
CHUNK = KT * CW
WBUFS = 3
SLOTS = 32
QUAD = P // SLOTS
QUADS = EXPERTS // QUAD
ALL_ROUNDS = -(-T // SLOTS)
PIECE = KT * D_FF

ALU = mybir.AluOpType
ACT = mybir.ActivationFunctionType
AX = mybir.AxisListType
F32 = mybir.dt.float32
F32R = mybir.dt.float32r

VEC = {}
_at = 0
for _name, _n in (("g1", KT), ("gmem", KT), ("conv_w", CONV_TAPS * CONV_T), ("conv_b", CONV_T), ("ssm_g", XS_T),
                  ("ssm_d", XS_T), ("gq", 1), ("gk", 1), ("gmq", 2), ("gmk", 2), ("g2", KT), ("sink_col", 1),
                  ("dt_bias", SSM_HEADS), ("a_log", SSM_HEADS), ("route_b", ROUTES), ("sink", 16)):
    VEC[_name] = (_at, _n)
    _at += _n
VEC_W = _at
TAB = {}
_at = 0
for _name, _n in (("ident", P), ("causal", 3 * P), ("rot", P), ("half_ones", P), ("ones", P), ("window", 2 * P),
                  ("cos", T), ("sin", T), ("first_g", GROUPS), ("first_e", PER_GROUP), ("slots", SLOTS),
                  ("eye8", 64), ("eye8_half", 128)):
    TAB[_name] = (_at, _n)
    _at += _n
TAB_W = _at

MAP = {}


def _place(*names):
    at = 0
    for name, words in names:
        MAP[name] = (at, words)
        at += words
    assert at <= 55200, at


_place(
    ("X", CONV_T * T),
    ("C", CONV_T * T),
    ("Q", 8 * T),
    ("KD", KV * T),
    ("MQ", 8 * T),
    ("VT", 3 * KV * HD),
    ("XD", 2 * D_INNER),
    ("pad", 32),
    ("Z", XS_T * T),
    ("G", 24 * T),
    ("SQ", 512 + 1024 + MEM),
    ("MK", 8 * MEM),
    ("MV", 2 * D_MODEL),
    ("S", 3072),
    ("tab", TAB_W), ("vec", VEC_W),
    ("DT", 3 * SSM_HEADS), ("DTA", 3 * SSM_HEADS), ("AC", 2 * SSM_HEADS), ("WE", 2 * SSM_HEADS),
    ("BT", 2 * 4 * STATE), ("RS", T), ("TQ", T), ("EX", 2 * XS_T * BATCH_S), ("XS", XS_T * BATCH_S),
    ("ST", 64),
    ("HN", KT * T),
    ("W", WBUFS * CHUNK),
)


def build_program(nc, ins, outs):
    ctx = ExitStack()
    with ctx:
        top = MAP["HN"][0]
        named = {}

        def under_name(off, words, dtype=F32R):
            key = (off, words, dtype)
            if key not in named:
                with ExitStack() as until_named:
                    name = f"at{off}_{words}_{'r' if dtype == F32R else 'f'}"
                    if off:
                        until_named.enter_context(nc.sbuf_tensor(name + "_ahead", [P, off], F32))
                    named[key] = until_named.enter_context(nc.sbuf_tensor(name, [P, words], dtype))
            return named[key]

        at_s, at_g, at_c, at_xd, at_x, at_z = (MAP[n][0] for n in ("S", "G", "C", "XD", "X", "Z"))
        x_high, x_low = under_name(at_z, KT * T), under_name(at_z + KT * T, KT * T)
        m_high, m_low = under_name(at_xd, KT * MEM), under_name(at_xd + KT * MEM, KT * MEM)
        twin_high = under_name(at_g + 5928, 2 * KT * P)
        twin_low = under_name(at_s + 1024, 2 * KT * P)
        twins_c = under_name(at_c + 2112, 4 * KT * P)
        for off in (at_xd, at_xd + 1024, at_xd + 2048, at_xd + 3072, at_x + 5120, at_g):
            under_name(off, KT * P)
        M = ctx.enter_context(nc.sbuf_tensor("M", [P, top], F32))
        apart = {name: ctx.enter_context(nc.sbuf_tensor(name, [P, MAP[name][1]], F32)) for name in ("HN", "W")}
        psum = [ctx.enter_context(nc.psum_tensor(f"bank{i}", [P, 512], F32)) for i in range(8)]
        filled = [ctx.enter_context(nc.semaphore(f"filled{i}")) for i in range(8)]
        drained = [ctx.enter_context(nc.semaphore(f"drained{i}")) for i in range(8)]
        sems, counts = {}, {}

        def sem(name):
            if name not in sems:
                sems[name] = ctx.enter_context(nc.semaphore(name))
                counts[name] = 0
            return sems[name]

        def at(name, a=0, b=None, rows=P):
            off, n = MAP[name]
            b = n if b is None else b
            if name in apart:
                return apart[name][0:rows, a:b]
            return M[0:rows, off + a:off + b]

        def tiles(name, w, a=0, b=None, rows=P):
            return at(name, a, b, rows).rearrange("p (j w) -> p j w", w=w)

        def tab(name, rows=P):
            a, n = TAB[name]
            return at("tab", a, a + n, rows)

        def vec(name, a=0, b=None, rows=P):
            off, n = VEC[name]
            b = n if b is None else b
            return at("vec", off + a, off + b, rows)

        def over(ap, n):
            return ap.unsqueeze(2).to_broadcast([ap.shape[0], ap.shape[1], n])

        def each(ap, n):
            return ap.unsqueeze(1).to_broadcast([ap.shape[0], n, ap.shape[1]])

        def done(eng, instruction, name):
            s = sem(name)
            counts[name] += 1
            instruction.then_inc(s, 1)
            eng.wait_ge(s, counts[name])

        HN, X, C, Z = tiles("HN", T), tiles("X", T), tiles("C", T), tiles("Z", T)
        Q, KD, MQ, G = tiles("Q", T), tiles("KD", T), tiles("MQ", T), tiles("G", T)
        MK, MV, VT = tiles("MK", MEM), tiles("MV", D_MODEL), tiles("VT", KV * HD)
        XD = tiles("XD", D_INNER)
        DT, DTA, AC, WE = (tiles(n, SSM_HEADS) for n in ("DT", "DTA", "AC", "WE"))
        BT = tiles("BT", 4 * STATE)
        RS, TQ = at("RS"), at("TQ")
        EX = at("EX").rearrange("p (a j b) -> p a j b", a=2, b=BATCH_S)
        XS = tiles("XS", BATCH_S)
        ident = tab("ident")
        ones = tab("ones")
        XT, XSQ = tiles("X", T, 0, 8 * T), tiles("X", T, 8 * T, 16 * T)
        MT, MSQ = tiles("G", MEM, 0, 2048), tiles("G", MEM, 2048, 4096)
        MN = tiles("HN", MEM, 0, KT * MEM)

        def by_tiles(tensor, w):
            return tensor[:, :].rearrange("p (j w) -> p j w", w=w)

        HN_SPLIT = by_tiles(x_high, T), by_tiles(x_low, T)
        MN_SPLIT = by_tiles(m_high, MEM), by_tiles(m_low, MEM)
        def low_part(eng, low, x, high):
            return eng.tensor_tensor(low, x, high.bitcast(F32), ALU.subtract)

        RSM = tiles("G", MEM, 4096, 5120)
        NEWC = at("G", 0, 27 * CONV_T).rearrange("p (j k) -> p j k", k=27)
        HIST = at("G", 648, 648 + 24 * CONV_T).rearrange("p (j b k) -> p j b k", b=BATCH_S, k=3)
        CB = tiles("G", 3 * P, 1224, 2760)
        KSQ, QSQ = tiles("G", T, 2760, 3816), tiles("G", T, 3816, 5928)
        DTX, DAX = at("XD", 0, 2048, 8), at("XD", 2048, 4096, 8)
        SBC = at("X", 4096, 5120, 8)
        HS = [at("X", 2048 * i, 2048 * (i + 1)).rearrange("p (j n) -> p j n", n=STATE) for i in range(2)]
        T2 = at("S", 0, 2048)
        BB = at("S", 2048, 3072)
        SM, PTs = at("XD", 0, 1024), at("XD", 1024, 2048)
        RING = [at("C", 4224, 6272), at("XD", 2048, 4096)]
        EIGHTS = at("SQ", 0, 512).rearrange("p (t b c) -> p t b c", b=BATCH_S, c=BATCH_S)
        FOURS = at("SQ", 512, 1536).rearrange("p (g b c) -> p g b c", g=KV, b=BATCH_S)
        ZEROS = at("SQ", 1536, 1536 + MEM)
        SSM = at("X", 5120, 5504)

        X1 = HN
        mk_at = MAP["MK"][0]
        MERGED = M[:, mk_at:mk_at + 8 * T].rearrange("p (j w) -> p j w", w=T)
        X1SQ = M[:, mk_at + 8 * T:mk_at + 12 * T].rearrange("p (j w) -> p j w", w=T)
        X1G = M[:, mk_at + 12 * T:mk_at + 16 * T].rearrange("p (j w) -> p j w", w=T)
        X1GS = tiles("S", BATCH_S, 160, 224)
        SSQ, RTOK = at("S", 224, 227), at("S", 227, 230)
        WR = at("S", 256, 256 + KT * ROUTES).rearrange("p (k n) -> p k n", n=ROUTES)
        COMB = at("S", 600, 600 + 3 * (EXPERTS + QUAD)).rearrange("p (t e) -> p t e", e=EXPERTS + QUAD)
        MASK = at("S", 720, 816).rearrange("p (t e) -> p t e", e=EXPERTS)
        PLACE = at("S", 840, 840 + 3 * (EXPERTS + QUAD)).rearrange("p (t e) -> p t e", e=EXPERTS + QUAD)
        ONE, *ONEW = (at("S", a, a + 3 * P).rearrange("p (t j s) -> p t j s", t=3, s=SLOTS) for a in (1600, 2000, 2680))
        BACK = at("S", 2400, 2400 + T)
        HTOK = tiles("W", D_MODEL, 0, 3 * D_MODEL)
        HG = tiles("W", P, 3072, 4096)
        DOWNED = at("W", 4096, 5120)
        SG, ACTV = at("W", 5120, 5376), at("W", 5376, 5632)
        ACTT = tiles("W", P, 5632, 5888)
        worst = ctx.enter_context(nc.sbuf_tensor("worst", [P, 1], mybir.dt.int32))
        assert mk_at + 16 * T <= MAP["S"][0] + 160

        y_end = MAP["C"][0] + XS_T * T
        free1 = [y_end, y_end + 4 * PIECE, y_end + 5 * PIECE, MAP["X"][0]]
        free2 = [MAP["X"][0] + PIECE, MAP["X"][0] + 2 * PIECE, y_end + PIECE, y_end + 2 * PIECE]
        free3 = [y_end + 3 * PIECE, MAP["Z"][0], MAP["Z"][0] + PIECE, MAP["C"][0]]
        late = MAP["G"][0] + 3 * PIECE
        free5 = [MAP["DT"][0], late, late + PIECE, late + 2 * PIECE]
        assert late + 3 * PIECE <= MAP["S"][0] + 160 and MAP["DT"][0] + PIECE <= MAP["ST"][0]
        free4 = [MAP["C"][0] + PIECE, MAP["G"][0], MAP["G"][0] + PIECE, MAP["G"][0] + 2 * PIECE]
        assert y_end + 6 * PIECE <= MAP["Z"][0]

        def piece(kind, q, j):
            o = {"gate": (free1, free4)[q % 2], "up": (free2, free5)[q % 2], "down": free3}[kind][j]
            return M[:, o:o + PIECE].rearrange("p (k n) -> p k n", n=D_MODEL if kind == "down" else D_FF)

        w_in, w_mem = ins["w_in"], ins["w_mem_kv"]
        chunks = []

        def cols(w, c0, n=CW, k0=0):
            return w[k0:k0 + D_MODEL, c0:c0 + n].rearrange("(k p) n -> p k n", p=P)

        for i in range(8):
            chunks.append((("mem", i), [(cols(w_mem, CW * i), 0, CW)]))
        for i in range(12):
            if i == 11:
                chunks.append((("dt", 0), [(cols(w_in, OFF_DT, SSM_HEADS), 0, SSM_HEADS)]))
            chunks.append((("xbc", i), [(cols(w_in, OFF_XBC + CW * i), 0, CW)]))
        chunks.append((("kd", 1), [(cols(w_in, OFF_K), 0, CW)]))
        chunks.append((("v", 0), [(cols(w_in, OFF_V), 0, CW)]))
        for i in range(4):
            chunks.append((("q", i), [(cols(w_in, OFF_Q + CW * i), 0, CW)]))
        for i in range(4):
            chunks.append((("mq", i), [(cols(w_in, OFF_MQ + CW * i), 0, CW)]))
        for i in range(8):
            chunks.append((("z", i), [(cols(w_in, OFF_Z + CW * i), 0, CW)]))
        for i in range(12):
            chunks.append((("gate", i), [(cols(w_in, OFF_GATE + CW * i), 0, CW)]))
        for i in range(4):
            chunks.append((("swa", i), [(cols(ins["w_br_swa"], CW * i), 0, CW)]))
            chunks.append((("memb", i), [(cols(ins["w_br_mem"], CW * i), 0, CW)]))
        for i in range(4):
            chunks.append((("ssma", i), [(cols(ins["w_br_ssm"], CW * i), 0, CW)]))
            chunks.append((("ssmb", i), [(cols(ins["w_br_ssm"], CW * i, CW, D_MODEL), 0, CW)]))
        for i in range(4):
            chunks.append((("out", i), [(cols(ins["w_out"], CW * i), 0, CW)]))
        number = {name: n for n, (name, _) in enumerate(chunks)}
        number["kd", 0] = number["kd", 1]
        chunk_in = [sem(f"chunk_in{i}") for i in range(WBUFS)]
        chunk_value, seen = {}, [0] * WBUFS
        for n, (_, parts) in enumerate(chunks):
            seen[n % WBUFS] += 16 * len(parts)
            chunk_value[n] = seen[n % WBUFS]
        split_use = {}

        def chunk(n):
            return tiles("W", CW, CHUNK * (n % WBUFS), CHUNK * (n % WBUFS + 1))

        split_number = {}
        for name, _ in chunks:
            for part in ((("kd", 0), name) if name == ("kd", 1) else (name,)):
                if part[0] in ("mem", "xbc", "kd", "q", "mq"):
                    split_number[part] = len(split_number)
        SPLIT = list(split_number)
        DVE_LOWS = 8

        stay = [(at_g + 5928, at_s + 1024), (at_g + 5928 + 1024, at_s + 2048)]
        assert stay[1][0] + 1024 <= MAP["SQ"][0] + MAP["SQ"][1]
        part_places, held_before, last_at = [], [], {}
        for half in range(2 * len(SPLIT)):
            name = SPLIT[half // 2]
            if name[0] == "mem" or (name[0] == "xbc" and name[1] < 6):
                pairs = stay + [(at_c + 2112, at_c + 3136), (at_c + 4160, at_c + 5184)]
            elif name[0] in ("xbc", "kd"):
                pairs = stay + [(at_xd, at_xd + 1024), (at_xd + 2048, at_xd + 3072)]
            else:
                pairs = stay + [(at_x + 5120, at_g)]
            pair = pairs[(half - 2 * split_number["q", 0]) % len(pairs)]
            part_places.append(pair)
            held_before.append(last_at.get(pair))
            last_at[pair] = half

        def part_at(off):
            for tensor, start in ((twin_high, at_g + 5928), (twin_low, at_s + 1024)):
                if start <= off < start + 2 * KT * P:
                    return tensor, off - start
            if at_c + 2112 <= off < at_c + 2112 + 4 * KT * P:
                return twins_c, off - at_c - 2112
            return named[off, KT * P, F32R], 0

        def w_whole(name):
            out = []
            for first, second in zip(*(part_places[2 * split_number[name] + c] for c in range(2))):
                tensor, o = part_at(first)
                step = second - first
                out.append(tensor[:, :].rearrange("p (i w) -> p i w", w=KT * P)[:, o // (KT * P)::step // (KT * P), :])
            return out

        def w_split(name, c):
            out = []
            for off in part_places[2 * split_number[name] + c]:
                tensor, o = part_at(off)
                out.append(tensor[:, o:o + KT * P].rearrange("p (k n) -> p k n", n=P))
            return out

        def low_made(m, c):
            if m < DVE_LOWS and c == 1:
                return sem("lows_by_vector"), m + 1
            return sem(f"low_ready{c}"), m + 1 - DVE_LOWS * c

        def raw_half(name, c):
            o = CHUNK * (number[name] % WBUFS)
            raw = apart["W"][:, o:o + CHUNK].rearrange("p (k n) -> p k n", n=CW)
            if name[0] == "kd":
                c0 = HD * (2 * name[1] + c)
                return raw[:, :, c0:c0 + HD].unsqueeze(2).to_broadcast([P, KT, 2, HD])
            return raw[:, :, P * c:P * (c + 1)]

        def like_raw(part, name):
            return part.rearrange("p k (t n) -> p k t n", t=2) if name[0] == "kd" else part

        place, uses, last_use = {}, [0] * 8, {}
        gate_in = [sem(f"gate_in{b}") for b in range(2)]
        up_in = [sem(f"up_in{b}") for b in range(2)]
        down_in = sem("down_in")

        def by_rounds(eng, experts):
            eng.wait_ge(sem("worst_ready"), 1)
            fullest = eng.value_load(worst[0:1, 0:1])
            with eng.If(fullest <= SLOTS):
                experts(1)
            with eng.Else():
                experts(ALL_ROUNDS)

        def steps(eng, rounds, body):
            with eng.Fori(0, QUADS // 2) as it:
                for b in range(2):
                    q = it * 2 + b
                    if rounds == 1:
                        body(b, q, q)
                    else:
                        with eng.Fori(0, rounds) as r:
                            body(b, q, q * rounds + r)

        def wait_filled(eng, name):
            bank, n = place[name]
            eng.wait_ge(filled[bank], n + 1)
            return psum[bank]

        def wait_drained(eng, name):
            bank, n = place[name]
            eng.wait_ge(drained[bank], n + 1)

        def drains(instruction, name):
            instruction.then_inc(drained[place[name][0]], 1)

        block = ctx.enter_context(nc.Block())

        @block.tensor
        def _(pe):
            ring, ring_banks = [0], [3]

            def opened(name, bank):
                n = uses[bank]
                uses[bank] += 1
                place[name] = (bank, n)
                if n:
                    pe.wait_ge(drained[bank], n)
                return psum[bank]

            def full(mm, name):
                mm.then_inc(filled[place[name][0]], 1)

            def next_proj(name):
                ring[0] += 1
                return opened(name, (ring[0] - 1) % ring_banks[0])

            def arrive(name):
                n = number[name]
                pe.wait_ge(chunk_in[n % WBUFS], chunk_value[n])
                return chunk(n)

            def feature_tile(name, w, c, x, n, chunk_name):
                bank = next_proj(name)
                for k in range(KT):
                    mm = pe.matmul(bank[:, 0:n], w[:, k, P * c:P * (c + 1)], x[:, k, 0:n],
                                   start=(k == 0), stop=(k == KT - 1))
                full(mm, name)
                last_use[chunk_name] = name

            def split_tile(name, c, x, n, chunk_name):
                pe.wait_ge(*low_made(split_number[chunk_name], c))
                bank = next_proj(name)
                high, low = w_split(chunk_name, c)
                for k in range(KT):
                    for i, (w, x_) in enumerate(((high, x[0]), (high, x[1]), (low, x[0]))):
                        mm = pe.matmul(bank[:, 0:n], w[:, k, :], x_[:, k, 0:n],
                                       start=(k + i == 0), stop=(k == KT - 1 and i == 2))
                full(mm, name)
                split_use[chunk_name, c] = name

            def squares(name, bank, sq, first, n_tiles, n, weights=None):
                b = opened(name, bank)
                for k in range(n_tiles):
                    mm = pe.matmul(b[:, 0:n], ones if weights is None else weights, sq[:, first + k, 0:n],
                                   start=(k == 0), stop=(k == n_tiles - 1))
                full(mm, name)

            pe.wait_ge(sem("tables_in"), 32)
            pe.wait_ge(sem("mem_squared"), 1)
            squares("ss_mem", 4, MSQ, 0, KT, MEM)
            pe.wait_ge(sem("x_squared"), 1)
            squares("ss_x", 3, XSQ, 0, KT, T)

            pe.wait_ge(sem("mem_normed"), 1)
            for i in range(4):
                for c in range(2):
                    split_tile(("mk", 2 * i + c), c, MN_SPLIT, MEM, ("mem", i))
            for i in range(4):
                whole = w_whole(("mem", 4 + i))
                for c in range(2):
                    pe.wait_ge(*low_made(split_number["mem", 4 + i], c))
                for mt in range(2):
                    name = ("mv", i, mt)
                    b = next_proj(name)
                    for k in range(KT):
                        for part, (x_, w) in enumerate(((0, 0), (0, 1), (1, 0))):
                            mm = pe.matmul(b[:, 0:CW], MN_SPLIT[x_][:, k, P * mt:P * (mt + 1)],
                                           whole[w][:, :, P * k:P * (k + 1)],
                                           start=(k + part == 0), stop=(k == KT - 1 and part == 2))
                    full(mm, name)
                    for c in range(2):
                        split_use[("mem", 4 + i), c] = name
            pe.wait_ge(sem("mk_squared"), 1)
            for h in range(MEM_H):
                squares(("ss_mk", h), 3 + h, MSQ, 2 * h, 2, MEM)

            pe.wait_ge(sem("x_normed"), 1)
            for i in range(12):
                for c in range(2):
                    split_tile(("xbc", 2 * i + c), c, HN_SPLIT, T, ("xbc", i))
            arrive(("dt", 0))
            off = CHUNK * (number[("dt", 0)] % WBUFS)
            w = at("W", off, off + KT * SSM_HEADS).rearrange("p (k n) -> p k n", n=SSM_HEADS)
            b = next_proj("dt")
            for t, rows in enumerate((P, P, BATCH_S)):
                for k in range(KT):
                    mm = pe.matmul(b[0:rows, 32 * t:32 * t + 32], HN[:, k, P * t:P * t + rows], w[:, k, :],
                                   start=(k == 0), stop=(k == KT - 1))
            full(mm, "dt")
            last_use[("dt", 0)] = "dt"
            for i in range(2):
                for c in range(2):
                    split_tile(("kd", 2 * i + c), c, HN_SPLIT, T, ("kd", i))
            w = arrive(("v", 0))
            for t, rows in enumerate((P, P, BATCH_S)):
                b = next_proj(("v", t))
                for k in range(KT):
                    mm = pe.matmul(b[0:rows, 0:CW], HN[:, k, P * t:P * t + rows], w[:, k, :],
                                   start=(k == 0), stop=(k == KT - 1))
                full(mm, ("v", t))
                last_use[("v", 0)] = ("v", t)
            for i in range(4):
                for c in range(2):
                    split_tile(("q", 2 * i + c), c, HN_SPLIT, T, ("q", i))
                if i == 1:
                    pe.wait_ge(sem("dta"), 1)
                    b = opened("acum", 3)
                    pe.matmul(b[:, 0:32], tab("causal")[:, 0:P], DTA[:, 0, :], start=True, stop=True)
                    pe.matmul(b[:, 32:64], ones, DTA[:, 0, :], start=True, stop=False)
                    pe.matmul(b[:, 32:64], tab("causal")[:, 0:P], DTA[:, 1, :], start=False, stop=True)
                    pe.matmul(b[:, 64:96], ones, DTA[:, 0, :], start=True, stop=False)
                    full(pe.matmul(b[:, 64:96], ones, DTA[:, 1, :], start=False, stop=True), "acum")
                    pe.wait_ge(sem("dt_expanded"), 1)
                    b = opened("ex", 4)
                    for a, src in enumerate((DTX, DAX)):
                        for j in range(XS_T):
                            c0 = (a * XS_T + j) * BATCH_S
                            mm = pe.matmul(b[:, c0:c0 + BATCH_S], src[:, P * j:P * (j + 1)], ident[0:8, 0:8],
                                           start=True, stop=True)
                    full(mm, "ex")

            for i in range(4):
                for c in range(2):
                    split_tile(("mq", 2 * i + c), c, HN_SPLIT, T, ("mq", i))
                    j = 2 * i + c
                    if j == 0:
                        pe.wait_ge(sem("conv_active"), 3)
                    if j < 4:
                        for half in range(2):
                            b = opened(("xtok", half, j), 3 + half)
                            for q in range(4):
                                mm = pe.transpose(b[:, P * q:P * (q + 1)], C[:, 4 * j + q, P * half:P * (half + 1)],
                                                  ident)
                            full(mm, ("xtok", half, j))
                    if j == 4:
                        for half in range(2):
                            b = opened(("btok", half), 5 + half)
                            for q in range(4):
                                mm = pe.transpose(b[:, P * q:P * (q + 1)], C[:, XS_T + q, P * half:P * (half + 1)],
                                                  ident)
                            full(mm, ("btok", half))
                        for a in range(2):
                            b = opened(("sbc", a), 3 + a)
                            for q in range(4):
                                mm = pe.transpose(b[0:8, P * q:P * (q + 1)], C[:, XS_T + 4 * a + q, SEQ:T], ident)
                            full(mm, ("sbc", a))
                    if j == 5:
                        for g in range(4):
                            b = opened(("cb", g), 3 + g)
                            pe.matmul(b[:, 0:SEQ], C[:, XS_T + g, 0:P], C[:, XS_T + 4 + g, 0:SEQ],
                                      start=True, stop=True)
                            full(pe.matmul(b[:, SEQ:3 * P], C[:, XS_T + g, P:SEQ], C[:, XS_T + 4 + g, P:SEQ],
                                           start=True, stop=True), ("cb", g))

            def ssd_bcast(u):
                for a in range(2):
                    b = opened(("acb", u, a), 3 + a)
                    for q in range(2):
                        h = 4 * u + 2 * a + q
                        o = b[:, SEQ * q:SEQ * (q + 1)]
                        pe.matmul(o, DTA[:, 0, h:h + 1].to_broadcast([P, P]), tab("causal")[:, 0:SEQ],
                                  start=True, stop=False)
                        mm = pe.matmul(o[:, P:SEQ], DTA[:, 1, h:h + 1].to_broadcast([P, P]),
                                       tab("causal")[:, 0:P], start=False, stop=True)
                    full(mm, ("acb", u, a))

            def ssd_y(u):
                pe.wait_ge(sem("decay_ready"), u + 1)
                D = tiles("S", 3 * P, 1536 * (u % 2), 1536 * (u % 2 + 1))
                b = opened(("y", u), 5)
                for q in range(4):
                    h = 4 * u + q
                    o = b[64 * (q % 2):64 * (q % 2) + 64, SEQ * (q // 2):SEQ * (q // 2 + 1)]
                    pe.matmul(o, XD[:, 0, HEADDIM * h:HEADDIM * (h + 1)], D[:, q, 0:SEQ], start=True, stop=False)
                    mm = pe.matmul(o[:, P:SEQ], XD[:, 1, HEADDIM * h:HEADDIM * (h + 1)], D[:, q, SEQ:3 * P],
                                   start=False, stop=True)
                full(mm, ("y", u))

            def qk(j):
                src, sq = (Q[:, j, :], QSQ[:, j, :]) if j < 8 else (KD[:, j - 8, :], KSQ[:, j - 8, :])
                if j == 0:
                    pe.wait_ge(sem("qk_squared"), 2)
                    pe.wait_ge(sem("qk_scaled"), 2)
                b = opened(("qk_ss", j), 6)
                full(pe.matmul(b[:, 0:T], tab("half_ones"), sq, start=True, stop=True), ("qk_ss", j))
                b = opened(("qk_rot", j), 7)
                full(pe.matmul(b[:, 0:T], tab("rot"), src, start=True, stop=True), ("qk_rot", j))

            def state(g):
                if g == 0:
                    pe.wait_ge(sem("xd_weighed"), 1)
                b = opened(("state", g), 3 + g % 2)
                for q in range(4):
                    j = 4 * g + q
                    for half in range(2):
                        mm = pe.matmul(b[:, P * q:P * (q + 1)], XD[:, half, P * j:P * (j + 1)],
                                       BT[:, half, P * g:P * (g + 1)], start=(half == 0), stop=(half == 1))
                full(mm, ("state", g))

            def swa_scores(u):
                g, blk = u // 2, u % 2
                for hh in range(2):
                    b = opened(("s", u, hh), 3 + hh)
                    rows = slice(64 * hh, 64 * hh + 64)
                    for jj in range(2):
                        for back in range(blk + 1):
                            mm = pe.matmul(b[:, 256 * jj + P * back:256 * jj + P * (back + 1)],
                                           Q[rows, 2 * g + jj, P * blk:P * (blk + 1)],
                                           KD[rows, g, P * (blk - back):P * (blk - back + 1)],
                                           start=True, stop=True)
                    full(mm, ("s", u, hh))

            def swa_turn(u):
                pe.wait_ge(sem("probs"), u + 1)
                p = SM.rearrange("p (k w) -> p k w", w=256)
                for back in range(u % 2 + 1):
                    b = opened(("pt", u, back), 5 + back)
                    for hh in range(2):
                        for jj in range(2):
                            mm = pe.transpose(b[:, P * (2 * hh + jj):P * (2 * hh + jj + 1)],
                                              p[:, 2 * jj + hh, P * back:P * (back + 1)], ident)
                    full(mm, ("pt", u, back))

            def swa_out(u):
                g, blk = u // 2, u % 2
                for back in range(blk + 1):
                    wait_drained(pe, ("pt", u, back))
                b = opened(("o", u), 7)
                for hh in range(2):
                    for back in range(blk + 1):
                        mm = pe.matmul(b[64 * hh:64 * hh + 64, 0:256], VT[:, blk - back, HD * g:HD * (g + 1)],
                                       PTs[:, 512 * back + 256 * hh:512 * back + 256 * (hh + 1)],
                                       start=(back == 0), stop=(back == blk))
                full(mm, ("o", u))

            def mem_scores(h):
                b = opened(("ms", h), 3)
                for qb in range(2):
                    for dt in range(2):
                        mm = pe.matmul(b[:, MEM * qb:MEM * (qb + 1)], MQ[:, 2 * h + dt, P * qb:P * (qb + 1)],
                                       MK[:, 2 * h + dt, :], start=(dt == 0), stop=(dt == 1))
                full(mm, ("ms", h))

            def mem_turn(h):
                pe.wait_ge(sem("probs"), 8 + h + 1)
                b = opened(("mpt", h), 5)
                for mt in range(2):
                    for qb in range(2):
                        mm = pe.transpose(b[:, P * (2 * mt + qb):P * (2 * mt + qb + 1)],
                                          SM[:, MEM * qb + P * mt:MEM * qb + P * (mt + 1)], ident)
                full(mm, ("mpt", h))

            def mem_out(h):
                wait_drained(pe, ("mpt", h))
                b = opened(("mo", h), 7)
                for dt in range(2):
                    for mt in range(2):
                        mm = pe.matmul(b[:, 256 * dt:256 * (dt + 1)],
                                       MV[:, mt, MEM_D * h + P * dt:MEM_D * h + P * (dt + 1)],
                                       PTs[:, 256 * mt:256 * (mt + 1)], start=(mt == 0), stop=(mt == 1))
                full(mm, ("mo", h))

            def sample_bc(b_):
                for a in range(2):
                    name = ("bb", b_, a)
                    b = opened(name, 3 + a)
                    full(pe.matmul(b[:, :], ident[0:8, b_:b_ + 1].to_broadcast([8, P]),
                                   SBC[:, 512 * a:512 * (a + 1)], start=True, stop=True), name)

            def ring_arrives(r):
                pe.wait_ge(sem(f"ring_in{r % 2}"), 16 * (r // 2 + 1) + 16 * BATCH_S * (r == 18))
                return RING[r % 2]

            def sample_mem_scores(b_):
                kc = ring_arrives(b_).rearrange("p (h dt m) -> p h dt m", dt=2, m=MEM)
                if b_ == 0:
                    pe.wait_ge(sem("sample_queries"), 1)
                    opened("s_scores", 2)
                    pe.matmul(psum[2][:, 0:MEM], ones[0:8, :], ZEROS[0:8, :], start=True, stop=False)
                for dt in range(2):
                    for h in range(MEM_H):
                        mm = pe.matmul(psum[2][32 * h:32 * h + 8, 0:MEM], EIGHTS[:, 2 * h + dt, b_, :],
                                       kc[:, h, dt, :], start=False, stop=(b_ == BATCH_S - 1 and dt == 1))
                mm.then_inc(sem("ring_used"), 1)

            def sample_swa_scores(part):
                ring_arrives(8 + part)
                pe.wait_ge(sem("new_key"), part + 1)
                kc = RING[part].rearrange("p (g b m) -> p g b m", b=4, m=P)
                for b_ in range(4):
                    for g in range(KV):
                        mm = pe.matmul(psum[2][32 * g:32 * (g + 1), MEM:MEM + P], FOURS[:, g, 4 * part + b_, :],
                                       kc[:, g, b_, :], start=(part + b_ == 0), stop=(part == 1 and b_ == 3))
                if part:
                    full(mm, "s_scores")
                else:
                    mm.then_inc(sem("ring_used"), 1)

            def sample_turn():
                pe.wait_ge(sem("sample_probs"), 2)
                b = opened("spt", 6)
                for c in range(3):
                    mm = pe.transpose(b[:, P * c:P * (c + 1)], SSM[:, P * c:P * (c + 1)], ident)
                full(mm, "spt")

            def sample_mem_out(b_):
                vc = ring_arrives(10 + b_).rearrange("p (mt n) -> p mt n", mt=2)
                if b_ == 0:
                    wait_drained(pe, "spt")
                    opened("s_out", 2)
                    pe.matmul(psum[2][:, 0:MEM_D], ones[0:8, :], ZEROS[0:8, :], start=True, stop=False)
                for mt in range(2):
                    for h in range(MEM_H):
                        mm = pe.matmul(psum[2][32 * h:32 * h + 8, 0:MEM_D], EIGHTS[:, 4 * mt + h, b_, :],
                                       vc[:, mt, MEM_D * h:MEM_D * (h + 1)],
                                       start=False, stop=(b_ == BATCH_S - 1 and mt == 1))
                mm.then_inc(sem("ring_used"), 1)

            def sample_swa_out():
                vc = ring_arrives(18).rearrange("p (b n) -> p b n", b=BATCH_S)
                for b_ in range(BATCH_S):
                    for g in range(KV):
                        mm = pe.matmul(psum[2][32 * g:32 * (g + 1), MEM_D:MEM_D + P], FOURS[:, g, b_, :],
                                       each(vc[:, b_, HD * g:HD * (g + 1)], 2),
                                       start=(b_ == 0), stop=(b_ == BATCH_S - 1))
                full(mm, "s_out")

            def sample_back():
                wait_drained(pe, "s_out")
                b = opened("s_back", 6)
                for c in range(3):
                    mm = pe.transpose(b[:, P * c:P * (c + 1)], SSM[:, P * c:P * (c + 1)], ident)
                full(mm, "s_back")

            for i in range(40):
                name = ("z", i // 2) if i < 16 else ("gate", (i - 16) // 2)
                w = arrive(name)
                ring_banks[0] = 2 if 14 <= i < 39 else 3
                feature_tile(("zg", i), w, i % 2, HN, T, name)
                if i < 8:
                    ssd_bcast(i)
                if 1 <= i < 9:
                    ssd_y(i - 1)
                if i < 12:
                    qk(i)
                if 10 <= i < 14:
                    state(i - 10)
                if i in (12, 13):
                    for h in (2 * i - 24, 2 * i - 23):
                        if h == 0:
                            pe.wait_ge(sem("mq_squared"), 1)
                        squares(("ss_mq", h), 6 + h % 2, QSQ, 2 * h, 2, T)
                if i == 14:
                    pe.wait_ge(sem("qk_ready"), 12)
                if 14 <= i < 22:
                    swa_scores(i - 14)
                if 15 <= i < 23:
                    swa_turn(i - 15)
                if 16 <= i < 24:
                    swa_out(i - 16)
                if i == 23:
                    pe.wait_ge(sem("mq_ready"), 1)
                    pe.wait_ge(sem("mk_ready"), 1)
                if 23 <= i < 27:
                    mem_scores(i - 23)
                if 24 <= i < 28:
                    mem_turn(i - 24)
                if 25 <= i < 29:
                    mem_out(i - 25)
                if 14 <= i < 38 and (i - 14) % 3 == 0:
                    sample_bc((i - 14) // 3)
                if i == 15:
                    sample_mem_scores(0)
                if 15 <= i < 22:
                    sample_mem_scores(i - 14)
                if i in (22, 23):
                    sample_swa_scores(i - 22)
                if i == 26:
                    sample_turn()
                if 28 <= i < 36:
                    sample_mem_out(i - 28)
                if i == 37:
                    sample_swa_out()
                if i == 39:
                    sample_back()

            wait_drained(pe, ("mo", 3))
            wait_drained(pe, "s_back")
            for i in range(4):
                for kind, x in (("swa", Q), ("memb", MQ)):
                    w = arrive((kind, i))
                    for c in range(2):
                        feature_tile((kind, 2 * i + c), w, c, x, T, (kind, i))
            pe.wait_ge(sem("y_squared"), 2)
            squares("ss_y", 3, Z, 0, XS_T, T)
            pe.wait_ge(sem("y_ready"), 1)
            for i in range(4):
                wa = arrive(("ssma", i))
                banks = [next_proj(("ssm", 2 * i + c)) for c in range(2)]
                for part in range(2):
                    w = arrive(("ssmb", i)) if part else wa
                    for c in range(2):
                        for k in range(KT):
                            mm = pe.matmul(banks[c][:, 0:T], w[:, k, P * c:P * (c + 1)], C[:, KT * part + k, :],
                                           start=(part + k == 0), stop=(part == 1 and k == KT - 1))
                        if part:
                            full(mm, ("ssm", 2 * i + c))
                    if part == 0:
                        mm.then_inc(sem("ssma_used"), 1)
                last_use[("ssmb", i)] = ("ssm", 2 * i + 1)
            pe.wait_ge(sem("merged"), 8)
            pe.wait_ge(sem("router_in"), 16)
            token_banks = (3, 4, 6, 7)
            for m in range(KT + 2):
                if m < KT:
                    feature_tile(("out", m), arrive(("out", m // 2)), m % 2, MERGED, T, ("out", m // 2))
                if m < 2:
                    continue
                k = m - 2
                if k == 0:
                    opened("route", 5)
                if k % 4 == 0:
                    for t in range(2):
                        opened(("htok", t, k // 4), token_banks[2 * t + k // 4])
                pe.wait_ge(sem("x1_squared"), k + 1)
                pe.wait_ge(sem("x1_by_gain"), k + 1)
                for t in range(2):
                    o = psum[token_banks[2 * t + k // 4]]
                    mm = pe.transpose(o[:, P * (k % 4):P * (k % 4 + 1)], X1G[:, k % 4, P * t:P * (t + 1)], ident)
                    if k % 4 == 3:
                        full(mm, ("htok", t, k // 4))
                for t, rows in ((0, P), (2, BATCH_S), (1, P)):
                    tokens, c0 = slice(P * t, P * t + rows), 64 * t
                    pe.matmul(psum[5][0:rows, c0:c0 + ROUTES], X1G[:, k % 4, tokens], WR[:, k, :],
                              start=(k + t == 0), stop=False)
                    mm = pe.matmul(psum[5][0:rows, c0 + 40:c0 + 42], X1SQ[:, k % 4, tokens], ones[:, 0:2],
                                   start=False, stop=(k == KT - 1 and t == 1))
                if k < KT - 1:
                    mm.then_inc(sem("x1_tile_used"), 1)
                else:
                    full(mm, "route")
            for half in range(2):
                b = opened(("htok", 2, half), half)
                for q in range(4):
                    mm = pe.transpose(b[0:BATCH_S, P * q:P * (q + 1)], X1GS[:, 4 * half + q, :], ident)
                full(mm, ("htok", 2, half))
            pe.wait_ge(sem("chosen"), 1)
            b = opened("count", 5)
            causal = tab("causal")
            pe.matmul(b[:, 0:32], causal[:, 0:P], MASK[:, 0, :], start=True, stop=True)
            pe.matmul(b[:, 32:64], ones, MASK[:, 0, :], start=True, stop=False)
            pe.matmul(b[:, 32:64], causal[:, 0:P], MASK[:, 1, :], start=False, stop=True)
            pe.matmul(b[0:8, 64:96], ones[:, 0:8], MASK[:, 0, :], start=True, stop=False)
            pe.matmul(b[0:8, 64:96], ones[:, 0:8], MASK[:, 1, :], start=False, stop=False)
            pe.matmul(b[0:8, 64:96], causal[0:8, 0:8], MASK[0:8, 2, :], start=False, stop=True)
            pe.matmul(b[:, 96:128], ones, MASK[:, 0, :], start=True, stop=False)
            pe.matmul(b[:, 96:128], ones, MASK[:, 1, :], start=False, stop=False)
            full(pe.matmul(b[:, 96:128], ones[0:8, :], MASK[0:8, 2, :], start=False, stop=True), "count")

            for b in range(8):
                if uses[b]:
                    pe.wait_ge(drained[b], uses[b])

            def experts(rounds):
                def gather(n):
                    pe.wait_ge(sem("slots_ready"), n + 1)
                    for k in range(KT):
                        for t, rows in enumerate((P, P, BATCH_S)):
                            mm = pe.matmul(psum[4 + k // 4][:, P * (k % 4):P * (k % 4 + 1)],
                                           HTOK[0:rows, t, P * k:P * (k + 1)],
                                           ONE[0:rows, t].rearrange("p j s -> p (j s)"), start=(t == 0), stop=(t == 2))
                        if k % 4 == 3:
                            mm.then_inc(sem(f"gathered{k // 4}"), 1)

                def body(buf, q, n):
                    if rounds > 1:
                        gather(n)
                    pe.wait_ge(sem("gathered_stored"), n * 2 + 2)
                    for bank, kind in enumerate(("gate", "up")):
                        if kind == "gate":
                            pe.wait_ge(gate_in[buf], (q - buf) * (16 * QUAD // 2) + 16 * QUAD)
                        else:
                            pe.wait_ge(up_in[buf], (q - buf) * (16 * QUAD // 2) + 16 * QUAD)
                        for k in range(KT):
                            for j in range(QUAD):
                                mm = pe.matmul(psum[bank][SLOTS * j:SLOTS * (j + 1), 0:D_FF],
                                               HG[:, k, SLOTS * j:SLOTS * (j + 1)], piece(kind, buf, j)[:, k, :],
                                               start=(k == 0), stop=(k == KT - 1))
                        mm.then_inc(sem(f"{kind}_filled"), 1)
                    if rounds == 1:
                        gather(n + 1)
                    pe.wait_ge(sem("act_ready"), n + 1)
                    for f in range(FF_T):
                        mm = pe.transpose(psum[1][:, P * f:P * (f + 1)], ACTV[:, P * f:P * (f + 1)], ident)
                    mm.then_inc(sem("act_turned"), 1)
                    pe.wait_ge(sem("tile_added"), n * KT + 2)
                    for t, rows in enumerate((P, P, BATCH_S)):
                        mm = pe.transpose(psum[6][:, P * t:P * t + rows],
                                          ONEW[buf if rounds == 1 else 0][0:rows, t].rearrange("p j s -> p (j s)"),
                                          ident[0:rows, 0:rows])
                    mm.then_inc(sem("back_filled"), 1)
                    pe.wait_ge(down_in, q * (16 * QUAD) + 16 * QUAD)
                    pe.wait_ge(sem("actT_ready"), n + 1)
                    for half in range(2):
                        for f in range(FF_T):
                            for j in range(QUAD):
                                mm = pe.matmul(psum[2 + half][SLOTS * j:SLOTS * (j + 1), :],
                                               ACTT[:, f, SLOTS * j:SLOTS * (j + 1)],
                                               piece("down", buf, j)[:, f, 512 * half:512 * (half + 1)],
                                               start=(f == 0), stop=(f == 1))
                        mm.then_inc(sem(f"down_filled{half}"), 1)
                    pe.wait_ge(sem("back_ready"), n + 1)
                    for m in range(KT):
                        if m % 4 == 0:
                            pe.wait_ge(sem(f"down_stored{m // 4}"), n + 1)
                        pe.wait_ge(sem("tile_added"), n * KT + (m + 1))
                        pe.matmul(psum[6 + m % 2][:, 0:T], DOWNED[:, P * m:P * (m + 1)], BACK,
                                  start=True, stop=True).then_inc(sem("tile_filled"), 1)

                if rounds == 1:
                    gather(0)
                steps(pe, rounds, body)

            by_rounds(pe, experts)

        @block.sync
        def _(sp):
            sp.dma_start(MT, ins["memT"]).then_inc(sem("mem_in"), 16)
            sp.dma_start(at("tab"), ins["tables"]).then_inc(sem("tables_in"), 16)
            sp.dma_start(at("vec"), ins["vectors"]).then_inc(sem("tables_in"), 16)
            sp.dma_start(XT, ins["xT"]).then_inc(sem("x_in"), 16)

            def load_chunk(n):
                name, parts = chunks[n]
                if n >= WBUFS:
                    held = chunks[n - WBUFS][0]
                    if held in split_number:
                        for c in range(2):
                            sp.wait_ge(*low_made(split_number[held], c))
                    elif held[0] == "ssma":
                        sp.wait_ge(sem("ssma_used"), held[1] + 1)
                    else:
                        wait_filled(sp, last_use[held])
                for src, c0, width in parts:
                    if name == ("dt", 0):
                        off = CHUNK * (n % WBUFS)
                        dst = at("W", off, off + KT * width).rearrange("p (k n) -> p k n", n=width)
                    else:
                        dst = chunk(n)[:, :, c0:c0 + width]
                    sp.dma_start(dst, src).then_inc(chunk_in[n % WBUFS], 16)

            def load_ring(r):
                dst = RING[r % 2]
                if r == 0:
                    for g in range(4):
                        wait_filled(sp, ("cb", g))
                    for a in range(2):
                        wait_filled(sp, ("sbc", a))
                        wait_filled(sp, ("btok", a))
                elif r == 1:
                    wait_filled(sp, ("state", 3))
                elif r == 11:
                    wait_filled(sp, "s_scores")
                else:
                    sp.wait_ge(sem("ring_used"), r - 1 if r < 11 else r - 2)
                if r in (10, 11):
                    sp.wait_ge(sem(f"s_k_out{r - 10}"), 16)
                if r < 8:
                    src = ins["mem_kT"][r]
                elif r < 10:
                    src = ins["swa_kT"][r - 8]
                elif r < 18:
                    src = ins["mem_v"][r - 10]
                else:
                    src = ins["swa_v"]
                sp.dma_start(dst, src).then_inc(sem(f"ring_in{r % 2}"), 16)

            def new_values():
                sp.wait_ge(sem("ring_in0"), 160)
                wait_drained(sp, ("v", 2))
                for b_ in range(BATCH_S):
                    sp.dma_start(RING[0][0:1, 256 * b_:256 * (b_ + 1)], VT[b_:b_ + 1, 2, :]
                                 ).then_inc(sem("ring_in0"), 16)

            first_z = number[("z", 0)]
            r = 0
            for n in range(number[("swa", 0)]):
                m = n - first_z
                while r < 18 and m >= (6 if r == 0 else (17 + r) / 2 if r < 10 else (21 + r) / 2):
                    load_ring(r)
                    r += 1
                load_chunk(n)
            while r < 19:
                load_ring(r)
                r += 1
            new_values()

            def load_piece(kind, e, q, j):
                src = ins[f"w_exp_{kind}"][e].rearrange("(k p) f -> p k f", p=P)
                sp.dma_start(piece(kind, q, j), src).then_inc(
                    {"gate": gate_in[q % 2], "up": up_in[q % 2], "down": down_in}[kind], 16)

            for n in range(number[("swa", 0)], len(chunks)):
                name = chunks[n][0]
                load_chunk(n)
                if name == ("memb", 0):
                    wait_filled(sp, "s_back")
                    wait_filled(sp, ("mo", 3))
                    sp.wait_ge(sem("s_v_out"), 16)
                    sp.wait_ge(sem("samples_done"), 1)
                    for b in range(2):
                        sp.wait_ge(sem(f"s_ssm_out{b}"), 16 * BATCH_S // 2)
                    load_piece("gate", 0, 0, 0)
                    load_piece("gate", 1, 0, 1)
                elif name == ("swa", 1):
                    load_piece("gate", 2, 0, 2)
                    sp.dma_start(HN, ins["xT"]).then_inc(sem("x_again"), 16)
                elif name == ("memb", 1):
                    load_piece("gate", 3, 0, 3)
                elif name == ("memb", 2):
                    load_piece("up", 0, 0, 0)
                elif name == ("memb", 3):
                    load_piece("up", 1, 0, 1)
                elif name == ("ssmb", 1):
                    wait_filled(sp, ("swa", 7))
                    wait_filled(sp, ("memb", 7))
                    load_piece("up", 2, 0, 2)
                    load_piece("up", 3, 0, 3)
                elif name == ("ssmb", 2):
                    load_piece("down", 0, 0, 0)
                    wait_filled(sp, "ss_y")
                    load_piece("down", 1, 0, 1)
                elif name == ("ssmb", 3):
                    load_piece("down", 2, 0, 2)
            sp.wait_ge(sem("merged"), 8)
            load_piece("down", 3, 0, 3)
            for j in range(QUAD):
                load_piece("gate", QUAD + j, 1, j)
            load_piece("up", QUAD, 1, 0)
            wait_filled(sp, ("out", 7))
            load_piece("up", QUAD + 1, 1, 1)
            wait_filled(sp, "route")
            for j in range(2, QUAD):
                load_piece("up", QUAD + j, 1, j)

            def experts(rounds):
                def next_pieces(kind, q, buf):
                    if kind == "down":
                        sp.wait_ge(sem("down_filled1"), q * rounds)
                    else:
                        sp.wait_ge(sem(f"{kind}_filled"), (q - 1) * rounds)
                    for j in range(QUAD):
                        load_piece(kind, q * QUAD + j, buf, j)

                next_pieces("gate", 2, 0)
                with sp.Fori(0, QUADS // 2 - 2) as it:
                    for b in range(1, 3):
                        q = it * 2 + b
                        next_pieces("down", q, b % 2)
                        next_pieces("up", q + 1, (b + 1) % 2)
                        next_pieces("gate", q + 2, b % 2)
                next_pieces("down", QUADS - 3, 1)
                next_pieces("up", QUADS - 2, 0)
                next_pieces("gate", QUADS - 1, 1)
                next_pieces("down", QUADS - 2, 0)
                next_pieces("up", QUADS - 1, 1)
                next_pieces("down", QUADS - 1, 1)
                for half in range(2):
                    sp.wait_ge(sem("tile_added"), 2 + KT * QUADS * rounds - KT // 2 * (1 - half))
                    tiles_ = slice(KT // 2 * half, KT // 2 * (half + 1))
                    sp.dma_start(outs["yT"][:, tiles_, :], X1[:, tiles_, :]).then_inc(sem("y_out"), 16)

            by_rounds(sp, experts)
            sp.wait_ge(sem("y_out"), 32)

        @block.gpsimd
        def _(pool):
            def lows(first, end):
                for m in range(first, end):
                    for c in range(1 if m < DVE_LOWS else 2):
                        pool.wait_ge(sem(f"high_ready{c}"), m + 1)
                        high, low = w_split(SPLIT[m], c)
                        low_part(nc.gpsimd, like_raw(low, SPLIT[m]), raw_half(SPLIT[m], c), like_raw(high, SPLIT[m])).then_inc(sem(f"low_ready{c}"), 1)

            lows(0, 2)
            pool.wait_ge(sem("mem_normed"), 1)
            pool.dma_start(HIST, ins["histT"]).then_inc(sem("hist_in"), 16)
            lows(2, 12)
            pool.wait_ge(sem("mk_ready"), 1)
            pool.dma_start(outs["p_mem_kT"], MK).then_inc(sem("p_mem_out"), 16)
            lows(12, 14)
            for i in range(4):
                for c in range(2):
                    wait_drained(pool, ("mv", i, c))
            pool.dma_start(outs["p_mem_v"], MV).then_inc(sem("p_mem_out"), 16)
            lows(14, 22)
            pool.wait_ge(sem("new_conv"), 1)
            pool.dma_start(outs["newconvT"], NEWC).then_inc(sem("conv_out"), 16)
            lows(22, len(SPLIT))
            for t in range(3):
                wait_drained(pool, ("v", t))
            pool.dma_start(outs["p_swa_v"], VT[:, 1, :]).then_inc(sem("p_v_out"), 16)

            def load_state(b):
                if b >= 2:
                    pool.wait_ge(sem(f"s_ssm_out{b % 2}"), 16 * (b // 2))
                pool.dma_start(HS[b % 2], ins["state_ssm"][b].rearrange("(j p) n -> p j n", p=P)
                               ).then_inc(sem(f"state_in{b % 2}"), 16)

            pool.wait_ge(sem("conv_active"), 3)
            load_state(0)
            load_state(1)
            pool.wait_ge(sem("qk_ready"), 12)
            pool.dma_start(outs["p_swa_kT"], KD[0:64, :, P:SEQ]).then_inc(sem("p_k_out"), 16)
            for g in range(4):
                wait_drained(pool, ("state", g))
            pool.dma_start(outs["p_ssm"].rearrange("(j p) n -> p j n", p=P),
                           at("S", 0, 2048).rearrange("p (j n) -> p j n", n=STATE)).then_inc(sem("p_ssm_out"), 16)

            def store_state(b):
                pool.wait_ge(sem("state_new"), b + 1)
                pool.dma_start(outs["s_ssm"][b].rearrange("(j p) n -> p j n", p=P), HS[b % 2]
                               ).then_inc(sem(f"s_ssm_out{b % 2}"), 16)

            def decay_state(b):
                H = HS[b % 2]
                pool.wait_ge(sem(f"state_in{b % 2}"), 16 * (b // 2 + 1))
                nc.gpsimd.tensor_tensor(H, H, EX[:, 1, :, b].unsqueeze(2).to_broadcast([P, XS_T, STATE]), ALU.mult
                                        ).then_inc(sem("state_decayed"), 1)

            decay_state(0)
            for b in range(BATCH_S):
                if b + 1 < BATCH_S:
                    decay_state(b + 1)
                store_state(b)
                if b + 2 < BATCH_S:
                    pool.wait_ge(sem("sample_y"), b + 1)
                    load_state(b + 2)
                if b == 2:
                    for part in range(2):
                        pool.wait_ge(sem("new_key"), part + 1)
                        pool.dma_start(outs["s_swa_kT"][part], RING[part][0:64, :]).then_inc(sem(f"s_k_out{part}"), 16)
            pool.wait_ge(sem("ring_in0"), 160 + 16 * BATCH_S)
            pool.dma_start(outs["s_swa_v"], RING[0]).then_inc(sem("s_v_out"), 16)
            pool.wait_ge(sem("samples_done"), 1)
            pool.dma_start(WR, ins["w_router"].rearrange("(k p) n -> p k n", p=P)).then_inc(sem("router_in"), 16)
            for name, n in (("p_mem_out", 32), ("p_v_out", 16), ("conv_out", 16), ("p_k_out", 16), ("p_ssm_out", 16),
                            ("s_ssm_out0", 64), ("s_ssm_out1", 64), ("s_k_out0", 16), ("s_k_out1", 16), ("s_v_out", 16)):
                pool.wait_ge(sem(name), n)

        @block.scalar
        def _(act):
            a = nc.scalar

            def evac(name, dst, n, rows=P, src=None):
                b = wait_filled(act, name)
                drains(a.activation(dst, b[0:rows, 0:n] if src is None else src(b), ACT.Copy), name)

            def rstd(name, dst, width, n):
                b = wait_filled(act, name)
                a.preload_act_table_set("natural_log_exp_and_others")
                drains(a.activation(dst, b[:, 0:n], ACT.Ln, scale=1.0 / width, bias=EPS), name)
                wait_drained(act, name)
                done(act, a.activation(dst, dst, ACT.Exp, scale=-0.5), "rstd")

            halves_made = [0]

            def highs(end):
                while halves_made[0] < min(end, 2 * len(SPLIT)):
                    half = halves_made[0]
                    name, c = SPLIT[half // 2], half % 2
                    n = number[name]
                    act.wait_ge(chunk_in[n % WBUFS], chunk_value[n])
                    if held_before[half] is not None:
                        before = held_before[half]
                        wait_filled(act, split_use[SPLIT[before // 2], before % 2])
                    if name == ("q", 1) and c == 0:
                        act.wait_ge(sem("new_conv"), 1)
                        act.wait_ge(sem("conv_out"), 16)
                    a.activation(like_raw(w_split(name, c)[0], name), raw_half(name, c), ACT.Copy).then_inc(sem(f"high_ready{c}"), 1)
                    halves_made[0] += 1

            act.wait_ge(sem("mem_in"), 16)
            a.activation(MSQ, MT, ACT.Square).then_inc(sem("mem_squared"), 1)
            act.wait_ge(sem("x_in"), 16)
            a.activation(XSQ, XT, ACT.Square).then_inc(sem("x_squared"), 1)
            highs(1)
            rstd("ss_mem", TQ[:, 0:MEM], D_MODEL, MEM)
            rstd("ss_x", RS, D_MODEL, T)
            highs(4)
            for j in range(8):
                evac(("mk", j), MK[:, j, :], MEM)
                highs(j + 4)
            wait_drained(act, ("mk", 7))
            a.activation(MSQ, MK, ACT.Square).then_inc(sem("mk_squared"), 1)
            for i in range(4):
                for mt in range(2):
                    evac(("mv", i, mt), MV[:, mt, CW * i:CW * (i + 1)], CW)
                    highs(8 + 2 * i + 2 * mt + 4)
            for h in range(MEM_H):
                rstd(("ss_mk", h), RSM[:, h, :], MEM_D, MEM)

            def silu_conv(batch):
                act.wait_ge(sem("convolved"), batch + 1)
                v = C[:, 8 * batch:8 * (batch + 1), :]
                a.activation(v, v, ACT.Silu).then_inc(sem("conv_active"), 1)

            for j in range(CONV_T):
                evac(("xbc", j), X[:, j, :], T)
                highs(16 + j + 4)
                if j == 13:
                    silu_conv(0)
                if j == 21:
                    silu_conv(1)
            act.wait_ge(sem("dt_zeroed"), 1)
            b = wait_filled(act, "dt")
            a.activation(at("S", 0, 64), b[:, 0:64], ACT.Copy)
            drains(a.activation(at("S", 64, 96, BATCH_S), b[0:BATCH_S, 64:96], ACT.Copy), "dt")
            for j in range(KV):
                evac(("kd", j), KD[:, j, :], T)
                highs(min(40 + j + 4, 44))
            wait_drained(act, ("kd", 3))
            a.activation(KSQ, KD, ACT.Square).then_inc(sem("qk_squared"), 1)
            for t, rows in enumerate((P, P, BATCH_S)):
                if t == 2:
                    highs(46)
                evac(("v", t), VT[0:rows, t, :], CW, rows)
            act.wait_ge(sem("dt_minus_abs"), 1)
            a.preload_act_table_set("natural_log_exp_and_others")
            E1, U1, L1 = (at("S", 96 * i, 96 * (i + 1)) for i in range(1, 4))
            done(act, a.activation(E1, E1, ACT.Exp), "dt_exp")
            act.wait_ge(sem("dt_one_plus"), 1)
            done(act, a.activation(L1, U1, ACT.Ln), "dt_ln")
            a.activation(at("S", 384, 384 + 32), vec("a_log"), ACT.Exp).then_inc(sem("a_exp"), 1)
            for j in range(8):
                evac(("q", j), Q[:, j, :], T)
                highs(44 + j + 3)
                if j == 0:
                    act.wait_ge(sem("dta"), 1)
                    a.activation(at("S", 416, 448, 8), DTA[0:8, 2, :], ACT.Exp).then_inc(sem("da_exp"), 1)
                if j == 1:
                    silu_conv(2)
            wait_drained(act, ("q", 7))
            a.activation(QSQ, Q, ACT.Square).then_inc(sem("qk_squared"), 1)
            act.wait_ge(sem("to_end"), 1)
            a.activation(WE, WE, ACT.Exp).then_inc(sem("end_decay"), 1)
            for j in range(8):
                evac(("mq", j), MQ[:, j, :], T)
                highs(52 + j + 3)
                if j == 4:
                    for half in range(2):
                        evac(("btok", half), BT[:, half, :], 512)
                    for k in range(2):
                        evac(("sbc", k), SBC[:, 512 * k:512 * (k + 1)], 512, 8)

            for i in range(42):
                if i < 40:
                    evac(("zg", i), Z[:, i, :] if i < 16 else G[:, i - 16, :], T)
                if i < 8:
                    act.wait_ge(sem("segments"), i + 1)
                    D = at("S", 1536 * (i % 2), 1536 * (i % 2 + 1))
                    a.activation(D, D, ACT.Exp).then_inc(sem("decay_exp"), 1)
                if i < 12:
                    if i:
                        act.wait_ge(sem("qk_ready"), i)
                    rstd(("qk_ss", i), RS, HD, T)
                if i == 9:
                    wait_filled(act, ("qk_ss", 7))
                    wait_drained(act, ("mq", 7))
                    a.activation(QSQ, MQ, ACT.Square).then_inc(sem("mq_squared"), 1)
                if 10 <= i < 14:
                    if i == 10:
                        wait_filled(act, ("y", 7))
                    g = i - 10
                    evac(("state", g), at("S", 512 * g, 512 * (g + 1)), 512)
                if i in (12, 13):
                    for h in (2 * i - 24, 2 * i - 23):
                        if h == 0:
                            act.wait_ge(sem("qk_ready"), 12)
                        else:
                            act.wait_ge(sem("mq_scaled"), h)
                        rstd(("ss_mq", h), RS, MEM_D, T)
                if 16 <= i < 24:
                    u = i - 16
                    g, blk = u // 2, u % 2
                    evac(("o", u), Q[:, 2 * g:2 * g + 2, P * blk:P * (blk + 1)], 256,
                         src=lambda b: b[:, 0:256].rearrange("p (j q) -> p j q", j=2))
                if 25 <= i < 29:
                    h = i - 25
                    evac(("mo", h), MQ[:, 2 * h:2 * h + 2, 0:SEQ], 512,
                         src=lambda b: b[:, :].rearrange("p (j q) -> p j q", j=2))
                if 14 <= i < 22:
                    u = i - 14
                    width = P * (u % 2 + 1)
                    act.wait_ge(sem("swa_max"), u + 1)
                    for k in range(4):
                        p = SM[:, 256 * k:256 * k + width]
                        a.activation(p, p, ACT.Exp, bias=at("ST", 4 + k, 5 + k), accum_out=at("ST", 8 + k, 9 + k))
                    a.activation(at("ST", 12, 16), at("ST", 12, 16), ACT.Exp).then_inc(sem("exps"), 1)
                if 23 <= i < 27:
                    h = i - 23
                    act.wait_ge(sem("mem_max"), h + 1)
                    if h:
                        wait_filled(act, ("mpt", h - 1))
                    else:
                        wait_filled(act, ("pt", 7, 1))
                    b = wait_filled(act, ("ms", h))
                    a.activation(SM[:, 0:MEM], b[:, 0:MEM], ACT.Exp, bias=at("ST", 20, 21), scale=MEM_D ** -0.5,
                                 accum_out=at("ST", 24, 25)).then_inc(sem("mem_exp0"), 1)
                    done(act, a.activation(SM[:, MEM:2 * MEM], b[:, MEM:2 * MEM], ACT.Exp, bias=at("ST", 21, 22),
                                           scale=MEM_D ** -0.5, accum_out=at("ST", 25, 26)), "exps")
                if 14 <= i < 38 and (i - 14) % 3 == 0:
                    b_ = (i - 14) // 3
                    if b_ == 0:
                        act.wait_ge(sem("p_ssm_out"), 16)
                    else:
                        act.wait_ge(sem("sample_y"), b_)
                    for k in range(2):
                        evac(("bb", b_, k), BB[:, 512 * k:512 * (k + 1)], 512)
                if i == 28:
                    wait_drained(act, ("zg", 15))
                    a.activation(at("Z"), at("Z"), ACT.Silu).then_inc(sem("z_active"), 1)
                if i == 31:
                    act.wait_ge(sem("y_gated"), 1)
                    a.activation(Z[:, :, 0:SEQ], C[:, 0:XS_T, 0:SEQ], ACT.Square).then_inc(sem("y_squared"), 1)
                if i == 24:
                    act.wait_ge(sem("sample_max"), 1)
                    b = wait_filled(act, "s_scores")
                    a.activation(SSM[:, 0:MEM], b[:, 0:MEM], ACT.Exp, bias=at("ST", 32, 33),
                                 scale=MEM_D ** -0.5, accum_out=at("ST", 34, 35)).then_inc(sem("sexp0"), 1)
                    a.activation(SSM[:, MEM:MEM + P], b[:, MEM:MEM + P], ACT.Exp, bias=at("ST", 33, 34),
                                 scale=HD ** -0.5, accum_out=at("ST", 35, 36)).then_inc(sem("sexp1"), 1)
                    a.activation(at("ST", 36, 37), at("ST", 36, 37), ACT.Exp).then_inc(sem("sample_exps"), 1)
                if i == 38:
                    wait_filled(act, "spt")
                    evac("s_out", SSM, 384)
                if i == 40:
                    b = wait_filled(act, "s_back")
                    for dt in range(2):
                        dst = MQ.rearrange("p (h dt) t -> p h dt t", dt=2)[:, :, dt, SEQ:T]
                        src = b[:, P * dt:P * (dt + 1)].rearrange("p (h c) -> p h c", h=MEM_H)[:, :, 0:BATCH_S]
                        a.activation(dst, src, ACT.Copy)
                    for hh in range(2):
                        rows = slice(64 * hh, 64 * (hh + 1))
                        dst = Q[rows, :, SEQ:T].rearrange("p (g j) b -> p g j b", j=2)
                        src = b[rows, 2 * P:3 * P].rearrange("p (g b j hh) -> p g j b hh", g=KV, j=2, hh=2)[..., hh]
                        last = a.activation(dst, src, ACT.Copy)
                    drains(last, "s_back")
            wait_drained(act, ("zg", 39))
            wait_drained(act, ("zg", 38))
            wait_drained(act, ("zg", 37))
            act.wait_ge(sem("y_gated"), 2)
            a.activation(Z[:, :, SEQ:T], C[:, 0:XS_T, SEQ:T], ACT.Square).then_inc(sem("y_squared"), 1)
            a.activation(at("G"), at("G"), ACT.Sigmoid).then_inc(sem("gates_active"), 1)
            rstd("ss_y", RS, D_INNER, T)
            act.wait_ge(sem("p_mem_out"), 32)
            for m in range(KT):
                act.wait_ge(sem("x1_made"), m + 1)
                if m >= 4:
                    act.wait_ge(sem("x1_tile_used"), m - 3)
                a.activation(X1SQ[:, m % 4, :], X1[:, m, :], ACT.Square).then_inc(sem("x1_squared"), 1)
            act.wait_ge(sem("ssq_ready"), 1)
            done(act, a.activation(RTOK, SSQ, ACT.Ln, scale=1.0 / D_MODEL, bias=EPS), "rtok_ln")
            done(act, a.activation(RTOK, RTOK, ACT.Exp, scale=-0.5), "rtok")
            for t, rows in enumerate((P, P, BATCH_S)):
                for half in range(2):
                    name = ("htok", t, half)
                    b = wait_filled(act, name)
                    drains(a.activation(HTOK[0:rows, t, 512 * half:512 * (half + 1)], b[0:rows, :], ACT.Copy,
                                        scale=RTOK[0:rows, t:t + 1]), name)
            act.wait_ge(sem("route_args"), 1)
            done(act, a.activation(at("S", 1100, 1112), at("S", 1100, 1112), ACT.Exp), "route_exp")
            done(act, a.activation(at("S", 1112, 1115), at("S", 1112, 1115), ACT.Exp), "route_exp")

            def experts(rounds):
                def store_gathered(n):
                    act.wait_ge(sem("gathered0"), n + 1)
                    a.activation(HG[:, 0:4, :].rearrange("p k s -> p (k s)"), psum[4][:, :], ACT.Copy
                                 ).then_inc(sem("gathered_stored"), 1)

                def body(buf, q, n):
                    if rounds > 1:
                        store_gathered(n)
                    act.wait_ge(sem("gate_filled"), n + 1)
                    a.activation(SG, psum[0][:, 0:D_FF], ACT.Silu).then_inc(sem("silu"), 1)
                    if rounds == 1:
                        store_gathered(n + 1)
                    act.wait_ge(sem("down_filled0"), n + 1)
                    a.activation(DOWNED[:, 0:512], psum[2][:, :], ACT.Copy).then_inc(sem("down_stored0"), 1)

                if rounds == 1:
                    store_gathered(0)
                steps(act, rounds, body)

            by_rounds(act, experts)

        @block.vector
        def _(dve):
            v = nc.vector

            def link(ins_):
                done(dve, ins_, "vector_chain")

            v.memset(at("S", 0, 96), 0.0).then_inc(sem("dt_zeroed"), 1)
            dve.wait_ge(sem("tables_in"), 32)
            def normed(out, x, r, gain, n, name):
                for k in range(KT):
                    last = v.scalar_tensor_tensor(out[:, k, 0:n], x[:, k, 0:n], vec(gain, k, k + 1), r,
                                                  ALU.mult, ALU.mult)
                last.then_inc(sem(name), 1)

            dve.wait_ge(sem("mem_in"), 16)
            dve.wait_ge(sem("rstd"), 1)
            normed(MN, MT, TQ[:, 0:MEM], "gmem", MEM, "mem_scaled")
            dve.wait_ge(sem("mem_scaled"), 1)
            done(dve, v.tensor_copy(m_high[:, :], apart["HN"][:, 0:KT * MEM]), "mem_high")
            low_part(v, m_low[:, :], apart["HN"][:, 0:KT * MEM], m_high[:, :]).then_inc(sem("mem_normed"), 1)
            dve.wait_ge(sem("mem_normed"), 1)
            def vector_lows(first, end):
                for m in range(first, end):
                    dve.wait_ge(sem("high_ready1"), m + 1)
                    high, low = w_split(SPLIT[m], 1)
                    low_part(v, low, raw_half(SPLIT[m], 1), high).then_inc(sem("lows_by_vector"), 1)

            vector_lows(0, 3)
            dve.wait_ge(sem("x_in"), 16)
            dve.wait_ge(sem("rstd"), 2)
            normed(HN, XT, RS, "g1", T, "x_scaled")
            dve.wait_ge(sem("x_scaled"), 1)
            done(dve, v.tensor_copy(x_high[:, :], apart["HN"][:, :]), "x_high")
            low_part(v, x_low[:, :], apart["HN"][:, :], x_high[:, :]).then_inc(sem("x_normed"), 1)
            vector_lows(3, DVE_LOWS)
            for h in range(MEM_H):
                dve.wait_ge(sem("rstd"), 3 + h)
                for dt in range(2):
                    t = MK[:, 2 * h + dt, :]
                    last = v.scalar_tensor_tensor(t, t, vec("gmk", dt, dt + 1), RSM[:, h, :], ALU.mult, ALU.mult)
            last.then_inc(sem("mk_ready"), 1)

            def tap(j, k):
                a_, _n = VEC["conv_w"]
                return at("vec", a_ + CONV_T * k + j, a_ + CONV_T * k + j + 1)

            def conv(batch):
                js = range(8 * batch, 8 * (batch + 1))
                wait_drained(dve, ("xbc", js[-1]))
                wait_drained(dve, ("xbc", js[-2]))
                wait_drained(dve, ("xbc", js[-3]))
                for j in js:
                    last = v.tensor_scalar(C[:, j, 0:SEQ], X[:, j, 0:SEQ], tap(j, 3), vec("conv_b", j, j + 1),
                                           ALU.mult, ALU.add)
                link(last)
                for back in range(1, CONV_TAPS):
                    for j in js:
                        last = v.scalar_tensor_tensor(C[:, j, back:SEQ], X[:, j, 0:SEQ - back], tap(j, 3 - back),
                                                      C[:, j, back:SEQ], ALU.mult, ALU.add)
                    link(last)
                cs, xs_ = C[:, js[0]:js[-1] + 1, SEQ:T], X[:, js[0]:js[-1] + 1, SEQ:T]
                tmp = at("S", 512, 512 + 64).rearrange("p (j b) -> p j b", b=BATCH_S)

                def w(k):
                    return over(vec("conv_w", CONV_T * k + js[0], CONV_T * k + js[-1] + 1), BATCH_S)

                link(v.tensor_tensor(cs, xs_, w(3), ALU.mult))
                dve.wait_ge(sem("hist_in"), 16)
                for k in range(3):
                    link(v.tensor_tensor(tmp, HIST[:, js[0]:js[-1] + 1, :, k], w(k), ALU.mult))
                    link(v.tensor_tensor(cs, cs, tmp, ALU.add))
                done(dve, v.tensor_tensor(cs, cs, over(vec("conv_b", js[0], js[-1] + 1), BATCH_S), ALU.add),
                     "convolved")

            conv(0)
            conv(1)
            conv(2)
            new = NEWC[:, :, 0:24].rearrange("p j (b k) -> p j b k", k=3)
            link(v.tensor_copy(new[:, :, :, 0:2], HIST[:, :, :, 1:3]))
            link(v.tensor_copy(new[:, :, :, 2], X[:, :, SEQ:T]))
            done(dve, v.tensor_copy(NEWC[:, :, 24:27], X[:, :, SEQ - 3:SEQ]), "new_conv")

            R0, E1, U1, L1 = (at("S", 96 * i, 96 * (i + 1)) for i in range(4))
            AEXP, DAS = at("S", 384, 416), at("S", 416, 448, 8)
            R3 = R0.rearrange("p (t h) -> p t h", t=3)
            wait_drained(dve, "dt")
            link(v.tensor_tensor(R3, R3, each(vec("dt_bias"), 3), ALU.add))
            link(v.tensor_scalar(E1, R0, -1.0, None, ALU.mult))
            done(dve, v.tensor_tensor(E1, E1, R0, ALU.min), "dt_minus_abs")
            dve.wait_ge(sem("dt_exp"), 1)
            done(dve, v.tensor_scalar(U1, E1, 1.0, None, ALU.add), "dt_one_plus")
            link(v.tensor_scalar(at("S", 448, 544), U1, -1.0, None, ALU.add))
            link(v.tensor_scalar(at("S", 544, 640), at("S", 448, 544), 0.0, None, ALU.is_equal))
            link(v.tensor_tensor(at("S", 448, 544), at("S", 448, 544), at("S", 544, 640), ALU.add))
            link(v.reciprocal(at("S", 448, 544), at("S", 448, 544)))
            dve.wait_ge(sem("dt_ln"), 1)
            link(v.tensor_tensor(L1, L1, at("S", 544, 640), ALU.add))
            link(v.tensor_tensor(L1, L1, E1, ALU.mult))
            link(v.tensor_tensor(L1, L1, at("S", 448, 544), ALU.mult))
            link(v.tensor_scalar(R0, R0, 0.0, None, ALU.max))
            link(v.tensor_tensor(at("DT"), R0, L1, ALU.add))
            dve.wait_ge(sem("a_exp"), 1)
            link(v.tensor_tensor(DTA, DT, each(AEXP, 3), ALU.mult))
            done(dve, v.tensor_scalar(at("DTA"), at("DTA"), -1.0, None, ALU.mult), "dta")
            dve.wait_ge(sem("da_exp"), 1)
            wait_filled(dve, ("kd", 3))
            link(v.tensor_copy(DTX.rearrange("p (h d) -> p h d", d=HEADDIM), over(DT[0:8, 2, :], HEADDIM)))
            done(dve, v.tensor_copy(DAX.rearrange("p (h d) -> p h d", d=HEADDIM), over(DAS, HEADDIM)), "dt_expanded")
            b = wait_filled(dve, "acum")
            link(v.tensor_copy(at("AC"), b[:, 0:64]))
            drains(v.tensor_tensor(WE, each(b[:, 64:96], 2), AC, ALU.subtract), "acum")
            wait_drained(dve, "acum")
            done(dve, v.tensor_scalar(at("WE"), at("WE"), 0.0, None, ALU.min), "to_end")
            b = wait_filled(dve, "ex")
            drains(v.tensor_copy(at("EX"), b[:, 0:256]), "ex")
            wait_drained(dve, "ex")
            dve.wait_ge(sem("qk_squared"), 2)
            done(dve, v.tensor_scalar(at("KD"), at("KD"), vec("gk"), None, ALU.mult), "qk_scaled")
            done(dve, v.tensor_scalar(at("Q"), at("Q"), vec("gq"), None, ALU.mult), "qk_scaled")
            dve.wait_ge(sem("conv_active"), 3)
            link(v.tensor_tensor(XS, C[:, 0:XS_T, SEQ:T], EX[:, 0, :, :], ALU.mult))
            for j in range(4):
                for half in range(2):
                    b = wait_filled(dve, ("xtok", half, j))
                    drains(v.tensor_tensor(XD[:, half, 512 * j:512 * (j + 1)].rearrange("p (h d) -> p h d", d=HEADDIM),
                                           b[:, :].rearrange("p (h d) -> p h d", d=HEADDIM),
                                           over(DT[:, half, 8 * j:8 * (j + 1)], HEADDIM), ALU.mult),
                           ("xtok", half, j))
            for g in range(4):
                b = wait_filled(dve, ("cb", g))
                drains(v.tensor_tensor(CB[:, g, :], b[:, 0:3 * P], tab("causal"), ALU.mult), ("cb", g))
                wait_drained(dve, ("cb", g))

            def segments(u):
                if u >= 2:
                    wait_filled(dve, ("y", u - 2))
                D = tiles("S", 3 * P, 1536 * (u % 2), 1536 * (u % 2 + 1))
                for a_ in range(2):
                    b = wait_filled(dve, ("acb", u, a_))
                    for q in range(2):
                        h = 4 * u + 2 * a_ + q
                        o = b[:, SEQ * q:SEQ * (q + 1)]
                        v.tensor_scalar(D[:, 2 * a_ + q, 0:SEQ], o, AC[:, 0, h:h + 1], 0.0,
                                        ALU.subtract, ALU.min)
                        last = v.tensor_scalar(D[:, 2 * a_ + q, SEQ:3 * P], o[:, P:SEQ], AC[:, 1, h:h + 1], 0.0,
                                               ALU.subtract, ALU.min)
                    if a_ == 0:
                        drains(last, ("acb", u, 0))
                drains(last, ("acb", u, 1))
                wait_drained(dve, ("acb", u, 1))
                done(dve, v.tensor_scalar(at("ST", 60, 61), AC[:, 0, 0:1], 0.0, None, ALU.mult), "segments")

            def decays(u):
                dve.wait_ge(sem("decay_exp"), u + 1)
                D = tiles("S", 3 * P, 1536 * (u % 2), 1536 * (u % 2 + 1))
                done(dve, v.tensor_tensor(D, D, each(CB[:, u // 2, :], 4), ALU.mult), "decay_ready")

            def y_add(u):
                b = wait_filled(dve, ("y", u))
                for q in range(2):
                    j = 2 * u + q
                    last = v.scalar_tensor_tensor(C[:, j, 0:SEQ], C[:, j, 0:SEQ], vec("ssm_d", j, j + 1),
                                                  b[:, SEQ * q:SEQ * (q + 1)], ALU.mult, ALU.add)
                drains(last, ("y", u))

            def rotate(j):
                src = Q[:, j, :] if j < 8 else KD[:, j - 8, :]
                b = wait_filled(dve, ("qk_rot", j))
                drains(v.tensor_tensor(TQ, b[:, 0:T], tab("sin"), ALU.mult), ("qk_rot", j))
                wait_drained(dve, ("qk_rot", j))
                link(v.tensor_tensor(src, src, tab("cos"), ALU.mult))
                link(v.tensor_tensor(src, src, TQ, ALU.add))
                dve.wait_ge(sem("rstd"), 7 + j)
                done(dve, v.tensor_tensor(src, src, RS, ALU.mult), "qk_ready")

            EYE8 = tab("eye8").rearrange("p (b c) -> p b c", b=8)

            def swa_max(u):
                g, blk = u // 2, u % 2
                width = P * (blk + 1)
                if u:
                    for back in range((u - 1) % 2 + 1):
                        wait_filled(dve, ("pt", u - 1, back))
                for hh in range(2):
                    b = wait_filled(dve, ("s", u, hh))
                    for jj in range(2):
                        k = 2 * jj + hh
                        h = 4 * g + k
                        last = v.tensor_tensor_reduce(SM[:, 256 * k:256 * k + width],
                                                      b[:, 256 * jj:256 * jj + width],
                                                      tab("window")[:, 0:width], HD ** -0.5, vec("sink", h, h + 1),
                                                      ALU.add, ALU.max, at("ST", k, k + 1))
                    drains(last, ("s", u, hh))
                    wait_drained(dve, ("s", u, hh))
                link(v.tensor_scalar(at("ST", 4, 8), at("ST", 0, 4), -1.0, None, ALU.mult))
                done(dve, v.tensor_tensor(at("ST", 12, 16), vec("sink", 4 * g, 4 * g + 4), at("ST", 0, 4),
                                          ALU.subtract), "swa_max")

            def swa_probs(u):
                width = P * (u % 2 + 1)
                dve.wait_ge(sem("exps"), u + 1)
                link(v.tensor_tensor(at("ST", 8, 12), at("ST", 8, 12), at("ST", 12, 16), ALU.add))
                link(v.reciprocal(at("ST", 8, 12), at("ST", 8, 12)))
                p = SM.rearrange("p (k w) -> p k w", w=256)[:, :, 0:width]
                done(dve, v.tensor_tensor(p, p, over(at("ST", 8, 12), width), ALU.mult), "probs")

            def swa_turned(u):
                if u:
                    wait_filled(dve, ("o", u - 1))
                for back in range(u % 2 + 1):
                    b = wait_filled(dve, ("pt", u, back))
                    drains(v.tensor_copy(PTs[:, 512 * back:512 * (back + 1)], b[:, :]), ("pt", u, back))

            def mem_max(h):
                b = wait_filled(dve, ("ms", h))
                link(v.tensor_reduce(at("ST", 18, 20), b[:, :].rearrange("p (q m) -> p q m", q=2), AX.X, ALU.max))
                done(dve, v.tensor_scalar(at("ST", 20, 22), at("ST", 18, 20), -(MEM_D ** -0.5), None, ALU.mult),
                     "mem_max")
                dve.wait_ge(sem("exps"), 8 + h + 1)
                drains(v.reciprocal(at("ST", 24, 26), at("ST", 24, 26)), ("ms", h))
                wait_drained(dve, ("ms", h))
                p = SM[:, 0:2 * MEM].rearrange("p (q m) -> p q m", q=2)
                done(dve, v.tensor_tensor(p, p, over(at("ST", 24, 26), MEM), ALU.mult), "probs")

            def mem_turned(h):
                wait_filled(dve, ("mo", h - 1) if h else ("o", 7))
                b = wait_filled(dve, ("mpt", h))
                drains(v.tensor_copy(PTs[:, 0:512], b[:, :]), ("mpt", h))

            def sample(b_, piece):
                H = HS[b_ % 2]
                if piece == 0:
                    if b_ == 0:
                        dve.wait_ge(sem("p_ssm_out"), 16)
                    wait_drained(dve, ("bb", b_, 0))
                    t2 = T2.rearrange("p (g j n) -> p g j n", g=4, n=STATE)
                    bcast = BB[:, 0:512].rearrange("p (g n) -> p g n", g=4).unsqueeze(2).to_broadcast([P, 4, 4, STATE])
                    xdt = XS[:, :, b_].rearrange("p (g j) -> p g j", g=4).unsqueeze(3).to_broadcast([P, 4, 4, STATE])
                    link(v.tensor_tensor(t2, bcast, xdt, ALU.mult))
                elif piece == 1:
                    dve.wait_ge(sem("state_decayed"), b_ + 1)
                    h2 = H.rearrange("p j n -> p (j n)")
                    done(dve, v.tensor_tensor(h2, h2, T2, ALU.add), "state_new")
                else:
                    wait_drained(dve, ("bb", b_, 1))
                    t2 = T2.rearrange("p (g j n) -> p g j n", g=4, n=STATE)
                    bcast = BB[:, 512:1024].rearrange("p (g n) -> p g n", g=4).unsqueeze(2).to_broadcast(
                        [P, 4, 4, STATE])
                    h4 = H.rearrange("p (g j) n -> p g j n", g=4)
                    link(v.tensor_tensor(t2, h4, bcast, ALU.mult))
                    done(dve, v.tensor_reduce(EX[:, 0, :, b_], T2.rearrange("p (j n) -> p j n", n=STATE), AX.X,
                                              ALU.add), "sample_y")

            for i in range(40):
                if 1 <= i < 9:
                    decays(i - 1)
                if i < 8:
                    segments(i)
                if 1 <= i < 9:
                    y_add(i - 1)
                if i < 12:
                    rotate(i)
                if i == 9:
                    dve.wait_ge(sem("end_decay"), 1)
                    x3 = at("XD").rearrange("p (h d) -> p h d", d=HEADDIM)
                    done(dve, v.tensor_tensor(x3, x3, over(at("WE"), HEADDIM), ALU.mult), "xd_weighed")
                if i in (12, 13):
                    for h in (2 * i - 24, 2 * i - 23):
                        dve.wait_ge(sem("rstd"), 19 + h)
                        for dt in range(2):
                            t = MQ[:, 2 * h + dt, :]
                            last = v.scalar_tensor_tensor(t, t, vec("gmq", dt, dt + 1), RS, ALU.mult, ALU.mult)
                        done(dve, last, "mq_scaled")
                    if i == 13:
                        done(dve, v.tensor_scalar(at("ST", 61, 62), RS[:, 0:1], 0.0, None, ALU.mult), "mq_ready")
                        wait_filled(dve, ("state", 3))
                if 15 <= i < 23:
                    swa_probs(i - 15)
                    swa_turned(i - 15)
                if 24 <= i < 28:
                    mem_turned(i - 24)
                if 14 <= i < 22:
                    swa_max(i - 14)
                if i == 14:
                    link(v.memset(ZEROS, 0.0))
                    link(v.tensor_tensor(EIGHTS, MQ[:, :, SEQ:T].unsqueeze(3).to_broadcast([P, 8, 8, 8]),
                                         EYE8.unsqueeze(1).to_broadcast([P, 8, 8, 8]), ALU.mult))
                    eye_half = tab("eye8_half").rearrange("p (b c h) -> p b c h", b=8, h=2)
                    for g in range(KV):
                        own = FOURS[:, g].rearrange("p b (c j h) -> p b c j h", j=2, h=2)
                        for j in range(2):
                            q_ = Q[:, 2 * g + j, SEQ:T].unsqueeze(2).unsqueeze(3).to_broadcast([P, 8, 8, 2])
                            last = v.tensor_tensor(own[:, :, :, j, :], q_, eye_half, ALU.mult)
                    done(dve, last, "sample_queries")
                if 23 <= i < 27:
                    mem_max(i - 23)
                if 14 <= i < 38:
                    sample((i - 14) // 3, (i - 14) % 3)
                if i in (21, 22):
                    part = i - 21
                    dve.wait_ge(sem(f"ring_in{part}"), 16 * 5)
                    kc = RING[part].rearrange("p (g b m) -> p g b m", b=4, m=P)
                    done(dve, v.tensor_copy(kc[:, :, :, 0], KD[:, :, SEQ + 4 * part:SEQ + 4 * (part + 1)]), "new_key")
                yp = C[:, 0:XS_T, 0:SEQ]
                if i == 30:
                    dve.wait_ge(sem("z_active"), 1)
                    done(dve, v.tensor_tensor(yp, yp, Z[:, :, 0:SEQ], ALU.mult), "y_gated")
                if i == 33:
                    dve.wait_ge(sem("y_squared"), 1)
                    link(v.tensor_tensor(yp, yp, over(vec("ssm_g"), SEQ), ALU.mult))
                if i == 24:
                    b = wait_filled(dve, "s_scores")
                    link(v.tensor_reduce(at("ST", 32, 33), b[:, 0:MEM], AX.X, ALU.max))
                    link(v.tensor_scalar(at("ST", 32, 33), at("ST", 32, 33), -(MEM_D ** -0.5), None, ALU.mult))
                    link(v.tensor_reduce(at("ST", 33, 34), b[:, MEM:MEM + P], AX.X, ALU.max))
                    link(v.tensor_scalar(at("ST", 33, 34), at("ST", 33, 34), HD ** -0.5, vec("sink_col"),
                                         ALU.mult, ALU.max))
                    link(v.tensor_tensor(at("ST", 36, 37), vec("sink_col"), at("ST", 33, 34), ALU.subtract))
                    done(dve, v.tensor_scalar(at("ST", 33, 34), at("ST", 33, 34), -1.0, None, ALU.mult), "sample_max")
                if i == 25:
                    dve.wait_ge(sem("sample_exps"), 1)
                    drains(v.tensor_tensor(at("ST", 35, 36), at("ST", 35, 36), at("ST", 36, 37), ALU.add), "s_scores")
                    wait_drained(dve, "s_scores")
                    link(v.reciprocal(at("ST", 34, 36), at("ST", 34, 36)))
                    for a_, b_ in ((0, MEM), (MEM, MEM + P)):
                        k = 34 + (a_ > 0)
                        done(dve, v.tensor_scalar(SSM[:, a_:b_], SSM[:, a_:b_], at("ST", k, k + 1), None, ALU.mult),
                             "sample_probs")
                if i == 26:
                    b = wait_filled(dve, "spt")
                    pt = b[:, 0:MEM].rearrange("p (t c) -> p t c", c=32)[:, :, 0:BATCH_S]
                    v.tensor_tensor(EIGHTS, pt.unsqueeze(3).to_broadcast([P, 8, 8, 8]),
                                    EYE8.unsqueeze(1).to_broadcast([P, 8, 8, 8]), ALU.mult)
                    for g in range(KV):
                        own = FOURS[:, g].rearrange("p b (c h) -> p b c h", h=4)
                        pt = b[:, MEM + 32 * g:MEM + 32 * (g + 1)].rearrange("p (c h) -> p c h", h=4)
                        last = v.tensor_tensor(own, pt.unsqueeze(1).to_broadcast([P, 8, 8, 4]),
                                               EYE8.unsqueeze(3).to_broadcast([P, 8, 8, 4]), ALU.mult)
                    drains(last, "spt")
            ys = C[:, 0:XS_T, SEQ:T]
            link(v.tensor_tensor(ys, ys, over(vec("ssm_d"), BATCH_S), ALU.mult))
            done(dve, v.tensor_tensor(ys, ys, EX[:, 0, :, :], ALU.add), "samples_done")
            done(dve, v.tensor_tensor(ys, ys, Z[:, :, SEQ:T], ALU.mult), "y_gated")
            dve.wait_ge(sem("y_squared"), 2)
            done(dve, v.tensor_tensor(ys, ys, over(vec("ssm_g"), BATCH_S), ALU.mult), "y_ready")
            dve.wait_ge(sem("gates_active"), 1)
            dve.wait_ge(sem("p_mem_out"), 32)
            wait_filled(dve, ("mo", 3))
            for i in range(4):
                for c in range(2):
                    m = 2 * i + c
                    b = wait_filled(dve, ("swa", m))
                    drains(v.tensor_tensor(MERGED[:, m, :], b[:, 0:T], G[:, 8 + m, :], ALU.mult), ("swa", m))
                for c in range(2):
                    m = 2 * i + c
                    b = wait_filled(dve, ("memb", m))
                    drains(v.tensor_tensor(TQ, b[:, 0:T], G[:, 16 + m, :], ALU.mult), ("memb", m))
                    wait_drained(dve, ("memb", m))
                    link(v.tensor_tensor(MERGED[:, m, :], MERGED[:, m, :], TQ, ALU.add))
            dve.wait_ge(sem("rstd"), 23)
            for m in range(8):
                b = wait_filled(dve, ("ssm", m))
                drains(v.tensor_tensor(TQ, b[:, 0:T], RS, ALU.mult), ("ssm", m))
                wait_drained(dve, ("ssm", m))
                link(v.tensor_tensor(TQ, TQ, G[:, m, :], ALU.mult))
                done(dve, v.tensor_tensor(MERGED[:, m, :], MERGED[:, m, :], TQ, ALU.add), "merged")
            dve.wait_ge(sem("x_again"), 16)
            for m in range(KT):
                b = wait_filled(dve, ("out", m))
                drains(v.tensor_tensor(X1[:, m, :], X1[:, m, :], b[:, 0:T], ALU.add), ("out", m))
                wait_drained(dve, ("out", m))
                v.tensor_scalar(X1GS[:, m, :], X1[:, m, SEQ:T], vec("g2", m, m + 1), None, ALU.mult
                                ).then_inc(sem("x1_made"), 1)
                if m >= 4:
                    dve.wait_ge(sem("x1_tile_used"), m - 3)
                v.tensor_scalar(X1G[:, m % 4, :], X1[:, m, :], vec("g2", m, m + 1), None, ALU.mult
                                ).then_inc(sem("x1_by_gain"), 1)
            link(v.memset(PLACE, -1.0))
            link(v.memset(COMB, 0.0))

            def r(a_, n, w=None):
                ap = at("S", 1100 + a_, 1100 + a_ + n)
                return ap if w is None else ap.rearrange("p (t e) -> p t e", e=w)

            D4, M2, D8, O8, OG, SEL, LG = (r(0, 12, 4), r(12, 3), r(16, 24, 8), r(40, 24, 8), r(64, 12, 4),
                                           r(80, 96), r(176, 108, ROUTES))
            T12, T24, MX, OH2, ZS = r(300, 12, 4), r(320, 24, 8), r(344, 3), r(350, 24, 8), r(380, 24, 8)
            W1, W2 = r(404, 3), r(407, 3)
            dve.wait_ge(sem("router_in"), 16)
            link(v.memset(r(176, 108), 0.0))
            link(v.memset(SSQ, 1.0))
            b = wait_filled(dve, "route")
            link(v.tensor_copy(SSQ[:, 0:2], b[:, 0:P].rearrange("p (t n) -> p t n", n=64)[:, :, 40]))
            done(dve, v.tensor_copy(SSQ[0:BATCH_S, 2:3], b[0:BATCH_S, 168:169]), "ssq_ready")
            dve.wait_ge(sem("rtok"), 1)
            for t, rows in enumerate((P, P, BATCH_S)):
                last = v.scalar_tensor_tensor(LG[0:rows, t, :], b[0:rows, 64 * t:64 * t + ROUTES],
                                              RTOK[0:rows, t:t + 1], vec("route_b", rows=rows), ALU.mult, ALU.add)
            drains(last, "route")
            wait_drained(dve, "route")

            def first_best(src, width, order, mx, eq, out):
                link(v.tensor_reduce(mx, src, AX.X, ALU.max))
                link(v.tensor_tensor(eq, src, over(mx, width), ALU.is_equal))
                link(v.tensor_tensor(eq, eq, each(tab(order), 3), ALU.mult))
                link(v.tensor_reduce(MX2, eq, AX.X, ALU.max))
                link(v.tensor_tensor(out, eq, over(MX2, width), ALU.is_equal))

            MX2 = r(347, 3)
            first_best(LG[:, :, 0:GROUPS], GROUPS, "first_g", MX, T12, OG)
            link(v.tensor_tensor(D4, LG[:, :, 0:GROUPS], over(MX, GROUPS), ALU.subtract))
            for t in range(3):
                last = v.tensor_tensor(SEL[:, 32 * t:32 * (t + 1)].rearrange("p (g e) -> p g e", g=GROUPS),
                                       LG[:, t, GROUPS:ROUTES].rearrange("p (g e) -> p g e", g=GROUPS),
                                       over(OG[:, t, :], PER_GROUP), ALU.mult)
            link(last)
            link(v.tensor_reduce(ZS, SEL.rearrange("p (t g e) -> p t e g", t=3, g=GROUPS), AX.X, ALU.add))
            first_best(ZS, PER_GROUP, "first_e", MX, T24, O8)
            link(v.tensor_tensor(D8, ZS, over(MX, PER_GROUP), ALU.subtract))
            link(v.scalar_tensor_tensor(D8, O8, -1e30, D8, ALU.mult, ALU.add))
            first_best(D8, PER_GROUP, "first_e", M2, T24, OH2)
            done(dve, v.tensor_scalar(r(410, 3), M2, 1.0, None, ALU.mult), "route_args")
            link(v.tensor_tensor(T24, O8, OH2, ALU.add))
            for t in range(3):
                last = v.tensor_tensor(MASK[:, t, :].rearrange("p (g e) -> p g e", g=GROUPS),
                                       over(OG[:, t, :], PER_GROUP), each(T24[:, t, :], GROUPS), ALU.mult)
            done(dve, last, "chosen")
            dve.wait_ge(sem("route_exp"), 2)
            link(v.tensor_reduce(W1, D4, AX.X, ALU.add))
            link(v.reciprocal(W1, W1))
            link(v.tensor_scalar(W2, M2, 1.0, None, ALU.add))
            link(v.reciprocal(W2, W2))
            link(v.tensor_tensor(W1, W1, W2, ALU.mult))
            link(v.tensor_tensor(W2, W1, M2, ALU.mult))
            link(v.tensor_tensor(O8, O8, over(W1, PER_GROUP), ALU.mult))
            link(v.tensor_tensor(OH2, OH2, over(W2, PER_GROUP), ALU.mult))
            link(v.tensor_tensor(O8, O8, OH2, ALU.add))
            for t in range(3):
                last = v.tensor_tensor(COMB[:, t, 0:EXPERTS].rearrange("p (g e) -> p g e", g=GROUPS),
                                       over(OG[:, t, :], PER_GROUP), each(O8[:, t, :], GROUPS), ALU.mult)
            done(dve, last, "comb")
            b = wait_filled(dve, "count")
            link(v.tensor_reduce(MX2[:, 0:1], b[:, 96:128], AX.X, ALU.max))
            v.tensor_copy(worst[:, :], MX2[:, 0:1]).then_inc(sem("worst_ready"), 1)
            b3 = b[:, 0:64].rearrange("p (t e) -> p t e", t=2)
            link(v.tensor_tensor(PLACE[:, 0:2, 0:EXPERTS], b3, MASK[:, 0:2, :], ALU.mult))
            drains(v.tensor_tensor(PLACE[0:8, 2, 0:EXPERTS], b[0:8, 64:96], MASK[0:8, 2, :], ALU.mult), "count")
            wait_drained(dve, "count")
            for rows, t0, t1 in ((P, 0, 2), (BATCH_S, 2, 3)):
                place = PLACE[0:rows, t0:t1, 0:EXPERTS]
                link(v.tensor_scalar(place, place, -1.0, None, ALU.add))

            dve.sem_inc(sem("tile_added"), 2)

            def experts(rounds):
                def find_slots(buf, q, n):
                    mine = PLACE[:, :, bass.ds(q * QUAD, QUAD)]
                    slots = tab("slots").unsqueeze(1).unsqueeze(1).to_broadcast([P, 3, QUAD, SLOTS])
                    v.tensor_tensor(ONE, mine.unsqueeze(3).to_broadcast([P, 3, QUAD, SLOTS]), slots, ALU.is_equal
                                    ).then_inc(sem("slots_found"), 1)
                    dve.wait_ge(sem("slots_found"), n + 1)
                    v.tensor_tensor(ONEW[buf], ONE,
                                    COMB[:, :, bass.ds(q * QUAD, QUAD)].unsqueeze(3).to_broadcast([P, 3, QUAD, SLOTS]),
                                    ALU.mult).then_inc(sem("slots_ready"), 1)
                    if rounds > 1:
                        v.tensor_scalar(mine, mine, -float(SLOTS), None, ALU.add).then_inc(sem("place_moved"), 1)
                        dve.wait_ge(sem("place_moved"), n + 1)

                def store_gathered(n):
                    dve.wait_ge(sem("gathered1"), n + 1)
                    v.tensor_copy(HG[:, 4:8, :].rearrange("p k s -> p (k s)"), psum[5][:, :]
                                  ).then_inc(sem("gathered_stored"), 1)

                def body(buf, q, n):
                    if rounds > 1:
                        find_slots(0, q, n)
                        store_gathered(n)
                    else:
                        find_slots(1 - buf, q + 1, n + 1)
                    dve.wait_ge(sem("silu"), n + 1)
                    dve.wait_ge(sem("up_filled"), n + 1)
                    v.tensor_tensor(ACTV, psum[1][:, 0:D_FF], SG, ALU.mult).then_inc(sem("act_ready"), 1)
                    if rounds == 1:
                        store_gathered(n + 1)
                    dve.wait_ge(sem("act_turned"), n + 1)
                    v.tensor_copy(ACTT.rearrange("p f s -> p (f s)"), psum[1][:, 0:D_FF]
                                  ).then_inc(sem("actT_ready"), 1)
                    dve.wait_ge(sem("back_filled"), n + 1)
                    v.tensor_copy(BACK, psum[6][:, 0:T]).then_inc(sem("back_ready"), 1)
                    dve.wait_ge(sem("down_filled1"), n + 1)
                    v.tensor_copy(DOWNED[:, 512:1024], psum[3][:, :]).then_inc(sem("down_stored1"), 1)
                    for m in range(KT):
                        dve.wait_ge(sem("tile_filled"), n * KT + (m + 1))
                        v.tensor_tensor(X1[:, m, :], X1[:, m, :], psum[6 + m % 2][:, 0:T], ALU.add
                                        ).then_inc(sem("tile_added"), 1)

                if rounds == 1:
                    find_slots(0, 0, 0)
                    store_gathered(0)
                steps(dve, rounds, body)

            by_rounds(dve, experts)


def _tables():
    t = np.zeros((P, TAB_W), np.float32)

    def put(name, a):
        o, n = TAB[name]
        t[:, o:o + n] = a

    s, u = np.arange(P)[:, None], np.arange(P)[None, :]
    causal = (s <= u).astype(np.float32)
    put("ident", np.eye(P, dtype=np.float32))
    put("causal", np.concatenate([causal, np.ones((P, P), np.float32), causal], 1))
    rot = np.zeros((P, P), np.float32)
    for m in range(P):
        if m % 64 < 32:
            rot[m + 32, m] = -1.0
        else:
            rot[m - 32, m] = 1.0
    put("rot", rot)
    put("half_ones", (s // 64 == u // 64).astype(np.float32))
    put("ones", np.ones((P, P), np.float32))
    put("window", np.concatenate([np.where(u <= s, 0, -1e30), np.where(u > s, 0, -1e30)], 1))
    inv = np.float32(10000.0) ** (-np.arange(32, dtype=np.float32) / np.float32(32))
    pos = np.concatenate([np.arange(SEQ), np.full(BATCH_S, PAST_LEN)]).astype(np.float32)
    ang = (pos[None, :] * inv[:, None]).astype(np.float32)
    put("cos", np.tile(np.cos(ang), (4, 1)))
    put("sin", np.tile(np.sin(ang), (4, 1)))
    put("first_g", np.arange(GROUPS, 0, -1)[None, :])
    put("first_e", np.arange(PER_GROUP, 0, -1)[None, :])
    put("slots", np.arange(SLOTS)[None, :])
    eye = np.eye(BATCH_S, dtype=np.float32)
    put("eye8", eye.reshape(1, -1))
    put("eye8_half", (eye[None, :, :, None] * (s[:, :, None, None] // 64 == np.arange(2))).reshape(P, -1))
    return t


def _layout(inp):
    c = np.ascontiguousarray

    def feat(a):
        return a.reshape(-1, P).T

    def rows(a):
        return np.broadcast_to(a.reshape(1, -1), (P, a.size))

    i = {k: np.asarray(a) for k, a in inp.items()}
    xt = np.concatenate([i["x_prompt"][0], i["x_sample"][:, 0]], 0)
    sink = i["att_sink"][0]
    sink_col = np.tile(sink.reshape(KV, 1, 4), (1, BATCH_S, 1)).reshape(-1, 1)
    parts = {
        "g1": feat(i["norm1_g"][0]), "gmem": feat(i["mem_norm_g"][0]),
        "conv_w": np.concatenate([feat(i["ssm_conv_w"][0, k]) for k in range(CONV_TAPS)], 1),
        "conv_b": feat(i["ssm_conv_b"][0]), "ssm_g": feat(i["ssm_norm_g"][0]),
        "ssm_d": feat(np.repeat(i["ssm_d"][0], HEADDIM)),
        "gq": np.tile(i["att_q_norm_g"][0], 2)[:, None], "gk": np.tile(i["att_k_norm_g"][0], 2)[:, None],
        "gmq": feat(i["mem_q_norm_g"][0]), "gmk": feat(i["mem_k_norm_g"][0]), "g2": feat(i["norm2_g"][0]),
        "sink_col": sink_col, "dt_bias": rows(i["ssm_dt_bias"][0]), "a_log": rows(i["ssm_a_log"][0]),
        "route_b": rows(np.concatenate([i["b_router_group"][0], i["b_router_expert"][0]])), "sink": rows(sink),
    }

    def tiled(a):
        return c(a.T.reshape(-1, P, a.shape[0]).transpose(1, 0, 2))

    kt = i["cache_swa_k"][0].transpose(3, 2, 0, 1).reshape(HD, KV, 2, 4, P)
    kt = np.concatenate([kt, kt], 0).transpose(2, 0, 1, 3, 4)
    return {
        "tables": _tables(),
        "vectors": c(np.concatenate([parts[n] for n in VEC], 1)),
        "xT": tiled(xt),
        "memT": tiled(i["mem_prompt"][0]),
        "histT": c(i["state_conv"][0].transpose(2, 0, 1).reshape(CONV_T, P, BATCH_S, 3).transpose(1, 0, 2, 3)),
        "w_in": i["w_in"][0], "w_mem_kv": i["w_mem_kv"][0], "w_br_ssm": i["w_br_ssm"][0],
        "w_br_swa": i["w_br_swa"][0], "w_br_mem": i["w_br_mem"][0], "w_out": i["w_out"][0],
        "w_router": c(np.concatenate([i["w_router_group"][0], i["w_router_expert"][0]], 1)),
        "w_exp_gate": i["w_exp_gate"][0], "w_exp_up": i["w_exp_up"][0], "w_exp_down": i["w_exp_down"][0],
        "state_ssm": i["state_ssm"][0].reshape(BATCH_S, D_INNER, STATE),
        "mem_kT": c(i["cache_mem_k"][0].reshape(BATCH_S, MEM, MEM_H, 2, P).transpose(0, 4, 2, 3, 1)
                    .reshape(BATCH_S, P, 2048)),
        "mem_v": c(i["cache_mem_v"][0].reshape(BATCH_S, 2, P, D_MODEL).transpose(0, 2, 1, 3).reshape(BATCH_S, P, 2048)),
        "swa_kT": c(kt.reshape(2, P, 2048)),
        "swa_v": c(i["cache_swa_v"][0].reshape(BATCH_S, P, KV * HD).transpose(1, 0, 2).reshape(P, 2048)),
    }


_OUTS = {
    "yT": (P, KT, T), "p_mem_kT": (P, 8, MEM), "p_mem_v": (P, 2, D_MODEL), "p_swa_v": (P, KV * HD),
    "newconvT": (P, CONV_T, 27), "p_swa_kT": (64, KV, P), "p_ssm": (D_INNER, STATE),
    "s_ssm": (BATCH_S, D_INNER, STATE), "s_swa_kT": (2, 64, 2048), "s_swa_v": (P, 2048),
}


def _results(o):
    c = np.ascontiguousarray
    y = o["yT"].transpose(1, 0, 2).reshape(D_MODEL, T).T
    conv = o["newconvT"].transpose(1, 0, 2).reshape(CONV_CH, 27)
    roll = list(range(1, P)) + [0]
    sk = o["s_swa_kT"].reshape(2, HD, KV, 4, P).transpose(0, 3, 4, 2, 1).reshape(BATCH_S, P, KV, HD)[:, roll]
    sv = o["s_swa_v"].reshape(P, BATCH_S, KV, HD).transpose(1, 0, 2, 3)[:, roll]
    return (
        c(y[:SEQ])[None], c(y[SEQ:])[:, None],
        c(conv[:, 24:27].T)[None, None],
        o["p_ssm"].reshape(1, 1, SSM_HEADS, HEADDIM, STATE),
        c(o["p_swa_kT"].transpose(2, 1, 0))[None, None],
        o["p_swa_v"].reshape(1, 1, P, KV, HD),
        c(o["p_mem_kT"].transpose(2, 1, 0).reshape(MEM, MEM_H, MEM_D))[None, None],
        c(o["p_mem_v"].transpose(1, 0, 2).reshape(MEM, MEM_H, MEM_D))[None, None],
        c(conv[:, 0:24].reshape(CONV_CH, BATCH_S, 3).transpose(1, 2, 0))[None],
        o["s_ssm"].reshape(1, BATCH_S, SSM_HEADS, HEADDIM, STATE),
        c(sk)[None], c(sv)[None],
    )


def kernel(**inputs):
    import concourse.bacc as bacc
    from concourse.bass_utils import run_bass_kernel_spmd

    nc = bacc.Bacc("TRN2", target_bir_lowering=False, num_devices=1, dynamic_dma_scratch_size=8192)
    arrays = _layout(inputs)
    ins = {n: nc.dram_tensor(f"in_{n}", a.shape, mybir.dt.from_np(a.dtype), kind="ExternalInput").ap()
           for n, a in arrays.items()}
    outs = {n: nc.dram_tensor(f"out_{n}", s, F32, kind="ExternalOutput").ap() for n, s in _OUTS.items()}
    build_program(nc, ins, outs)
    got = run_bass_kernel_spmd(nc, [{f"in_{n}": a for n, a in arrays.items()}], core_ids=[0])
    return _results({n: got.results[0][f"out_{n}"] for n in _OUTS})
```
